# Optimizing a Trainium2 kernel written in Bass

```python
import jax, jax.numpy as jnp
from jax import lax
import numpy as np
import math

D_MODEL = 1024
BATCH = 1
SEQ = 1024
DEPTH = 1

GRID_W = 64
HEAD_DIM = 64
D_MIX = D_MODEL
A_HEADS = 8
A_KV_HEADS = 2
B_HEADS = 8
A_WIDTH = A_HEADS * HEAD_DIM
A_KV_WIDTH = A_KV_HEADS * HEAD_DIM
B_WIDTH = B_HEADS * HEAD_DIM
SPLITS = (A_WIDTH, A_KV_WIDTH, A_KV_WIDTH, A_WIDTH, B_WIDTH, B_WIDTH, B_WIDTH, B_WIDTH)
D_IN = sum(SPLITS)
Q_BLOCK = 128
AXIS_DIM = HEAD_DIM // 2
ROPE_PAIRS = AXIS_DIM // 2
ROPE_THETA = 10000.0
NA_KH = 8
NA_KW = 16
NA_COL_BLOCK = 16
NA_BAND = NA_COL_BLOCK + NA_KW
EPS = 1e-6


def _rmsnorm(x, gain):
    x32 = x.astype(jnp.float32)
    y = x32 * lax.rsqrt(jnp.mean(x32 * x32, axis=-1, keepdims=True) + EPS)
    return (y * gain.astype(jnp.float32)).astype(x.dtype)

def _axial_rope_tables(seq, dtype):
    t = jnp.arange(seq, dtype=jnp.int32)
    row = (t // GRID_W).astype(jnp.float32)
    col = (t % GRID_W).astype(jnp.float32)
    inv = ROPE_THETA ** (-jnp.arange(ROPE_PAIRS, dtype=jnp.float32) * (2.0 / AXIS_DIM))
    ang_r = row[:, None] * inv[None, :]
    ang_c = col[:, None] * inv[None, :]
    ang = jnp.concatenate([ang_r, ang_r, ang_c, ang_c], axis=-1)
    return jnp.cos(ang)[:, None, :].astype(dtype), jnp.sin(ang)[:, None, :].astype(dtype)

def _rotate_half_axial(x):
    shp = x.shape
    xr = x.reshape(shp[:-1] + (2, 2, ROPE_PAIRS))
    x1 = xr[..., 0, :]
    x2 = xr[..., 1, :]
    return jnp.stack([-x2, x1], axis=-2).reshape(shp)

def _gqa_blocked(q, k, v):
    b, s, h, d = q.shape
    hk = k.shape[2]
    g = h // hk
    nb = s // Q_BLOCK
    qb = q.reshape(b, nb, Q_BLOCK, hk, g, d).transpose(1, 0, 2, 3, 4, 5)
    scale = d ** -0.5

    def block(qi):
        sc = jnp.einsum('bqkgd,bskd->bkgqs', qi, k).astype(jnp.float32) * scale
        p = jax.nn.softmax(sc, axis=-1).astype(v.dtype)
        return jnp.einsum('bkgqs,bskd->bqkgd', p, v)

    o = lax.map(block, qb)
    return o.transpose(1, 0, 2, 3, 4, 5).reshape(b, s, h * d)

def _neighbourhood_attn(q, k, v, rpb):
    b, s, h, d = q.shape
    rows = s // GRID_W
    kh = min(NA_KH, rows)
    n_cb = GRID_W // NA_COL_BLOCK
    qg = q.reshape(b, rows, GRID_W, h, d)
    kg = k.reshape(b, rows, GRID_W, h, d)
    vg = v.reshape(b, rows, GRID_W, h, d)
    c = np.arange(GRID_W)
    col_start = np.clip(c - NA_KW // 2, 0, GRID_W - NA_KW)
    band_start = np.clip(np.arange(n_cb) * NA_COL_BLOCK - NA_KW // 2, 0, GRID_W - NA_BAND)
    band_cols = band_start[:, None] + np.arange(NA_BAND)[None, :]
    qc = c.reshape(n_cb, NA_COL_BLOCK)
    qcs = col_start.reshape(n_cb, NA_COL_BLOCK)
    kc = band_cols[:, None, :]
    col_valid = (kc >= qcs[..., None]) & (kc < qcs[..., None] + NA_KW)
    col_idx = np.clip(kc - qc[..., None] + (NA_KW - 1), 0, 2 * NA_KW - 2)
    rpb_col = rpb[:, :, col_idx]
    mask = jnp.asarray(col_valid[:, :, None, :])
    scale = d ** -0.5

    def row_block(args):
        r, q_row = args
        r0 = jnp.clip(r - kh // 2, 0, rows - kh)
        k_rows = lax.dynamic_slice_in_dim(kg, r0, kh, axis=1)
        v_rows = lax.dynamic_slice_in_dim(vg, r0, kh, axis=1)
        k_band = jnp.take(k_rows, band_cols, axis=2)
        v_band = jnp.take(v_rows, band_cols, axis=2)
        qb = q_row.reshape(b, n_cb, NA_COL_BLOCK, h, d)
        sc = jnp.einsum('bjqhd,bkjchd->bhjqkc', qb, k_band).astype(jnp.float32) * scale
        row_idx = r0 + jnp.arange(kh) - r + (NA_KH - 1)
        bias = rpb_col[:, row_idx].transpose(0, 2, 3, 1, 4)
        sc = jnp.where(mask, sc + bias.astype(jnp.float32), -jnp.inf)
        p = jax.nn.softmax(sc, axis=(-2, -1)).astype(v.dtype)
        o = jnp.einsum('bhjqkc,bkjchd->bjqhd', p, v_band)
        return o.reshape(b, GRID_W, h * d)

    o = lax.map(row_block, (jnp.arange(rows), qg.transpose(1, 0, 2, 3, 4)))
    return o.transpose(1, 0, 2, 3).reshape(b, s, h * d)

def first_inputs(seed: int = 0) -> dict:
    key = jax.random.key(seed)
    ks = jax.random.split(key, 9)
    x = jax.random.normal(ks[0], (BATCH, SEQ, D_MODEL), jnp.float32)
    norm_gain = 1.0 + 0.02 * jax.random.normal(ks[1], (DEPTH, D_MODEL), jnp.float32)
    w_in = jax.random.normal(ks[2], (DEPTH, D_MODEL, D_IN), jnp.float32) * D_MODEL ** -0.5
    q_norm_a = 1.0 + 0.02 * jax.random.normal(ks[3], (DEPTH, HEAD_DIM), jnp.float32)
    k_norm_a = 1.0 + 0.02 * jax.random.normal(ks[4], (DEPTH, HEAD_DIM), jnp.float32)
    na_rpb = 0.02 * jax.random.normal(ks[5], (DEPTH, B_HEADS, 2 * NA_KH - 1, 2 * NA_KW - 1), jnp.float32)
    w_out = jax.random.normal(ks[6], (DEPTH, D_MIX, D_MODEL), jnp.float32) * D_MIX ** -0.5
    final_norm_gain = 1.0 + 0.02 * jax.random.normal(ks[7], (D_MODEL,), jnp.float32)
    return {"x": x, "norm_gain": norm_gain, "w_in": w_in, "q_norm_a": q_norm_a,
            "k_norm_a": k_norm_a, "na_rpb": na_rpb, "w_out": w_out,
            "final_norm_gain": final_norm_gain}

def first_block(x, norm_gain, w_in, q_norm_a, k_norm_a, na_rpb, w_out, final_norm_gain):
    b, s, _ = x.shape
    cos, sin = _axial_rope_tables(s, x.dtype)
    split_at = [int(v) for v in np.cumsum(SPLITS)[:-1]]
    for l in range(DEPTH):
        h = _rmsnorm(x, norm_gain[l])
        proj = h @ w_in[l]
        q_a, k_a, v_a, g_a, q_b, k_b, v_b, g_b = jnp.split(proj, split_at, axis=-1)
        q_a = _rmsnorm(q_a.reshape(b, s, A_HEADS, HEAD_DIM), q_norm_a[l])
        k_a = _rmsnorm(k_a.reshape(b, s, A_KV_HEADS, HEAD_DIM), k_norm_a[l])
        q_a = q_a * cos + _rotate_half_axial(q_a) * sin
        k_a = k_a * cos + _rotate_half_axial(k_a) * sin
        v_a = v_a.reshape(b, s, A_KV_HEADS, HEAD_DIM)
        o_a = _gqa_blocked(q_a, k_a, v_a) * jax.nn.silu(g_a)
        o_b = _neighbourhood_attn(q_b.reshape(b, s, B_HEADS, HEAD_DIM),
                                  k_b.reshape(b, s, B_HEADS, HEAD_DIM),
                                  v_b.reshape(b, s, B_HEADS, HEAD_DIM), na_rpb[l])
        o_b = o_b * jax.nn.silu(g_b)
        mixed = jnp.concatenate([o_a, o_b], axis=-1)
        x = x + mixed @ w_out[l]
    return _rmsnorm(x, final_norm_gain)


D_DN = 512
DN_HEADS = 4
DN_HEAD_DIM = 128
CONV_WIDTH = 4
CHUNK = 64
D_ATT = 512
ATT_HEADS = 8
ATT_HEAD_DIM = 64
DILATED_PATTERNS = ((128, 1), (512, 4), (2048, 16))
N_BUCKETS = 32
MAX_DISTANCE = 2048
D_MIX_2 = D_DN + D_ATT
D_IN_2 = 4 * D_DN + 2 * DN_HEADS + 4 * D_ATT


def rms_norm(x, w):
    xf = x.astype(jnp.float32)
    return xf * lax.rsqrt(jnp.mean(xf * xf, axis=-1, keepdims=True) + EPS) * w.astype(jnp.float32)

def l2_norm(x):
    return x * lax.rsqrt(jnp.sum(x * x, axis=-1, keepdims=True) + EPS)

def split_heads(t, n_heads):
    b, s, _ = t.shape
    return t.reshape(b, s, n_heads, -1).transpose(0, 2, 1, 3)

def causal_depthwise_conv(u, w):
    k_width = w.shape[0]
    s = u.shape[1]
    up = jnp.pad(u, ((0, 0), (k_width - 1, 0), (0, 0)))
    y = up[:, 0:s] * w[0]
    for i in range(1, k_width):
        y = y + up[:, i:i + s] * w[i]
    return y

def gated_delta_rule(q, k, v, g, beta):
    b, h, s, dk = q.shape
    dv = v.shape[-1]
    n = s // CHUNK
    q = q * (dk ** -0.5)
    qc = q.reshape(b, h, n, CHUNK, dk)
    kc = k.reshape(b, h, n, CHUNK, dk)
    vc = v.reshape(b, h, n, CHUNK, dv)
    bc = beta.reshape(b, h, n, CHUNK)
    gc = jnp.cumsum(g.reshape(b, h, n, CHUNK), axis=-1)
    tril_incl = np.tril(np.ones((CHUNK, CHUNK), dtype=bool))
    tril_strict = np.tril(np.ones((CHUNK, CHUNK), dtype=bool), -1)
    diff = gc[..., :, None] - gc[..., None, :]
    decay = jnp.exp(jnp.where(tril_incl, diff, -jnp.inf))
    kb = kc * bc[..., None]
    a_mat = jnp.where(tril_strict, jnp.einsum('bhnid,bhnjd->bhnij', kb, kc) * decay, 0.0)
    l_mat = a_mat + jnp.eye(CHUNK, dtype=a_mat.dtype)
    u = lax.linalg.triangular_solve(l_mat, vc * bc[..., None], left_side=True, lower=True, unit_diagonal=True)
    w = lax.linalg.triangular_solve(l_mat, kb * jnp.exp(gc)[..., None], left_side=True, lower=True, unit_diagonal=True)
    attn_intra = jnp.einsum('bhnid,bhnjd->bhnij', qc, kc) * decay
    q_dec = qc * jnp.exp(gc)[..., None]
    k_tail = kc * jnp.exp(gc[..., -1:] - gc)[..., None]
    g_last = jnp.exp(gc[..., -1])
    xs = tuple(jnp.moveaxis(t, 2, 0) for t in (attn_intra, q_dec, k_tail, u, w, g_last))

    def step(state, inp):
        a_i, qd_i, kt_i, u_i, w_i, gl_i = inp
        v_new = u_i - jnp.einsum('bhck,bhkv->bhcv', w_i, state)
        o_i = jnp.einsum('bhck,bhkv->bhcv', qd_i, state) + jnp.einsum('bhij,bhjv->bhiv', a_i, v_new)
        state = state * gl_i[..., None, None] + jnp.einsum('bhck,bhcv->bhkv', kt_i, v_new)
        return state, o_i

    s0 = jnp.zeros((b, h, dk, dv), jnp.float32)
    _, o = lax.scan(step, s0, xs)
    return jnp.moveaxis(o, 0, 2).reshape(b, h, s, dv)

def t5_bucket(dist):
    max_exact = N_BUCKETS // 2
    d = np.maximum(dist, 1).astype(np.float64)
    large = max_exact + (np.log(d / max_exact) / math.log(MAX_DISTANCE / max_exact)
                         * (N_BUCKETS - max_exact)).astype(np.int32)
    large = np.minimum(large, N_BUCKETS - 1)
    return np.where(dist < max_exact, dist, large).astype(np.int32)

def dilated_pattern(q, k, v, rel_bias, window, dilation):
    b, h, s, hd = q.shape
    r = dilation
    l_sub = s // r
    w_steps = window // r
    blk = w_steps
    n_blk = -(-l_sub // blk)
    l_pad = n_blk * blk

    def to_blocks(t):
        t = t.reshape(b, h, l_sub, r, hd).transpose(0, 1, 3, 2, 4)
        t = jnp.pad(t, ((0, 0), (0, 0), (0, 0), (0, l_pad - l_sub), (0, 0)))
        return t.reshape(b, h, r, n_blk, blk, hd)

    def with_prev(t):
        prev = jnp.pad(t, ((0, 0), (0, 0), (0, 0), (1, 0), (0, 0), (0, 0)))[:, :, :, :-1]
        return jnp.concatenate([prev, t], axis=4)

    qb = to_blocks(q)
    kw = with_prev(to_blocks(k))
    vw = with_prev(to_blocks(v))
    qi = np.arange(blk)[:, None]
    kj = np.arange(2 * blk)[None, :]
    step = qi - kj + blk
    band = (step >= 0) & (step <= w_steps)
    key_idx = np.arange(n_blk)[:, None, None] * blk + kj[None] - blk
    mask = band[None] & (key_idx >= 0)
    buckets = t5_bucket(np.clip(step, 0, None) * r)
    bias = rel_bias.astype(jnp.float32)[:, buckets]
    scores = jnp.einsum('bhrnqd,bhrnkd->bhrnqk', qb, kw).astype(jnp.float32) + bias[:, None, None]
    scores = jnp.where(mask, scores, -jnp.inf)
    lse = jax.nn.logsumexp(scores, axis=-1)
    p = jnp.exp(scores - lse[..., None])
    o = jnp.einsum('bhrnqk,bhrnkd->bhrnqd', p, vw.astype(jnp.float32))
    o = o.reshape(b, h, r, l_pad, hd)[:, :, :, :l_sub].transpose(0, 1, 3, 2, 4).reshape(b, h, s, hd)
    lse = lse.reshape(b, h, r, l_pad)[:, :, :, :l_sub].transpose(0, 1, 3, 2).reshape(b, h, s)
    return o, lse

def deltanet_branch(qkv, z, b_proj, a_proj, conv_w, a_log, dt_bias, dn_norm_w):
    bsz, s, _ = qkv.shape
    qkv = jax.nn.silu(causal_depthwise_conv(qkv.astype(jnp.float32), conv_w.astype(jnp.float32)))
    q, k, v = jnp.split(qkv, 3, axis=-1)
    q = l2_norm(split_heads(q, DN_HEADS))
    k = l2_norm(split_heads(k, DN_HEADS))
    v = split_heads(v, DN_HEADS)
    beta = jax.nn.sigmoid(b_proj.astype(jnp.float32)).transpose(0, 2, 1)
    g = -jnp.exp(a_log.astype(jnp.float32)) * jax.nn.softplus(a_proj.astype(jnp.float32) + dt_bias.astype(jnp.float32))
    g = g.transpose(0, 2, 1)
    o = gated_delta_rule(q, k, v, g, beta)
    o = rms_norm(o, dn_norm_w).transpose(0, 2, 1, 3).reshape(bsz, s, D_DN)
    return o * jax.nn.silu(z.astype(jnp.float32))

def dilated_attention_branch(qkv, gate, q_norm_w, k_norm_w, rel_bias):
    bsz, s, _ = qkv.shape
    q, k, v = jnp.split(qkv, 3, axis=-1)
    q = rms_norm(split_heads(q, ATT_HEADS), q_norm_w) * (ATT_HEAD_DIM ** -0.5)
    k = rms_norm(split_heads(k, ATT_HEADS), k_norm_w)
    v = split_heads(v, ATT_HEADS).astype(jnp.float32)
    outs, lses = [], []
    for window, dilation in DILATED_PATTERNS:
        o_p, lse_p = dilated_pattern(q, k, v, rel_bias, window, dilation)
        outs.append(o_p)
        lses.append(lse_p)
    wts = jax.nn.softmax(jnp.stack(lses), axis=0)
    o = jnp.sum(wts[..., None] * jnp.stack(outs), axis=0)
    o = o.transpose(0, 2, 1, 3).reshape(bsz, s, D_ATT)
    return o * jax.nn.silu(gate.astype(jnp.float32))

def hybrid_layer(x, norm_w, w_in, conv_w, a_log, dt_bias, dn_norm_w, q_norm_w, k_norm_w, rel_bias, w_out):
    h = rms_norm(x, norm_w).astype(x.dtype)
    proj = h @ w_in
    cuts = [3 * D_DN, 4 * D_DN, 4 * D_DN + DN_HEADS, 4 * D_DN + 2 * DN_HEADS,
            4 * D_DN + 2 * DN_HEADS + 3 * D_ATT]
    qkv_dn, z_dn, b_dn, a_dn, qkv_att, gate_att = jnp.split(proj, cuts, axis=-1)
    y_dn = deltanet_branch(qkv_dn, z_dn, b_dn, a_dn, conv_w, a_log, dt_bias, dn_norm_w)
    y_att = dilated_attention_branch(qkv_att, gate_att, q_norm_w, k_norm_w, rel_bias)
    mixed = jnp.concatenate([y_dn, y_att], axis=-1).astype(x.dtype)
    return x + mixed @ w_out

def second_inputs(seed: int = 0) -> dict:
    key = jax.random.key(seed)
    ks = jax.random.split(key, 11)
    x = jax.random.normal(ks[0], (BATCH, SEQ, D_MODEL), jnp.float32)
    norm_w = 1.0 + 0.1 * jax.random.normal(ks[1], (DEPTH, D_MODEL), jnp.float32)
    w_in = jax.random.normal(ks[2], (DEPTH, D_MODEL, D_IN_2), jnp.float32) * (D_MODEL ** -0.5)
    conv_w = jax.random.normal(ks[3], (DEPTH, CONV_WIDTH, 3 * D_DN), jnp.float32) * (CONV_WIDTH ** -0.5)
    a_log = jnp.log(jax.random.uniform(ks[4], (DEPTH, DN_HEADS), jnp.float32, minval=1.0, maxval=16.0))
    dt = jnp.exp(jax.random.uniform(ks[5], (DEPTH, DN_HEADS), jnp.float32,
                                    minval=math.log(1e-3), maxval=math.log(1e-1)))
    dt_bias = dt + jnp.log(-jnp.expm1(-dt))
    dn_norm_w = 1.0 + 0.1 * jax.random.normal(ks[6], (DEPTH, DN_HEAD_DIM), jnp.float32)
    q_norm_w = 1.0 + 0.1 * jax.random.normal(ks[7], (DEPTH, ATT_HEAD_DIM), jnp.float32)
    k_norm_w = 1.0 + 0.1 * jax.random.normal(ks[8], (DEPTH, ATT_HEAD_DIM), jnp.float32)
    rel_bias = 0.5 * jax.random.normal(ks[9], (ATT_HEADS, N_BUCKETS), jnp.float32)
    w_out = jax.random.normal(ks[10], (DEPTH, D_MIX_2, D_MODEL), jnp.float32) * (D_MIX_2 ** -0.5)
    return {"x": x, "norm_w": norm_w, "w_in": w_in, "conv_w": conv_w, "a_log": a_log,
            "dt_bias": dt_bias, "dn_norm_w": dn_norm_w, "q_norm_w": q_norm_w,
            "k_norm_w": k_norm_w, "rel_bias": rel_bias, "w_out": w_out}

def second_block(x, norm_w, w_in, conv_w, a_log, dt_bias, dn_norm_w, q_norm_w, k_norm_w, rel_bias, w_out):
    for layer in range(DEPTH):
        x = hybrid_layer(x, norm_w[layer], w_in[layer], conv_w[layer], a_log[layer], dt_bias[layer],
                         dn_norm_w[layer], q_norm_w[layer], k_norm_w[layer], rel_bias, w_out[layer])
    return x


def setup_inputs(seed=0):
    out = dict(first_inputs(seed))
    for name, value in second_inputs(seed + 1).items():
        if name != "x":
            out[name + "_2"] = value
    return out


def reference(
    x, norm_gain, w_in, q_norm_a, k_norm_a, na_rpb, w_out, final_norm_gain, norm_w_2, w_in_2,
    conv_w_2, a_log_2, dt_bias_2, dn_norm_w_2, q_norm_w_2, k_norm_w_2, rel_bias_2, w_out_2,
):
    x = first_block(
        x, norm_gain, w_in, q_norm_a, k_norm_a, na_rpb, w_out, final_norm_gain,
    )
    return second_block(
        x, norm_w_2, w_in_2, conv_w_2, a_log_2, dt_bias_2, dn_norm_w_2, q_norm_w_2, k_norm_w_2,
        rel_bias_2, w_out_2,
    )


_drawn_inputs = setup_inputs


def setup_inputs(seed=0):
    import zlib

    import numpy as np

    out = dict(_drawn_inputs(seed))
    spreads = {}
    factors = {'norm_gain': 8.0,
     'q_norm_a': 8.0,
     'k_norm_a': 8.0,
     'na_rpb': 8.0,
     'q_norm_w_2': 8.0,
     'k_norm_w_2': 8.0,
     'rel_bias_2': 3.013}
    for name, (base, spread) in spreads.items():
        noise = np.random.default_rng([zlib.crc32(name.encode()), seed]).standard_normal(out[name].shape)
        drawn = base * np.exp(spread * noise) if base else spread * noise
        out[name] = __import__('jax').numpy.asarray(drawn.astype(out[name].dtype))
    for name, factor in factors.items():
        out[name] = (out[name] * factor).astype(out[name].dtype)
    return out
```

```python
from contextlib import ExitStack

import numpy as np
import concourse.bass as bass
from concourse import mybir

F32 = mybir.dt.float32
F32R = mybir.dt.float32r
ACT = mybir.ActivationFunctionType
ALU = mybir.AluOpType
AX = mybir.AxisListType

P = 128
SEQ = 1024
NT = SEQ // P
D = 1024
KT = D // P
HD = 64
EPS = 1e-6
NEG = -1.0e30

A_HEADS, A_KV, B_HEADS = 8, 2, 8
GROUP = A_HEADS // A_KV
D_IN = 3328
QA0, KA0, VA0, GA0, QB0, KB0, VB0, GB0 = 0, 512, 640, 768, 1280, 1792, 2304, 2816
GRID_W, ROWS = 64, 16
NA_KH, NA_KW = 8, 16
RIDX = 2 * NA_KH - 1
CIDX = 2 * NA_KW - 1

D_IN2 = 4104
DN_HEADS, DK = 4, 128
CHUNK = 64
Z2, BA2, AQ2, AK2, AV2, AG2 = 1536, 2048, 2056, 2568, 3080, 3592
ATT_HEADS = 8
DILATION = (1, 4, 16)
LEVELS = 6
CW = 256


class Kit:

    def __init__(self, nc, ctx, clears=True):
        self.nc, self.ctx, self.owned = nc, ctx, []
        if clears:
            ctx.callback(self.retire)

    def retire(self):
        if self.owned:
            self.nc.clear_and_free_semaphores(self.owned)
            self.nc.all_engine_barrier()

    def sb(self, name, shape, dt=F32):
        return self.ctx.enter_context(self.nc.sbuf_tensor(name, shape, dt))

    def psum(self, name, shape=(P, 8, 512)):
        return self.ctx.enter_context(self.nc.psum_tensor(name, list(shape), F32))

    def sem(self, name):
        self.owned.append(self.nc.alloc_semaphore(name))
        return self.owned[-1]

    def sems(self, name, n):
        return [self.sem(f"{name}{i}") for i in range(n)]


def rows(ap, t, c0=0, c1=None):
    return ap[t * P:(t + 1) * P, c0:c1 if c1 is not None else ap.shape[1]]


def stage_norm(nc, tag, x_dram, gain_row, ident_sb, hT_hi, hT_lo, table=None):
    with ExitStack() as ctx:
        k = Kit(nc, ctx)
        x = k.sb(tag + "x", [P, NT, D])
        h = k.sb(tag + "h", [P, 2, D])
        junk = k.sb(tag + "junk", [P, D])
        gain = k.sb(tag + "gain", [P, D])
        stat = k.sb(tag + "stat", [P, 4, NT])
        ps = k.psum(tag + "ps")
        x_loaded = k.sems(tag + "x_loaded", NT)
        gain_loaded = k.sem(tag + "gain_loaded")
        squares_summed = k.sem(tag + "squares_summed")
        var_ready = k.sem(tag + "var_ready")
        std_ready = k.sem(tag + "std_ready")
        rstd_ready = k.sem(tag + "rstd_ready")
        h_ready = k.sem(tag + "h_ready")
        half_transposed = k.sem(tag + "half_transposed")
        hi_ready = k.sem(tag + "hi_ready")
        lo_ready = k.sem(tag + "lo_ready")
        tab = table(k) if table else None
        block = ctx.enter_context(nc.Block())

        @block.sync
        def _(sp):
            if tab:
                tab.sync(sp)
            for t in range(NT):
                sp.dma_start(x[:, t, :], rows(x_dram, t)).then_inc(x_loaded[t], 16)
                if t == 0:
                    sp.dma_start(gain[:, :], gain_row).then_inc(gain_loaded, 16)
            if tab:
                tab.last_sync(sp)

        @block.scalar
        def _(act):
            def split_hi(t):
                for half in range(2):
                    n = 2 * t + half
                    act.wait_ge(half_transposed, n + 1)
                    nc.scalar.copy(hT_hi[:, 4 * half:4 * half + 4, t * P:(t + 1) * P],
                                   ps[:, n % 4, :].rearrange("p (k c) -> p k c", k=4)).then_inc(hi_ready, 1)

            for t in range(NT):
                act.wait_ge(x_loaded[t], 16)
                nc.scalar.activation(junk[:, :], x[:, t, :], ACT.Square,
                                     accum_out=stat[:, 0, t:t + 1]).then_inc(squares_summed, 1)
                act.wait_ge(var_ready, t + 1)
                nc.scalar.activation(stat[:, 2, t:t + 1], stat[:, 1, t:t + 1], ACT.Sqrt).then_inc(std_ready, 1)
                if t >= 1:
                    split_hi(t - 1)
            split_hi(NT - 1)

        @block.vector
        def _(dve):
            def split_lo(t):
                for half in range(2):
                    n = 2 * t + half
                    hi = hT_hi[:, 4 * half:4 * half + 4, t * P:(t + 1) * P]
                    dve.wait_ge(hi_ready, n + 1)
                    nc.vector.tensor_tensor(hT_lo[:, 4 * half:4 * half + 4, t * P:(t + 1) * P],
                                            ps[:, n % 4, :].rearrange("p (k c) -> p k c", k=4),
                                            hi.bitcast(F32), ALU.subtract).then_inc(lo_ready, 1)

            if tab:
                tab.vector(dve, ps)
            for t in range(NT):
                dve.wait_ge(squares_summed, t + 1)
                nc.vector.tensor_scalar(stat[:, 1, t:t + 1], stat[:, 0, t:t + 1], 1.0 / D, EPS,
                                        ALU.mult, ALU.add).then_inc(var_ready, 1)
                dve.wait_ge(std_ready, t + 1)
                nc.vector.reciprocal(stat[:, 3, t:t + 1], stat[:, 2, t:t + 1]).then_inc(rstd_ready, 1)
                dve.wait_ge(rstd_ready, t + 1)
                if t == 0:
                    dve.wait_ge(gain_loaded, 16)
                if t >= 2:
                    dve.wait_ge(half_transposed, 2 * (t - 1))
                nc.vector.scalar_tensor_tensor(h[:, t % 2, :], x[:, t, :], stat[:, 3, t:t + 1], gain[:, :],
                                               ALU.mult, ALU.mult).then_inc(h_ready, 1)
                if t >= 1:
                    split_lo(t - 1)
            split_lo(NT - 1)

        @block.tensor
        def _(pe):
            if tab:
                tab.tensor(pe, ps)
            for t in range(NT):
                pe.wait_ge(h_ready, t + 1)
                for half in range(2):
                    n = 2 * t + half
                    if n >= 4:
                        pe.wait_ge(lo_ready, n - 3)
                    for j in range(4):
                        c = 4 * half + j
                        last = nc.tensor.transpose(ps[:, n % 4, j * P:(j + 1) * P],
                                                   h[:, t % 2, c * P:(c + 1) * P], ident_sb[:, :])
                    last.then_inc(half_transposed, 1)


class BiasTable:

    KC = 8

    def __init__(self, k, nc, table, rpb_t, onehot_d, mask_d):
        self.nc, self.table, self.rpb_t, self.onehot_d, self.mask_d = nc, table, rpb_t, onehot_d, mask_d
        self.onehot = k.sb("na_onehot", [32, 127])
        self.rpb = k.sb("na_rpb", [32, 2, 4 * RIDX])
        self.mask = k.sb("na_mask", [P, GRID_W])
        self.loaded = k.sem("na_loaded")
        self.shifted = k.sem("na_shifted")
        self.placed = k.sem("na_placed")

    def sync(self, sp):
        sp.dma_start(self.onehot[:, :], self.onehot_d).then_inc(self.loaded, 16)
        sp.dma_start(self.rpb[:, :, :], self.rpb_t).then_inc(self.loaded, 16)
        sp.dma_start(self.mask[:, :], self.mask_d).then_inc(self.loaded, 16)

    def last_sync(self, sp):
        pass

    def tensor(self, pe, ps):
        pe.wait_ge(self.loaded, 48)
        for kc in range(GRID_W):
            n = kc // self.KC
            if kc % self.KC == 0 and n >= 4:
                pe.wait_ge(self.placed, n - 3)
            c = (kc % self.KC) * 4 * RIDX
            for i in range(2):
                last = self.nc.tensor.matmul(ps[i * GRID_W:(i + 1) * GRID_W, 4 + n % 4, c:c + 4 * RIDX],
                                             self.onehot[:, GRID_W - 1 - kc:2 * GRID_W - 1 - kc],
                                             self.rpb[:, i, :], start=True, stop=True)
            if kc % self.KC == self.KC - 1:
                last.then_inc(self.shifted, 1)

    def vector(self, dve, ps):
        for n in range(GRID_W // self.KC):
            dve.wait_ge(self.shifted, n + 1)
            m = self.mask[:, n * self.KC:(n + 1) * self.KC].unsqueeze(1).to_broadcast([P, 4 * RIDX, self.KC])
            self.nc.vector.tensor_tensor(
                self.table[:, :, n * self.KC:(n + 1) * self.KC],
                ps[:, 4 + n % 4, 0:self.KC * 4 * RIDX].rearrange("p (c r) -> p r c", c=self.KC),
                m, ALU.add).then_inc(self.placed, 1)


class Chunk:

    def __init__(self, col0, width, by, chan=False, dst=None, spill=None, at=0, silu=False, scale=None,
                 before=None):
        self.col0, self.width, self.by, self.chan, self.dst = col0, width, by, chan, dst
        self.spill, self.at, self.silu, self.scale = spill, at, silu, scale
        self.before = before
        self.jobs = 2 * (width // P) if chan else NT


class Projection:
    BANKS = 6
    RING = 3

    def __init__(self, nc, k, tag, w_dram, chunks, hT_hi, hT_lo, ps):
        self.nc, self.w_dram, self.chunks, self.hi, self.lo, self.ps = nc, w_dram, chunks, hT_hi, hT_lo, ps
        self.raw = k.sb(tag + "w_raw", [P, KT, CW])
        self.w_hi = k.sb(tag + "w_hi", [P, 2, KT, CW], F32R)
        self.w_lo = k.sb(tag + "w_lo", [P, 2, KT, CW], F32R)
        self.stage = k.sb(tag + "spill", [P, self.RING, CW])
        self.w_loaded = k.sem(tag + "w_loaded")
        self.w_hi_ready = k.sem(tag + "w_hi_ready")
        self.w_lo_ready = k.sem(tag + "w_lo_ready")
        self.job_done = k.sem(tag + "job_done")
        self.emptied = {"act": k.sem(tag + "emptied_by_act"), "dve": k.sem(tag + "emptied_by_dve")}
        self.stored = k.sems(tag + "stored", self.RING)
        self.jobs = [(c, j) for c, ch in enumerate(chunks) for j in range(ch.jobs)]

    def emptied_before(self, n, by):
        return sum(self.chunks[c].by == by for c, _ in self.jobs[:n])

    def first_job(self, c):
        return sum(ch.jobs for ch in self.chunks[:c])

    def spills(self):
        return [(c, j) for c, j in self.jobs if self.chunks[c].spill is not None]

    def load(self, sp, c):
        ch = self.chunks[c]
        if c >= 1:
            sp.wait_ge(self.w_lo_ready, c)
        src = self.w_dram[:, ch.col0:ch.col0 + ch.width].rearrange("(k p) n -> p k n", p=P)
        sp.dma_start(self.raw[:, :, 0:ch.width], src).then_inc(self.w_loaded, 16)

    def store(self, sp, n):
        c, j = self.spills()[n]
        ch = self.chunks[c]
        sp.wait_ge(self.emptied[ch.by], self.emptied_before(self.first_job(c) + j + 1, ch.by))
        sp.dma_start(rows(ch.spill, j, ch.at, ch.at + ch.width),
                     self.stage[:, n % self.RING, 0:ch.width]).then_inc(self.stored[n % self.RING], 16)

    def sync(self, sp):
        for c in range(len(self.chunks)):
            if c + 1 < len(self.chunks):
                self.load(sp, c + 1)
            for n, (cc, _) in enumerate(self.spills()):
                if cc == c:
                    self.store(sp, n)
        for s in range(self.RING):
            sp.wait_ge(self.stored[s], 16 * len(range(s, len(self.spills()), self.RING)))

    def split_hi(self, act, c):
        if c >= len(self.chunks):
            return
        w = self.chunks[c].width
        act.wait_ge(self.w_loaded, 16 * (c + 1))
        if c >= 2:
            act.wait_ge(self.job_done, self.first_job(c - 1))
        self.nc.scalar.copy(self.w_hi[:, c % 2, :, 0:w], self.raw[:, :, 0:w]).then_inc(self.w_hi_ready, 1)

    def split_lo(self, pool, c):
        w = self.chunks[c].width
        pool.wait_ge(self.w_hi_ready, c + 1)
        self.nc.gpsimd.tensor_tensor(self.w_lo[:, c % 2, :, 0:w], self.raw[:, :, 0:w],
                                     self.w_hi[:, c % 2, :, 0:w].bitcast(F32), ALU.subtract).then_inc(self.w_lo_ready, 1)

    def gpsimd(self, pool):
        for c in range(len(self.chunks)):
            self.split_lo(pool, c)

    def tensor_chunk(self, pe, c):
        ch = self.chunks[c]
        pe.wait_ge(self.w_lo_ready, c + 1)
        w_hi, w_lo = self.w_hi[:, c % 2], self.w_lo[:, c % 2]
        for j in range(ch.jobs):
            n = self.first_job(c) + j
            if n >= self.BANKS:
                by = self.chunks[self.jobs[n - self.BANKS][0]].by
                pe.wait_ge(self.emptied[by], self.emptied_before(n - self.BANKS + 1, by))
            for kt in range(KT):
                if ch.chan:
                    tile, half = j // 2, j % 2
                    cols, toks = slice(tile * P, (tile + 1) * P), slice(half * 512, half * 512 + 512)
                    out = self.ps[:, n % self.BANKS, :]
                    passes = [(w_hi[:, kt, cols], self.hi[:, kt, toks]), (w_hi[:, kt, cols], self.lo[:, kt, toks]),
                              (w_lo[:, kt, cols], self.hi[:, kt, toks])]
                else:
                    toks = slice(j * P, (j + 1) * P)
                    out = self.ps[:, n % self.BANKS, 0:ch.width]
                    passes = [(self.hi[:, kt, toks], w_hi[:, kt, 0:ch.width]),
                              (self.hi[:, kt, toks], w_lo[:, kt, 0:ch.width]),
                              (self.lo[:, kt, toks], w_hi[:, kt, 0:ch.width])]
                for i, (lhs, rhs) in enumerate(passes):
                    last = self.nc.tensor.matmul(out, lhs, rhs, start=(kt == 0 and i == 0),
                                                 stop=(kt == KT - 1 and i == 2))
            last.then_inc(self.job_done, 1)

    def empty_chunk(self, eng, by, c):
        ch = self.chunks[c]
        if ch.by != by:
            return
        for j in range(ch.jobs):
            n = self.first_job(c) + j
            eng.wait_ge(self.job_done, n + 1)
            src = self.ps[:, n % self.BANKS, 0:512 if ch.chan else ch.width]
            if ch.spill is not None:
                m = self.spills().index((c, j))
                if m >= self.RING:
                    eng.wait_ge(self.stored[m % self.RING], 16 * (m // self.RING))
                dst = self.stage[:, m % self.RING, 0:ch.width]
            else:
                if ch.before is not None:
                    ch.before(eng, j)
                dst = ch.dst(j)
            if by == "act":
                op = self.nc.scalar.activation(dst, src, ACT.Silu if ch.silu else ACT.Copy)
            elif ch.scale is not None:
                op = self.nc.vector.tensor_scalar(dst, src, ch.scale, None, ALU.mult)
            else:
                op = self.nc.vector.tensor_copy(dst, src)
            op.then_inc(self.emptied[by], 1)


def stage_project_1(nc, g, hT_hi, hT_lo):
    with ExitStack() as ctx:
        k = Kit(nc, ctx)
        ps = k.psum("p1_ps")
        qkv = g.qkv_a

        def kb_dst(base):
            return lambda j: base[:, j // 2, (j % 2) * 512:(j % 2) * 512 + 512]

        chunks = [Chunk(QA0 + c * CW, CW, "act", dst=lambda t, c=c: qkv[:, t, c * CW:(c + 1) * CW]) for c in range(3)]
        chunks += [Chunk(GA0 + c * CW, CW, "act", spill=g.gate1, at=c * CW, silu=True) for c in range(2)]
        for c in range(2):
            chunks.append(Chunk(QB0 + c * CW, CW, "dve", chan=True, scale=HD ** -0.5, dst=kb_dst(g.qbT[:, 2 * c:2 * c + 2])))
        for c in range(2):
            chunks.append(Chunk(KB0 + c * CW, CW, "dve", chan=True, dst=kb_dst(g.kbT[:, 2 * c:2 * c + 2])))
        chunks += [Chunk(VB0 + c * CW, CW, "act", spill=g.vb, at=c * CW) for c in range(2)]
        chunks += [Chunk(GB0 + c * CW, CW, "act", spill=g.gate1, at=512 + c * CW, silu=True) for c in range(2)]
        pr = Projection(nc, k, "p1_", g.w_in, chunks, hT_hi, hT_lo, ps)
        NH = A_HEADS + A_KV
        tab = k.sb("rope_tab", [P, 2, NT, HD])
        gains = k.sb("rope_gain", [P, 2, 2, HD])
        rot = k.sb("rope_rot", [P, 2, 2, HD])
        tmp = k.sb("rope_tmp", [P, NH * HD])
        tmp2 = k.sb("rope_tmp2", [P, NH * HD])
        stat = k.sb("rope_stat", [P, 3, NT * NH])
        k_twice = k.sb("k_twice", [P, 2, 4, 2, HD])
        k_doubled = k.sem("k_doubled")
        tab_loaded = k.sem("tab_loaded")
        var_ready = k.sem("rope_var_ready")
        std_ready = k.sem("rope_std_ready")
        roped = k.sem("roped")
        dve_step = k.sem("rope_step")
        k_transposed = k.sem("k_transposed")
        kk_ready = k.sem("kk_ready")
        n_a = 3 * NT
        block = ctx.enter_context(nc.Block())

        @block.sync
        def _(sp):
            pr.load(sp, 0)
            sp.dma_start(tab[:, :, :, :], g.rope).then_inc(tab_loaded, 16)
            sp.dma_start(gains[:, :, :, :], g.gain_a).then_inc(tab_loaded, 16)
            pr.sync(sp)

        @block.gpsimd
        def _(pool):
            pr.gpsimd(pool)
            pool.wait_ge(roped, NT)
            for n in range(2 * A_KV):
                kv, half = n // 2, n % 2
                if n >= 2:
                    pool.wait_ge(k_transposed, n - 1)
                src = qkv[:, 4 * half:4 * half + 4, 512 + kv * HD:512 + (kv + 1) * HD]
                nc.gpsimd.tensor_copy(k_twice[:, n % 2, :, :, :],
                                      src.unsqueeze(2).to_broadcast([P, 4, 2, HD])).then_inc(k_doubled, 1)

        @block.tensor
        def _(pe):
            for c in range(len(chunks)):
                pr.tensor_chunk(pe, c)
            for n in range(2 * A_KV):
                pe.wait_ge(k_doubled, n + 1)
                if n >= 2:
                    pe.wait_ge(kk_ready, n - 1)
                for j in range(4):
                    last = nc.tensor.transpose(ps[:, 6 + n % 2, j * P:(j + 1) * P],
                                               k_twice[:, n % 2, j, :, :].rearrange("p a d -> p (a d)"), g.ident[:, :])
                last.then_inc(k_transposed, 1)

        @block.scalar
        def _(act):
            pr.split_hi(act, 0)
            for c in range(len(chunks)):
                pr.split_hi(act, c + 1)
                pr.empty_chunk(act, "act", c)
                if c == 3:
                    act.wait_ge(var_ready, 1)
                    nc.scalar.activation(stat[:, 1, :], stat[:, 0, :], ACT.Sqrt).then_inc(std_ready, 1)

        @block.vector
        def _(dve):
            steps = 0

            def step(op):
                nonlocal steps
                steps += 1
                op.then_inc(dve_step, 1)
                dve.wait_ge(dve_step, steps)

            for t in range(NT):
                dve.wait_ge(pr.emptied["act"], 2 * NT + t + 1)
                x = qkv[:, t, 0:NH * HD]
                step(nc.vector.tensor_tensor(tmp[:, :], x, x, ALU.mult))
                step(nc.vector.tensor_reduce(stat[:, 0, t * NH:(t + 1) * NH],
                                             tmp[:, :].rearrange("p (h d) -> p h d", d=HD), AX.X, ALU.add))
            nc.vector.tensor_scalar(stat[:, 0, :], stat[:, 0, :], 1.0 / HD, EPS, ALU.mult, ALU.add).then_inc(var_ready, 1)
            dve.wait_ge(std_ready, 1)
            step(nc.vector.reciprocal(stat[:, 2, :], stat[:, 1, :]))
            q_rstd = stat[:, 2, :].rearrange("p (t h) -> p t h", h=NH)[:, :, 0:A_HEADS]
            step(nc.vector.tensor_scalar(q_rstd, q_rstd, HD ** -0.5, None, ALU.mult))
            dve.wait_ge(tab_loaded, 32)
            for t in range(NT):
                x = qkv[:, t, 0:NH * HD].rearrange("p (h d) -> p h d", d=HD)
                r = stat[:, 2, t * NH:(t + 1) * NH].unsqueeze(2).to_broadcast([P, NH, HD])
                step(nc.vector.tensor_tensor(x, x, r, ALU.mult))
                for i in range(2):
                    c = tab[:, i, t, :].unsqueeze(1).to_broadcast([P, 2, HD])
                    step(nc.vector.tensor_tensor(rot[:, i, :, :], c, gains[:, i, :, :], ALU.mult))
                for i, (h0, h1) in enumerate(((0, A_HEADS), (A_HEADS, NH))):
                    n = h1 - h0
                    xs = x[:, h0:h1, :]
                    c = rot[:, 0, i, :].unsqueeze(1).to_broadcast([P, n, HD])
                    a = tmp[:, h0 * HD:h1 * HD].rearrange("p (h d) -> p h d", d=HD)
                    b = tmp2[:, h0 * HD:h1 * HD].rearrange("p (h x s e) -> p h x s e", x=2, s=2, e=16)
                    x5 = qkv[:, t, h0 * HD:h1 * HD].rearrange("p (h x s e) -> p h x s e", x=2, s=2, e=16)
                    s5 = rot[:, 1, i, :].rearrange("p (x s e) -> p x s e", x=2, s=2)
                    nc.vector.tensor_tensor(a, xs, c, ALU.mult)
                    for half in range(2):
                        s = s5[:, :, half, :].unsqueeze(1).to_broadcast([P, n, 2, 16])
                        op = nc.vector.tensor_tensor(b[:, :, :, half, :], x5[:, :, :, 1 - half, :], s, ALU.mult)
                    step(op)
                    op = nc.vector.tensor_tensor(xs, a, tmp2[:, h0 * HD:h1 * HD].rearrange("p (h d) -> p h d", d=HD), ALU.add)
                    if i == 0:
                        step(op)
                    else:
                        op.then_inc(roped, 1)
            for c in range(len(chunks)):
                pr.empty_chunk(dve, "dve", c)
            for n in range(2 * A_KV):
                kv, half = n // 2, n % 2
                dve.wait_ge(k_transposed, n + 1)
                both = g.kk[:, kv, half * 512:half * 512 + 512]
                step(nc.vector.tensor_copy(both, ps[:, 6 + n % 2, :]))
                lo = g.kk[HD:P, kv, half * 512:half * 512 + 512]
                nc.vector.tensor_tensor(lo, ps[HD:P, 6 + n % 2, :], lo.bitcast(F32), ALU.subtract).then_inc(kk_ready, 1)



def stage_attention_a(nc, g):
    with ExitStack() as ctx:
        k = Kit(nc, ctx)
        ps = k.psum("a_ps")
        units = [(t, h) for t in range(NT) for h in range(A_HEADS)]
        n_units = len(units)
        q_hi = k.sb("a_q_hi", [P, 2, 4 * P], F32R)
        q_lo = k.sb("a_q_lo", [P, 2, 4 * P], F32R)
        q_twice = k.sb("a_q_twice", [P, 2, 4, 2, HD])
        q_doubled = k.sem("a_q_doubled")
        prob = k.sb("a_prob", [P, 2, SEQ])
        prob_t = k.sb("a_prob_t", [P, 2, SEQ])
        stat = k.sb("a_stat", [P, 3, n_units])
        q_transposed = k.sem("a_q_transposed")
        q_hi_ready = k.sem("a_q_hi_ready")
        q_lo_ready = k.sem("a_q_lo_ready")
        scores_ready = k.sem("a_scores_ready")
        max_ready = k.sem("a_max_ready")
        prob_ready = k.sem("a_prob_ready")
        half_transposed = k.sem("a_half_transposed")
        pt_first_ready = k.sem("a_pt_first_ready")
        pt_second_ready = k.sem("a_pt_second_ready")
        out_ready = k.sem("a_out_ready")
        recip_ready = k.sem("a_recip_ready")
        out_stored = k.sem("a_out_stored")
        block = ctx.enter_context(nc.Block())

        @block.gpsimd
        def _(pool):
            for grp in range(n_units // 4):
                t, h = units[4 * grp]
                if grp >= 2:
                    pool.wait_ge(q_transposed, grp - 1)
                src = g.qkv_a[:, t, h * HD:(h + 4) * HD].rearrange("p (h d) -> p h d", d=HD)
                nc.gpsimd.tensor_copy(q_twice[:, grp % 2, :, :, :],
                                      src.unsqueeze(2).to_broadcast([P, 4, 2, HD])).then_inc(q_doubled, 1)

        @block.tensor
        def _(pe):
            def turn_q(grp):
                pe.wait_ge(q_doubled, grp + 1)
                if grp >= 1:
                    pe.wait_ge(q_lo_ready, grp)
                for i in range(4):
                    last = nc.tensor.transpose(ps[:, 6, i * P:(i + 1) * P],
                                               q_twice[:, grp % 2, i, :, :].rearrange("p a d -> p (a d)"), g.ident[:, :])
                last.then_inc(q_transposed, 1)

            def scores(u):
                t, h = units[u]
                grp, i = u // 4, u % 4
                pe.wait_ge(q_lo_ready, grp + 1)
                if u >= 2:
                    pe.wait_ge(prob_ready, u - 1)
                for half in range(2):
                    keys = g.kk[:, h // GROUP, half * 512:half * 512 + 512]
                    bank = ps[:, 2 * (u % 2) + half, :]
                    nc.tensor.matmul(bank, q_hi[:, grp % 2, i * P:(i + 1) * P], keys, start=True, stop=False)
                    last = nc.tensor.matmul(bank, q_lo[:, grp % 2, i * P:(i + 1) * P], keys, start=False, stop=True)
                last.then_inc(scores_ready, 1)

            def turn_probs(u):
                pe.wait_ge(prob_ready, u + 1)
                for half in range(2):
                    if u >= 1:
                        pe.wait_ge((pt_first_ready, pt_second_ready)[half], u)
                    for j in range(4):
                        c = 4 * half + j
                        last = nc.tensor.transpose(ps[:, 4 + half, j * P:(j + 1) * P],
                                                   prob[:, u % 2, c * P:(c + 1) * P], g.ident[:, :])
                    last.then_inc(half_transposed, 1)

            def values(u):
                t, h = units[u]
                pe.wait_ge(pt_first_ready, u + 1)
                pe.wait_ge(pt_second_ready, u + 1)
                if u % 4 == 0 and u >= 4:
                    pe.wait_ge(out_stored, u // 4)
                v0 = 640 + (h // GROUP) * HD
                for c in range(NT):
                    last = nc.tensor.matmul(ps[:, 7, (u % 4) * HD:(u % 4 + 1) * HD],
                                            prob_t[:, u % 2, c * P:(c + 1) * P], g.qkv_a[:, c, v0:v0 + HD],
                                            start=(c == 0), stop=(c == NT - 1))
                last.then_inc(out_ready, 1)

            turn_q(0)
            scores(0)
            for u in range(n_units):
                if u % 4 == 1 and u // 4 + 1 < n_units // 4:
                    turn_q(u // 4 + 1)
                if u + 1 < n_units:
                    scores(u + 1)
                if u >= 1:
                    values(u - 1)
                turn_probs(u)
            values(n_units - 1)

        @block.vector
        def _(dve):
            def q_low(grp):
                dve.wait_ge(q_hi_ready, grp + 1)
                nc.vector.tensor_tensor(q_lo[:, grp % 2, :], ps[:, 6, :], q_hi[:, grp % 2, :].bitcast(F32),
                                        ALU.subtract).then_inc(q_lo_ready, 1)

            def row_max(u):
                dve.wait_ge(scores_ready, u + 1)
                s = ps[:, 2 * (u % 2):2 * (u % 2) + 2, :].rearrange("p b n -> p (b n)")
                nc.vector.tensor_reduce(stat[:, 0, u:u + 1], s, AX.X, ALU.max, negate=True).then_inc(max_ready, 1)

            def empty_second(u):
                dve.wait_ge(half_transposed, 2 * u + 2)
                if u >= 2:
                    dve.wait_ge(out_ready, u - 1)
                nc.vector.tensor_copy(prob_t[:, u % 2, 512:SEQ], ps[:, 5, :]).then_inc(pt_second_ready, 1)

            def store(grp):
                t, h = units[4 * grp]
                dve.wait_ge(prob_ready, 4 * grp + 4)
                nc.vector.reciprocal(stat[:, 2, 4 * grp:4 * grp + 4], stat[:, 1, 4 * grp:4 * grp + 4]).then_inc(recip_ready, 1)
                dve.wait_ge(recip_ready, grp + 1)
                dve.wait_ge(out_ready, 4 * grp + 4)
                out = g.qkv_a[:, t, h * HD:(h + 4) * HD].rearrange("p (h d) -> p h d", d=HD)
                nc.vector.tensor_tensor(out, ps[:, 7, 0:4 * HD].rearrange("p (h d) -> p h d", d=HD),
                                        stat[:, 2, 4 * grp:4 * grp + 4].unsqueeze(2).to_broadcast([P, 4, HD]),
                                        ALU.mult).then_inc(out_stored, 1)

            q_low(0)
            row_max(0)
            for u in range(n_units):
                if u % 4 == 1 and u // 4 + 1 < n_units // 4:
                    q_low(u // 4 + 1)
                if u + 1 < n_units:
                    row_max(u + 1)
                if u % 4 == 0 and u >= 4:
                    store(u // 4 - 1)
                empty_second(u)
            store(n_units // 4 - 1)

        @block.scalar
        def _(act):
            def q_high(grp):
                act.wait_ge(q_transposed, grp + 1)
                if grp >= 2:
                    act.wait_ge(scores_ready, 4 * (grp - 1))
                nc.scalar.copy(q_hi[:, grp % 2, :], ps[:, 6, :]).then_inc(q_hi_ready, 1)

            def exponentials(u):
                act.wait_ge(max_ready, u + 1)
                if u >= 2:
                    act.wait_ge(half_transposed, 2 * (u - 1))
                s = ps[:, 2 * (u % 2):2 * (u % 2) + 2, :].rearrange("p b n -> p (b n)")
                nc.scalar.activation(prob[:, u % 2, :], s, ACT.Exp, bias=stat[:, 0, u:u + 1],
                                     accum_out=stat[:, 1, u:u + 1]).then_inc(prob_ready, 1)

            def empty_first(u):
                act.wait_ge(half_transposed, 2 * u + 1)
                if u >= 2:
                    act.wait_ge(out_ready, u - 1)
                nc.scalar.copy(prob_t[:, u % 2, 0:512], ps[:, 4, :]).then_inc(pt_first_ready, 1)

            q_high(0)
            exponentials(0)
            for u in range(n_units):
                if u % 4 == 1 and u // 4 + 1 < n_units // 4:
                    q_high(u // 4 + 1)
                if u + 1 < n_units:
                    exponentials(u + 1)
                empty_first(u)


def stage_attention_b(nc, g, w_hi, w_lo):
    with ExitStack() as ctx:
        k = Kit(nc, ctx)
        ws = WeightSplit(nc, k, "b_w_", g.w_out, w_hi, w_lo)
        ps = k.psum("b_ps")
        PAIRS = B_HEADS // 2
        units = [(p, r) for p in range(PAIRS) for r in range(ROWS)]
        n_units = len(units)
        W = NA_KH * GRID_W
        v = k.sb("b_v", [P, NT, 512])
        q_diag = k.sb("b_q_diag", [P, 2, P])
        prob = k.sb("b_prob", [P, 2, W + 2 * GRID_W])
        prob_t = k.sb("b_prob_t", [P, 2, 5 * P])
        out = k.sb("b_out", [P, 2, ROWS, HD])
        stat = k.sb("b_stat", [P, 3, n_units])
        v_loaded = k.sem("b_v_loaded")
        q_zeroed = k.sem("b_q_zeroed")
        margins_zeroed = k.sem("b_margins_zeroed")
        q_placed = k.sem("b_q_placed")
        scores_ready = k.sem("b_scores_ready")
        max_ready = k.sem("b_max_ready")
        prob_ready = k.sem("b_prob_ready")
        turned_first = k.sem("b_turned_first")
        turned_second = k.sem("b_turned_second")
        pt_first_ready = k.sem("b_pt_first_ready")
        pt_second_ready = k.sem("b_pt_second_ready")
        out_ready = k.sem("b_out_ready")
        recip_ready = k.sem("b_recip_ready")
        out_stored = k.sem("b_out_stored")
        pair_sent = k.sems("b_pair_sent", 2)

        def window(r):
            r0 = min(max(r - NA_KH // 2, 0), ROWS - NA_KH)
            return r0, r0 // 2, 4 + r0 % 2, GRID_W * (1 - r0 % 2)

        block = ctx.enter_context(nc.Block())

        @block.sync
        def _(sp):
            sp.dma_start(v[:, :, :], g.vb.rearrange("(t p) c -> p t c", p=P)).then_inc(v_loaded, 16)
            for kt in range(KT):
                ws.load(sp, kt)
            for p in range(PAIRS):
                sp.wait_ge(out_stored, 2 * ROWS * (p + 1))
                for i in range(2):
                    h = 2 * p + i
                    dst = g.out_b[:, h * HD:(h + 1) * HD].rearrange("(r c) d -> c r d", c=GRID_W)
                    sp.dma_start(dst, out[i * HD:(i + 1) * HD, p % 2, :, :]).then_inc(pair_sent[p % 2], 16)
            for i in range(2):
                sp.wait_ge(pair_sent[i], 32 * (PAIRS // 2))

        @block.gpsimd
        def _(pool):
            nc.gpsimd.memset(q_diag[:, :, :], 0.0).then_inc(q_zeroed, 1)
            nc.gpsimd.memset(prob[:, :, :], 0.0).then_inc(margins_zeroed, 1)
            pool.wait_ge(q_zeroed, 1)
            pool.wait_ge(margins_zeroed, 1)
            for u, (p, r) in enumerate(units):
                if u >= 2:
                    pool.wait_ge(scores_ready, u - 1)
                for i in range(2):
                    half = slice(i * HD, (i + 1) * HD)
                    nc.gpsimd.tensor_copy(q_diag[half, u % 2, half],
                                          g.qbT[half, p, r * GRID_W:(r + 1) * GRID_W]).then_inc(q_placed, 1)
                    pool.wait_ge(q_placed, 2 * u + i + 1)
                if u % 4 == 3 and u // 4 < KT:
                    ws.split(pool, u // 4)
                    pool.wait_ge(ws.lo_ready, u // 4 + 1)

        @block.tensor
        def _(pe):
            def scores(u):
                p, r = units[u]
                r0 = window(r)[0]
                pe.wait_ge(q_placed, 2 * u + 2)
                if u >= 2:
                    pe.wait_ge(max_ready, u - 1)
                nc.tensor.matmul(ps[:, u % 2, :], q_diag[:, u % 2, :], g.kbT[:, p, r0 * GRID_W:r0 * GRID_W + W],
                                 start=True, stop=True).then_inc(scores_ready, 1)

            def turn_probs(u):
                _, _, tiles, c0 = window(units[u][1])
                pe.wait_ge(prob_ready, u + 1)
                if u >= 2:
                    pe.wait_ge(pt_first_ready, u - 1)
                    pe.wait_ge(pt_second_ready, u - 1)
                for j in range(tiles):
                    bank, at = (2 * (u % 2) + 2, j) if j < 2 else (2 * (u % 2) + 3, j - 2)
                    op = nc.tensor.transpose(ps[:, bank, at * P:(at + 1) * P],
                                             prob[:, u % 2, c0 + j * P:c0 + (j + 1) * P], g.ident[:, :])
                    if j == 1:
                        op.then_inc(turned_first, 1)
                    if j == tiles - 1:
                        op.then_inc(turned_second, 1)

            def values(u):
                p, r = units[u]
                _, t0, tiles, _ = window(r)
                pe.wait_ge(pt_first_ready, u + 1)
                pe.wait_ge(pt_second_ready, u + 1)
                if u == 0:
                    pe.wait_ge(v_loaded, 16)
                if u >= 2:
                    pe.wait_ge(out_stored, 2 * (u - 1))
                for j in range(tiles):
                    last = nc.tensor.matmul(ps[:, 6 + u % 2, 0:P], prob_t[:, u % 2, j * P:(j + 1) * P],
                                            v[:, t0 + j, p * P:(p + 1) * P], start=(j == 0), stop=(j == tiles - 1))
                last.then_inc(out_ready, 1)

            scores(0)
            for u in range(n_units):
                if u + 1 < n_units:
                    scores(u + 1)
                if u >= 1:
                    values(u - 1)
                turn_probs(u)
            values(n_units - 1)

        @block.vector
        def _(dve):
            def bias_and_max(u):
                p, r = units[u]
                first = window(r)[0] - r + NA_KH - 1
                dve.wait_ge(scores_ready, u + 1)
                if u >= 2:
                    dve.wait_ge(turned_second, u - 1)
                bias = g.na_table[:, p * RIDX + first:p * RIDX + first + NA_KH, :].rearrange("p r c -> p (r c)")
                nc.vector.tensor_tensor_reduce(prob[:, u % 2, GRID_W:GRID_W + W], ps[:, u % 2, :], bias, -1.0, -NEG,
                                               ALU.add, ALU.min, stat[:, 0, u:u + 1]).then_inc(max_ready, 1)

            def empty_second(u):
                n = window(units[u][1])[2] - 2
                dve.wait_ge(turned_second, u + 1)
                if u >= 2:
                    dve.wait_ge(out_ready, u - 1)
                nc.vector.tensor_copy(prob_t[:, u % 2, 2 * P:(2 + n) * P],
                                      ps[:, 2 * (u % 2) + 3, 0:n * P]).then_inc(pt_second_ready, 1)

            def store(u):
                p, r = units[u]
                dve.wait_ge(prob_ready, u + 1)
                nc.vector.reciprocal(stat[:, 2, u:u + 1], stat[:, 1, u:u + 1]).then_inc(recip_ready, 1)
                dve.wait_ge(recip_ready, u + 1)
                dve.wait_ge(out_ready, u + 1)
                if r == 0 and p >= 2:
                    dve.wait_ge(pair_sent[p % 2], 32)
                for i in range(2):
                    half = slice(i * HD, (i + 1) * HD)
                    nc.vector.tensor_scalar(out[half, p % 2, r, :], ps[half, 6 + u % 2, half],
                                            stat[half, 2, u:u + 1], None, ALU.mult).then_inc(out_stored, 1)

            dve.wait_ge(margins_zeroed, 1)
            bias_and_max(0)
            for u in range(n_units):
                if u + 1 < n_units:
                    bias_and_max(u + 1)
                if u >= 2:
                    store(u - 2)
                empty_second(u)
            store(n_units - 2)
            store(n_units - 1)

        @block.scalar
        def _(act):
            def exponentials(u):
                act.wait_ge(max_ready, u + 1)
                s = prob[:, u % 2, GRID_W:GRID_W + W]
                nc.scalar.activation(s, s, ACT.Exp, bias=stat[:, 0, u:u + 1], scale=-1.0,
                                     accum_out=stat[:, 1, u:u + 1]).then_inc(prob_ready, 1)

            def empty_first(u):
                act.wait_ge(turned_first, u + 1)
                if u >= 2:
                    act.wait_ge(out_ready, u - 1)
                nc.scalar.copy(prob_t[:, u % 2, 0:2 * P], ps[:, 2 * (u % 2) + 2, 0:2 * P]).then_inc(pt_first_ready, 1)

            exponentials(0)
            for u in range(n_units):
                if u + 1 < n_units:
                    exponentials(u + 1)
                empty_first(u)


class WeightSplit:

    def __init__(self, nc, k, tag, w_dram, w_hi, w_lo):
        self.nc, self.w_dram, self.hi, self.lo = nc, w_dram, w_hi, w_lo
        self.raw = k.sb(tag + "raw", [P, 2, D])
        self.loaded = k.sems(tag + "loaded", 2)
        self.hi_ready = k.sem(tag + "hi_ready")
        self.lo_ready = k.sem(tag + "lo_ready")

    def load(self, sp, kt):
        if kt >= 2:
            sp.wait_ge(self.lo_ready, kt - 1)
        sp.dma_start(self.raw[:, kt % 2, :], rows(self.w_dram, kt)).then_inc(self.loaded[kt % 2], 16)

    def split(self, pool, kt):
        pool.wait_ge(self.loaded[kt % 2], 16 * (kt // 2 + 1))
        self.nc.gpsimd.tensor_copy(self.hi[:, kt, :], self.raw[:, kt % 2, :]).then_inc(self.hi_ready, 1)
        pool.wait_ge(self.hi_ready, kt + 1)
        self.nc.gpsimd.tensor_tensor(self.lo[:, kt, :], self.raw[:, kt % 2, :], self.hi[:, kt, :].bitcast(F32),
                                     ALU.subtract).then_inc(self.lo_ready, 1)


class OutProjection:

    def __init__(self, nc, k, tag, g, ps, w_hi, w_lo, mixed, mixed_ready):
        self.nc, self.g, self.ps, self.w_hi, self.w_lo = nc, g, ps, w_hi, w_lo
        self.mixed, self.mixed_ready = mixed, mixed_ready
        self.hi = k.sb(tag + "mT_hi", [P, 2, KT, P], F32R)
        self.lo = k.sb(tag + "mT_lo", [P, 2, KT, P], F32R)
        self.half_turned = k.sem(tag + "half_turned")
        self.hi_ready = k.sem(tag + "mT_hi_ready")
        self.lo_ready = k.sem(tag + "mT_lo_ready")
        self.job_done = k.sem(tag + "job_done")
        self.job_emptied = k.sem(tag + "job_emptied")

    def turn(self, pe, t):
        for half in range(2):
            n = 2 * t + half
            pe.wait_ge(self.mixed_ready[half], t + 1)
            if n >= 4:
                pe.wait_ge(self.lo_ready, n - 3)
            for j in range(4):
                c = 4 * half + j
                last = self.nc.tensor.transpose(self.ps[:, n % 4, j * P:(j + 1) * P],
                                                self.mixed[:, t % 2, c * P:(c + 1) * P], self.g.ident[:, :])
            last.then_inc(self.half_turned, 1)

    def multiply(self, pe, t):
        pe.wait_ge(self.lo_ready, 2 * t + 2)
        for half in range(2):
            n = 2 * t + half
            if n >= 4:
                pe.wait_ge(self.job_emptied, n - 3)
            cols = slice(half * 512, half * 512 + 512)
            for kt in range(KT):
                hi, lo = self.hi[:, t % 2, kt, :], self.lo[:, t % 2, kt, :]
                for i, (a, b) in enumerate(((hi, self.w_hi), (hi, self.w_lo), (lo, self.w_hi))):
                    last = self.nc.tensor.matmul(self.ps[:, 4 + n % 4, :], a, b[:, kt, cols],
                                                 start=(kt == 0 and i == 0), stop=(kt == KT - 1 and i == 2))
            last.then_inc(self.job_done, 1)

    def tensor(self, pe):
        self.turn(pe, 0)
        for t in range(NT):
            if t + 1 < NT:
                self.turn(pe, t + 1)
            self.multiply(pe, t)

    def split_hi(self, act, t):
        for half in range(2):
            n = 2 * t + half
            act.wait_ge(self.half_turned, n + 1)
            if n >= 4:
                act.wait_ge(self.job_done, 2 * (t - 1))
            self.nc.scalar.copy(self.hi[:, t % 2, 4 * half:4 * half + 4, :],
                                self.ps[:, n % 4, :].rearrange("p (k c) -> p k c", k=4)).then_inc(self.hi_ready, 1)

    def split_lo(self, dve, t):
        for half in range(2):
            n = 2 * t + half
            dve.wait_ge(self.hi_ready, n + 1)
            hi = self.hi[:, t % 2, 4 * half:4 * half + 4, :]
            self.nc.vector.tensor_tensor(self.lo[:, t % 2, 4 * half:4 * half + 4, :],
                                         self.ps[:, n % 4, :].rearrange("p (k c) -> p k c", k=4),
                                         hi.bitcast(F32), ALU.subtract).then_inc(self.lo_ready, 1)

    def add_residual(self, dve, t, y, x):
        for half in range(2):
            n = 2 * t + half
            cols = slice(half * 512, half * 512 + 512)
            dve.wait_ge(self.job_done, n + 1)
            self.nc.vector.tensor_tensor(y[:, cols], self.ps[:, 4 + n % 4, :], x[:, cols],
                                         ALU.add).then_inc(self.job_emptied, 1)


def stage_out_1(nc, g, w_hi, w_lo):
    with ExitStack() as ctx:
        k = Kit(nc, ctx)
        ps = k.psum("o1_ps")
        gate = k.sb("o1_gate", [P, 2, D])
        out_b = k.sb("o1_out_b", [P, 2, 512])
        x = k.sb("o1_x", [P, 2, D])
        mixed = k.sb("o1_mixed", [P, 2, D])
        y = k.sb("o1_y", [P, 2, D])
        junk = k.sb("o1_junk", [P, D])
        gain = k.sb("o1_gain", [P, D])
        stat = k.sb("o1_stat", [P, 4, NT])
        gate_loaded = k.sems("o1_gate_loaded", 2)
        b_loaded = k.sems("o1_b_loaded", 2)
        x_loaded = k.sems("o1_x_loaded", 2)
        gain_loaded = k.sem("o1_gain_loaded")
        mixed_a_ready = k.sem("o1_mixed_a_ready")
        mixed_b_ready = k.sem("o1_mixed_b_ready")
        squares_summed = k.sem("o1_squares_summed")
        var_ready = k.sem("o1_var_ready")
        std_ready = k.sem("o1_std_ready")
        rstd_ready = k.sem("o1_rstd_ready")
        y_ready = k.sem("o1_y_ready")
        y_stored = k.sems("o1_y_stored", 2)
        op = OutProjection(nc, k, "o1_", g, ps, w_hi, w_lo, mixed, (mixed_a_ready, mixed_b_ready))
        block = ctx.enter_context(nc.Block())

        @block.sync
        def _(sp):
            def load(t):
                if t >= 2:
                    sp.wait_ge(mixed_a_ready, t - 1)
                    sp.wait_ge(mixed_b_ready, t - 1)
                sp.dma_start(gate[:, t % 2, :], rows(g.gate1, t)).then_inc(gate_loaded[t % 2], 16)
                sp.dma_start(out_b[:, t % 2, :], rows(g.out_b, t)).then_inc(b_loaded[t % 2], 16)
                if t >= 2:
                    sp.wait_ge(op.job_emptied, 2 * (t - 1))
                sp.dma_start(x[:, t % 2, :], rows(g.x, t)).then_inc(x_loaded[t % 2], 16)

            def store(t):
                sp.wait_ge(y_ready, t + 1)
                sp.dma_start(rows(g.x1, t), y[:, t % 2, :]).then_inc(y_stored[t % 2], 16)

            load(0)
            load(1)
            sp.dma_start(gain[:, :], g.final_gain).then_inc(gain_loaded, 16)
            for t in range(2, NT):
                load(t)
                store(t - 2)
            store(NT - 2)
            store(NT - 1)
            for i in range(2):
                sp.wait_ge(y_stored[i], 16 * (NT // 2))

        @block.gpsimd
        def _(pool):
            for t in range(NT):
                if t >= 2:
                    pool.wait_ge(op.half_turned, 2 * (t - 1))
                pool.wait_ge(gate_loaded[t % 2], 16 * (t // 2 + 1))
                nc.gpsimd.tensor_tensor(mixed[:, t % 2, 0:512], g.qkv_a[:, t, 0:512], gate[:, t % 2, 0:512],
                                        ALU.mult).then_inc(mixed_a_ready, 1)
                pool.wait_ge(b_loaded[t % 2], 16 * (t // 2 + 1))
                nc.gpsimd.tensor_tensor(mixed[:, t % 2, 512:D], out_b[:, t % 2, :], gate[:, t % 2, 512:D],
                                        ALU.mult).then_inc(mixed_b_ready, 1)

        @block.tensor
        def _(pe):
            op.tensor(pe)

        @block.scalar
        def _(act):
            def norm(t):
                act.wait_ge(op.job_emptied, 2 * t + 2)
                nc.scalar.activation(junk[:, :], y[:, t % 2, :], ACT.Square,
                                     accum_out=stat[:, 0, t:t + 1]).then_inc(squares_summed, 1)
                act.wait_ge(var_ready, t + 1)
                nc.scalar.activation(stat[:, 2, t:t + 1], stat[:, 1, t:t + 1], ACT.Sqrt).then_inc(std_ready, 1)

            op.split_hi(act, 0)
            for t in range(NT):
                if t + 1 < NT:
                    op.split_hi(act, t + 1)
                norm(t)

        @block.vector
        def _(dve):
            def norm(t):
                dve.wait_ge(squares_summed, t + 1)
                nc.vector.tensor_scalar(stat[:, 1, t:t + 1], stat[:, 0, t:t + 1], 1.0 / D, EPS,
                                        ALU.mult, ALU.add).then_inc(var_ready, 1)
                dve.wait_ge(std_ready, t + 1)
                nc.vector.reciprocal(stat[:, 3, t:t + 1], stat[:, 2, t:t + 1]).then_inc(rstd_ready, 1)
                dve.wait_ge(rstd_ready, t + 1)
                if t == 0:
                    dve.wait_ge(gain_loaded, 16)
                yt = y[:, t % 2, :]
                nc.vector.scalar_tensor_tensor(yt, yt, stat[:, 3, t:t + 1], gain[:, :],
                                               ALU.mult, ALU.mult).then_inc(y_ready, 1)

            op.split_lo(dve, 0)
            for t in range(NT):
                if t + 1 < NT:
                    op.split_lo(dve, t + 1)
                dve.wait_ge(x_loaded[t % 2], 16 * (t // 2 + 1))
                if t >= 2:
                    dve.wait_ge(y_stored[t % 2], 16 * (t // 2))
                op.add_residual(dve, t, y[:, t % 2, :], x[:, t % 2, :])
                norm(t)


class DilatedTable:

    LINE = 384

    def __init__(self, k, nc, lines_dram, onehot_d, rel_d, places):
        self.nc, self.lines_dram, self.onehot_d, self.rel_d = nc, lines_dram, onehot_d, rel_d
        self.onehot = k.sb("di_onehot", [33, 3, self.LINE])
        self.rel = k.sb("di_rel", [33, ATT_HEADS])
        self.lines = [t[:, :, :].rearrange("p a b -> p (a b)")[:, 0:ATT_HEADS * self.LINE] for t in places]
        self.loaded = k.sem("di_loaded")
        self.line_ready = k.sem("di_line_ready")
        self.line_copied = k.sem("di_line_copied")
        self.stored = k.sem("di_stored")

    def sync(self, sp):
        sp.dma_start(self.onehot[:, :, :], self.onehot_d).then_inc(self.loaded, 16)
        sp.dma_start(self.rel[:, :], self.rel_d).then_inc(self.loaded, 16)

    def last_sync(self, sp):
        sp.wait_ge(self.line_copied, 3 * ATT_HEADS)
        for p in range(3):
            dst = self.lines_dram[:, p * ATT_HEADS:(p + 1) * ATT_HEADS, :].rearrange("q h u -> q (h u)")
            sp.dma_start(dst, self.lines[p]).then_inc(self.stored, 16)
        sp.wait_ge(self.stored, 48)

    def tensor(self, pe, ps):
        pe.wait_ge(self.loaded, 32)
        for n in range(3 * ATT_HEADS):
            if n >= 4:
                pe.wait_ge(self.line_copied, n - 3)
            p, h = n // ATT_HEADS, n % ATT_HEADS
            self.nc.tensor.matmul(ps[:, 4 + n % 4, 0:self.LINE], self.rel[:, h:h + 1].to_broadcast([33, P]),
                                  self.onehot[:, p, :], start=True, stop=True).then_inc(self.line_ready, 1)

    def vector(self, dve, ps):
        for n in range(3 * ATT_HEADS):
            dve.wait_ge(self.line_ready, n + 1)
            p, h = n // ATT_HEADS, n % ATT_HEADS
            self.nc.vector.tensor_copy(self.lines[p][:, h * self.LINE:(h + 1) * self.LINE], ps[:, 4 + n % 4, 0:self.LINE]).then_inc(self.line_copied, 1)


def stage_project_2(nc, g, hT_hi, hT_lo):
    with ExitStack() as ctx:
        k = Kit(nc, ctx)
        ps = k.psum("p2_ps")
        att_tok = g.qkT[:, :, :]
        conv_in = k.sb("conv_in", [P, 2, SEQ + 3])
        conv_y = k.sb("conv_y", [P, 2, SEQ])
        conv_w = k.sb("p2_conv_w", [P, 12, 4])
        gain = k.sb("p2_att_gain", [P, 2, HD])
        stat = k.sb("att_stat", [P, 3, NT * 16])
        nstat = k.sb("l2_stat", [P, 2, 64])
        consts_loaded = k.sem("p2_consts_loaded")
        var_ready = k.sem("att_var_ready")
        std_ready = k.sem("att_std_ready")
        att_normed = k.sem("att_normed")
        att_turned = k.sem("att_turned")
        att_placed = k.sem("att_placed")
        dve_step = k.sem("p2_dve_step")
        pads_zeroed = k.sem("pads_zeroed")
        conv_done = k.sem("conv_done")
        silu_done = k.sem("silu_done")
        squared = k.sem("l2_squared")
        l2_summed = k.sem("l2_summed")
        l2_var_ready = k.sem("l2_var_ready")
        l2_std_ready = k.sem("l2_std_ready")

        slots = [8, 9, 10, 11, 0, 1, 2, 3, 4, 5, 6, 7]
        att = [Chunk(AQ2 + c * CW, CW, "act", dst=lambda t, c=c: att_tok[:, t, c * CW:(c + 1) * CW]) for c in range(4)]
        small = [Chunk(BA2, 8, "act", dst=lambda t: g.ba[:, t, :])]
        spills = [Chunk(AV2 + c * CW, CW, "act", spill=g.v_att, at=c * CW) for c in range(2)]
        spills += [Chunk(AG2 + c * CW, CW, "act", spill=g.gate2, at=c * CW, silu=True) for c in range(2)]
        spills += [Chunk(Z2 + c * CW, CW, "act", spill=g.z, at=c * CW, silu=True) for c in range(2)]

        def conv_chunk(i):
            def before(act, j):
                n = 2 * i + j // 2
                if j % 2 == 0 and n >= 2:
                    act.wait_ge(conv_done, n - 1)
                if n < 2 and j == 0:
                    act.wait_ge(pads_zeroed, 1)

            def dst(j):
                n, half = 2 * i + j // 2, j % 2
                return conv_in[:, n % 2, 3 + half * 512:3 + half * 512 + 512]

            col = slots[2 * i] * P
            return Chunk(col, CW, "act", chan=True, dst=dst, before=before)

        conv = [conv_chunk(i) for i in range(6)]
        chunks = att + small + spills + conv
        first_conv = len(chunks) - 6
        TURN_AT = 8
        pr = Projection(nc, k, "p2_", g.w_in2, chunks, hT_hi, hT_lo, ps)
        block = ctx.enter_context(nc.Block())

        @block.sync
        def _(sp):
            pr.load(sp, 0)
            sp.dma_start(conv_w[:, :, :], g.conv_w).then_inc(consts_loaded, 16)
            sp.dma_start(gain[:, :, :], g.att_gain).then_inc(consts_loaded, 16)
            pr.sync(sp)

        @block.gpsimd
        def _(pool):
            nc.gpsimd.memset(conv_in[:, :, 0:3], 0.0).then_inc(pads_zeroed, 1)
            pr.gpsimd(pool)

        @block.tensor
        def _(pe):
            def l2_sums(s):
                pe.wait_ge(squared, s + 1)
                if s == 0:
                    pe.wait_ge(att_placed, 2 * NT)
                for t in range(NT):
                    last = nc.tensor.matmul(ps[:, 7, s * NT + t:s * NT + t + 1], conv_y[:, s % 2, t * P:(t + 1) * P],
                                            g.ones[:, 0:1], start=True, stop=True)
                last.then_inc(l2_summed, 1)

            for c in range(len(chunks)):
                pr.tensor_chunk(pe, c)
                if c == TURN_AT:
                    for n in range(2 * NT):
                        t, which = n // 2, n % 2
                        pe.wait_ge(att_normed, t + 1)
                        if n >= 2:
                            pe.wait_ge(att_placed, n - 1)
                        for j in range(4):
                            c0 = which * 512 + j * P
                            last = nc.tensor.transpose(ps[:, 6 + n % 2, j * P:(j + 1) * P],
                                                       att_tok[:, t, c0:c0 + P], g.ident[:, :])
                        last.then_inc(att_turned, 1)
                if c - first_conv >= 3:
                    s = 2 * (c - first_conv - 3)
                    l2_sums(s)
                    l2_sums(s + 1)
            l2_sums(6)
            l2_sums(7)

        @block.scalar
        def _(act):
            def silu(n):
                act.wait_ge(conv_done, n + 1)
                if n == 4:
                    act.wait_ge(att_turned, 2 * NT)
                dst = g.qkT[:, slots[n], :] if n >= 4 else g.vT[:, n, :]
                nc.scalar.activation(dst, conv_y[:, n % 2, :], ACT.Silu).then_inc(silu_done, 1)
                if n >= 4:
                    act.wait_ge(silu_done, n + 1)
                    nc.scalar.activation(conv_y[:, n % 2, :], dst, ACT.Square).then_inc(squared, 1)

            pr.split_hi(act, 0)
            for c in range(len(chunks)):
                pr.split_hi(act, c + 1)
                if c > first_conv:
                    silu(2 * (c - first_conv) - 2)
                    silu(2 * (c - first_conv) - 1)
                pr.empty_chunk(act, "act", c)
                if c == 5:
                    act.wait_ge(var_ready, 1)
                    nc.scalar.activation(stat[:, 1, :], stat[:, 0, :], ACT.Sqrt).then_inc(std_ready, 1)
            silu(10)
            silu(11)
            act.wait_ge(l2_var_ready, 1)
            nc.scalar.activation(nstat[:, 1, :], nstat[:, 0, :], ACT.Sqrt).then_inc(l2_std_ready, 1)

        @block.vector
        def _(dve):
            steps = 0

            def step(op):
                nonlocal steps
                steps += 1
                op.then_inc(dve_step, 1)
                dve.wait_ge(dve_step, steps)

            for t in range(NT):
                dve.wait_ge(pr.emptied["act"], 3 * NT + t + 1)
                x = att_tok[:, t, :]
                step(nc.vector.tensor_tensor(conv_y[:, 0, :], x, x, ALU.mult))
                step(nc.vector.tensor_reduce(stat[:, 0, t * 16:(t + 1) * 16],
                                             conv_y[:, 0, :].rearrange("p (h d) -> p h d", d=HD), AX.X, ALU.add))
            nc.vector.tensor_scalar(stat[:, 0, :], stat[:, 0, :], 1.0 / HD, EPS, ALU.mult, ALU.add).then_inc(var_ready, 1)
            dve.wait_ge(std_ready, 1)
            step(nc.vector.reciprocal(stat[:, 2, :], stat[:, 1, :]))
            q_rstd = stat[:, 2, :].rearrange("p (t h) -> p t h", h=16)[:, :, 0:ATT_HEADS]
            step(nc.vector.tensor_scalar(q_rstd, q_rstd, HD ** -0.5, None, ALU.mult))
            dve.wait_ge(consts_loaded, 32)
            for t in range(NT):
                x = att_tok[:, t, :].rearrange("p (h d) -> p h d", d=HD)
                step(nc.vector.tensor_tensor(x, x, stat[:, 2, t * 16:(t + 1) * 16].unsqueeze(2).to_broadcast([P, 16, HD]),
                                             ALU.mult))
                x4 = att_tok[:, t, :].rearrange("p (w h d) -> p w h d", w=2, d=HD)
                nc.vector.tensor_tensor(x4, x4, gain[:, :, :].unsqueeze(2).to_broadcast([P, 2, 8, HD]),
                                        ALU.mult).then_inc(att_normed, 1)
            for n in range(2 * NT):
                t, which = n // 2, n % 2
                dve.wait_ge(att_turned, n + 1)
                dst = (g.att_qT, g.att_kT)[which]
                nc.vector.tensor_copy(dst[:, :, t * P:(t + 1) * P],
                                      ps[:, 6 + n % 2, :].rearrange("p (k c) -> p k c", k=4)).then_inc(att_placed, 1)
            for n in range(12):
                s = slots[n]
                dve.wait_ge(pr.emptied["act"], pr.emptied_before(pr.first_job(first_conv) + 2 * n + 2, "act"))
                if 2 <= n < 6:
                    dve.wait_ge(silu_done, n - 1)
                elif n >= 6:
                    dve.wait_ge(l2_summed, n - 5)
                y = conv_y[:, n % 2, :]
                step(nc.vector.tensor_scalar(y, conv_in[:, n % 2, 3:3 + SEQ], conv_w[:, s, 3:4], None, ALU.mult))
                for i in (2, 1, 0):
                    op = nc.vector.scalar_tensor_tensor(y, conv_in[:, n % 2, i:i + SEQ], conv_w[:, s, i:i + 1], y,
                                                        ALU.mult, ALU.add)
                    if i:
                        step(op)
                    else:
                        op.then_inc(conv_done, 1)
            dve.wait_ge(l2_summed, 8)
            nc.vector.tensor_scalar(nstat[:, 0, :], ps[:, 7, 0:64], EPS, None, ALU.add).then_inc(l2_var_ready, 1)
            dve.wait_ge(l2_std_ready, 1)
            step(nc.vector.reciprocal(g.l2[:, :], nstat[:, 1, :]))
            step(nc.vector.tensor_scalar(g.l2[:, 0:32], g.l2[:, 0:32], DK ** -0.5, None, ALU.mult))


def stage_delta(nc, g):
    H4 = DN_HEADS
    with ExitStack() as ctx:
        k = Kit(nc, ctx)
        ps = k.psum("d_ps")
        upper = k.sb("d_upper", [P, P])
        strict = k.sb("d_strict", [P, P])
        levels = k.sb("d_levels", [P, LEVELS, P])
        ab = k.sb("d_ab", [P, 2, H4])
        sc = k.sb("d_sc", [P, 8, NT, H4])
        beta, gg, gc, egc, be = (k.sb(n, [P, NT, H4]) for n in ("d_beta", "d_g", "d_gc", "d_egc", "d_be"))
        dd = k.sb("d_dd", [P, 2, H4, P])
        dec = k.sb("d_dec", [P, 2, H4, P])
        tl = k.sb("d_tl", [P, 12])
        etl = k.sb("d_etl", [P, 3, 12])
        khat = k.sb("d_khat", [P, H4, P])
        khatT = k.sb("d_khatT", [P, H4, P])
        kbe = k.sb("d_kbe", [P, 2, H4, P])
        vb = k.sb("d_vb", [P, 2, H4, P])
        ktail = k.sb("d_ktail", [P, 3, H4, P])
        attnT = k.sb("d_attnT", [P, 3, H4, P])
        A = k.sb("d_A", [P, H4, P])
        Al = k.sb("d_Al", [P, 2, LEVELS, H4, P])
        T = k.sb("d_T", [P, 2, H4, P])
        X = k.sb("d_X", [P, 2, H4, P])
        Z = k.sb("d_Z", [P, H4, P])
        u = k.sb("d_u", [P, 2, H4, P])
        wT = k.sb("d_wT", [P, 2, H4, P])
        S = k.sb("d_S", [P, H4, P])
        Sg = k.sb("d_Sg", [P, H4, P])
        vnew = k.sb("d_vnew", [P, H4, P])
        oq = k.sb("d_oq", [P, H4, P])
        osq = k.sb("d_osq", [P, H4, P])

        def bank(b):
            return ps[:, b, :].rearrange("p (h c) -> p h c", h=H4)

        names = ("consts gate_dve gate_act g_ready gc_ready gates_ready gc_copied "
                 "gcb_ready kt_ready vt_ready diffs_done decays_done dec_masked decT_masked khat_ready khatT_turned "
                 "khatT_ready kbe_ready ktail_ready vb_ready G_ready A_ready attn_ready attnT_ready level_masked "
                 "T0_ready X0_turned X0_ready Z_ready Z_copied dX_ready dT_ready X_ready T_ready u_ready w_ready "
                 "u_copied w_copied wS_ready vnew_ready av_ready dS_ready S_ready Sg_ready oq_ready o_ready osq_ready "
                 "S_zeroed o_summed strict_done be_ready").split()
        s = {n: k.sem("d_" + n) for n in names}
        block = ctx.enter_context(nc.Block())
        N = NT

        def order(i, front, inv, rec):
            f, v, r = i < N, 0 <= i - 1 < N, 0 <= i - 2 < N
            if v:
                inv.z(i - 1, 1)
            if f:
                front.first(i)
            for l in range(1, LEVELS):
                if v and l >= 2:
                    inv.z(i - 1, l)
                if f and l >= 2:
                    (front.khat_turn, front.gram, front.attn, front.x0)[l - 2](i)
                if v:
                    inv.update(i - 1, l)
                if r and l <= 4:
                    (rec.read, rec.write)[(l - 1) % 2](i - 2, (l - 1) // 2)
            if v:
                inv.apply(i - 1)

        @block.sync
        def _(sp):
            sp.dma_start(upper[:, :], g.d_upper).then_inc(s["consts"], 16)
            sp.dma_start(strict[:, :], g.d_strict).then_inc(s["consts"], 16)
            sp.dma_start(levels[:, :, :], g.d_levels).then_inc(s["consts"], 16)
            sp.dma_start(ab[:, :, :], g.a_dt).then_inc(s["consts"], 16)

        @block.tensor
        def _(pe):
            class front:
                @staticmethod
                def first(t):
                    if t >= 1:
                        pe.wait_ge(s["attnT_ready"], t)
                        pe.wait_ge(s["X0_ready"], t)
                        pe.wait_ge(s["A_ready"], t)
                    for h in range(H4):
                        last = nc.tensor.matmul(bank(0)[:, h, :], gg[:, t, h:h + 1].to_broadcast([P, P]), upper[:, :],
                                                start=True, stop=True)
                    last.then_inc(s["gcb_ready"], 1)
                    for h in range(H4):
                        last = nc.tensor.transpose(bank(1)[:, h, :], g.qkT[:, 4 + h, t * P:(t + 1) * P], g.ident[:, :])
                    last.then_inc(s["kt_ready"], 1)
                    for h in range(H4):
                        last = nc.tensor.transpose(bank(2)[:, h, :], g.vT[:, h, t * P:(t + 1) * P], g.ident[:, :])
                    last.then_inc(s["vt_ready"], 1)

                @staticmethod
                def khat_turn(t):
                    pe.wait_ge(s["khat_ready"], t + 1)
                    for h in range(H4):
                        last = nc.tensor.transpose(bank(1)[:, h, :], khat[:, h, :], g.ident[:, :])
                    last.then_inc(s["khatT_turned"], 1)

                @staticmethod
                def gram(t):
                    pe.wait_ge(s["khatT_ready"], t + 1)
                    pe.wait_ge(s["vb_ready"], t + 1)
                    for h in range(H4):
                        last = nc.tensor.matmul(bank(2)[:, h, :], khatT[:, h, :], khatT[:, h, :], start=True, stop=True)
                    last.then_inc(s["G_ready"], 1)

                @staticmethod
                def attn(t):
                    pe.wait_ge(s["diffs_done"], t + 1)
                    for h in range(H4):
                        last = nc.tensor.matmul(bank(0)[:, h, :], khatT[:, h, :], g.qkT[:, h, t * P:(t + 1) * P],
                                                start=True, stop=True)
                    last.then_inc(s["attn_ready"], 1)

                @staticmethod
                def x0(t):
                    pe.wait_ge(s["T0_ready"], t + 1)
                    for h in range(H4):
                        last = nc.tensor.transpose(bank(1)[:, h, :], T[:, t % 2, h, :], g.ident[:, :])
                    last.then_inc(s["X0_turned"], 1)

            class inv:
                @staticmethod
                def z(t, l):
                    m = (LEVELS - 1) * t + l - 1
                    pe.wait_ge(s["X0_ready"], t + 1)
                    if m >= 1:
                        pe.wait_ge(s["X_ready"], m)
                        pe.wait_ge(s["T_ready"], (LEVELS - 2) * t + l - 1)
                    if l == 1 and t >= 1:
                        pe.wait_ge(s["u_copied"], t)
                    pe.wait_ge(s["level_masked"], LEVELS * t + l + 1)
                    for h in range(H4):
                        last = nc.tensor.matmul(bank(3)[:, h, :], Al[:, t % 2, l, h, :], X[:, t % 2, h, :],
                                                start=True, stop=True)
                    last.then_inc(s["Z_ready"], 1)

                @staticmethod
                def update(t, l):
                    m = (LEVELS - 1) * t + l - 1
                    pe.wait_ge(s["Z_copied"], m + 1)
                    if l == 1 and t >= 1:
                        pe.wait_ge(s["w_copied"], t)
                    for h in range(H4):
                        last = nc.tensor.matmul(bank(4)[:, h, :], T[:, t % 2, h, :], Z[:, h, :], start=True, stop=True)
                    last.then_inc(s["dX_ready"], 1)
                    if l < LEVELS - 1:
                        for h in range(H4):
                            last = nc.tensor.matmul(bank(3)[:, h, :], Z[:, h, :], T[:, t % 2, h, :], start=True, stop=True)
                        last.then_inc(s["dT_ready"], 1)

                @staticmethod
                def apply(t):
                    pe.wait_ge(s["X_ready"], (LEVELS - 1) * (t + 1))
                    pe.wait_ge(s["vb_ready"], t + 1)
                    pe.wait_ge(s["kbe_ready"], t + 1)
                    for h in range(H4):
                        last = nc.tensor.matmul(bank(3)[:, h, :], X[:, t % 2, h, :], vb[:, t % 2, h, :], start=True, stop=True)
                    last.then_inc(s["u_ready"], 1)
                    for h in range(H4):
                        last = nc.tensor.matmul(bank(4)[:, h, :], kbe[:, t % 2, h, :], X[:, t % 2, h, :], start=True, stop=True)
                    last.then_inc(s["w_ready"], 1)

            class rec:
                @staticmethod
                def read(t, c):
                    n = 2 * t + c
                    r = slice(c * CHUNK, (c + 1) * CHUNK)
                    pe.wait_ge(s["w_copied"], t + 1)
                    if n >= 1:
                        pe.wait_ge(s["S_ready"], n)
                    if c == 0 and t >= 1:
                        pe.wait_ge(s["oq_ready"], t)
                    for h in range(H4):
                        last = nc.tensor.matmul(bank(6)[r, h, :], wT[:, t % 2, h, r], S[:, h, :], start=True, stop=True)
                    last.then_inc(s["wS_ready"], 1)
                    for h in range(H4):
                        last = nc.tensor.matmul(bank(7)[r, h, :], g.qkT[:, h, t * P + c * CHUNK:t * P + (c + 1) * CHUNK],
                                                S[:, h, :], start=True, stop=True)

                @staticmethod
                def write(t, c):
                    n = 2 * t + c
                    r = slice(c * CHUNK, (c + 1) * CHUNK)
                    pe.wait_ge(s["vnew_ready"], n + 1)
                    if c == 0 and t >= 1:
                        pe.wait_ge(s["o_ready"], t)
                    for h in range(H4):
                        last = nc.tensor.matmul(bank(6)[:, h, :], ktail[r, t % 3, h, :], vnew[r, h, :], start=True, stop=True)
                    last.then_inc(s["dS_ready"], 1)
                    for h in range(H4):
                        last = nc.tensor.matmul(bank(5)[r, h, :], attnT[r, t % 3, h, r], vnew[r, h, :], start=True, stop=True)
                    last.then_inc(s["av_ready"], 1)

            pe.wait_ge(s["consts"], 64)
            pe.wait_ge(s["g_ready"], 1)
            nc.tensor.matmul(ps[:, 0, 0:NT * H4], upper[:, :], gg[:, :, :].rearrange("p t h -> p (t h)"),
                             start=True, stop=True).then_inc(s["gc_ready"], 1)
            pe.wait_ge(s["gc_copied"], 1)
            pe.wait_ge(s["S_zeroed"], 1)
            for i in range(N + 2):
                order(i, front, inv, rec)

        @block.vector
        def _(dve):
            def chained(op, n=[0]):
                n[0] += 1
                op.then_inc(s["gate_dve"], 1)
                dve.wait_ge(s["gate_dve"], n[0])

            class front:
                @staticmethod
                def first(t):
                    dve.wait_ge(s["gcb_ready"], t + 1)
                    if t >= 1:
                        dve.wait_ge(s["decays_done"], t)
                    for h in range(H4):
                        nc.vector.tensor_scalar(dd[:, 0, h, :], bank(0)[:, h, :], gc[:, t, h:h + 1], 0.0,
                                                ALU.subtract, ALU.max)
                        nc.vector.tensor_scalar(dd[:, 1, h, :], bank(0)[:, h, :], gc[:, t, h:h + 1], 0.0,
                                                ALU.subtract, ALU.min)
                    for c in range(2):
                        r = slice(c * CHUNK, (c + 1) * CHUNK)
                        nc.vector.tensor_tensor(tl[r, 0:H4], bank(0)[r, :, (c + 1) * CHUNK - 1], gc[r, t, :], ALU.subtract)
                    ends = bank(0).rearrange("p h (c j) -> p h c j", c=2)[:, :, :, CHUNK - 1]
                    nc.vector.tensor_copy(tl[:, 4:12].rearrange("p (h c) -> p h c", c=2), ends).then_inc(s["diffs_done"], 1)
                    dve.wait_ge(s["kt_ready"], t + 1)
                    if t >= 1:
                        dve.wait_ge(s["khatT_turned"], t)
                        dve.wait_ge(s["kbe_ready"], t)
                        dve.wait_ge(s["ktail_ready"], t)
                    rk = g.l2[:, 32:64].rearrange("p (h t) -> p t h", t=NT)[:, t, :]
                    nc.vector.tensor_tensor(khat[:, :, :], bank(1), rk.unsqueeze(2).to_broadcast([P, H4, P]),
                                            ALU.mult).then_inc(s["khat_ready"], 1)
                    dve.wait_ge(s["vt_ready"], t + 1)
                    if t >= 2:
                        dve.wait_ge(s["u_ready"], t - 1)
                    nc.vector.tensor_tensor(vb[:, t % 2, :, :], bank(2), beta[:, t, :].unsqueeze(2).to_broadcast([P, H4, P]),
                                            ALU.mult).then_inc(s["vb_ready"], 1)

                @staticmethod
                def khat_turn(t):
                    pass

                @staticmethod
                def gram(t):
                    dve.wait_ge(s["G_ready"], t + 1)
                    dve.wait_ge(s["dec_masked"], t + 1)
                    if t >= 1:
                        dve.wait_ge(s["level_masked"], LEVELS * t)
                    nc.vector.tensor_tensor(A[:, :, :], bank(2), dec[:, 0, :, :], ALU.mult).then_inc(s["A_ready"], 1)

                @staticmethod
                def attn(t):
                    dve.wait_ge(s["attn_ready"], t + 1)
                    dve.wait_ge(s["decT_masked"], t + 1)
                    if t >= 3:
                        dve.wait_ge(s["av_ready"], 2 * (t - 2))
                    nc.vector.tensor_tensor(attnT[:, t % 3, :, :], bank(0), dec[:, 1, :, :], ALU.mult).then_inc(s["attnT_ready"], 1)
                    dve.wait_ge(s["level_masked"], LEVELS * t + 1)
                    nc.vector.tensor_tensor(T[:, t % 2, :, :], g.ident[:, :].unsqueeze(1).to_broadcast([P, H4, P]),
                                            Al[:, t % 2, 0, :, :], ALU.subtract).then_inc(s["T0_ready"], 1)

                @staticmethod
                def x0(t):
                    pass

            class inv:
                @staticmethod
                def z(t, l):
                    pass

                @staticmethod
                def update(t, l):
                    m = (LEVELS - 1) * t + l - 1
                    dve.wait_ge(s["dX_ready"], m + 1)
                    nc.vector.tensor_tensor(X[:, t % 2, :, :], X[:, t % 2, :, :], bank(4), ALU.subtract).then_inc(s["X_ready"], 1)
                    if l < LEVELS - 1:
                        dve.wait_ge(s["dT_ready"], (LEVELS - 2) * t + l)
                        nc.vector.tensor_tensor(T[:, t % 2, :, :], T[:, t % 2, :, :], bank(3), ALU.subtract).then_inc(s["T_ready"], 1)

                @staticmethod
                def apply(t):
                    pass

            class rec:
                @staticmethod
                def read(t, c):
                    n = 2 * t + c
                    r = slice(c * CHUNK, (c + 1) * CHUNK)
                    dve.wait_ge(s["wS_ready"], n + 1)
                    dve.wait_ge(s["u_copied"], t + 1)
                    if n >= 2:
                        dve.wait_ge(s["av_ready"], n - 1)
                    nc.vector.tensor_tensor(vnew[r, :, :], u[r, t % 2, :, :], bank(6)[r, :, :], ALU.subtract).then_inc(s["vnew_ready"], 1)

                @staticmethod
                def write(t, c):
                    n = 2 * t + c
                    dve.wait_ge(s["dS_ready"], n + 1)
                    dve.wait_ge(s["Sg_ready"], n + 1)
                    nc.vector.tensor_tensor(S[:, :, :], Sg[:, :, :], bank(6), ALU.add).then_inc(s["S_ready"], 1)
                    if c == 1:
                        dve.wait_ge(s["av_ready"], n + 1)
                        if t >= 1:
                            dve.wait_ge(s["o_ready"], t)
                        nc.vector.tensor_tensor(oq[:, :, :], bank(7), egc[:, t, :].unsqueeze(2).to_broadcast([P, H4, P]),
                                                ALU.mult).then_inc(s["oq_ready"], 1)
                        dve.wait_ge(s["oq_ready"], t + 1)
                        o = g.vT[:, :, t * P:(t + 1) * P]
                        nc.vector.tensor_tensor(o, oq[:, :, :], bank(5), ALU.add).then_inc(s["o_ready"], 1)
                        if t >= 1:
                            dve.wait_ge(s["osq_ready"], t)
                            nc.vector.tensor_reduce(g.o_ss[:, t - 1, :], osq[:, :, :], AX.X, ALU.add).then_inc(s["o_summed"], 1)

            dve.wait_ge(s["consts"], 64)
            nc.vector.memset(S[:, :, :], 0.0).then_inc(s["S_zeroed"], 1)
            a_in = g.ba[:, :, H4:2 * H4]
            dve.wait_ge(s["gate_act"], 2)
            chained(nc.vector.tensor_scalar(sc[:, 1], sc[:, 0], 1.0, None, ALU.add))
            chained(nc.vector.reciprocal(beta[:, :, :], sc[:, 1]))
            chained(nc.vector.tensor_tensor(sc[:, 2], a_in, ab[:, 1, :].unsqueeze(1).to_broadcast([P, NT, H4]), ALU.add))
            chained(nc.vector.tensor_scalar(sc[:, 3], sc[:, 2], -1.0, None, ALU.mult))
            chained(nc.vector.tensor_tensor(sc[:, 3], sc[:, 2], sc[:, 3], ALU.min))
            nc.vector.tensor_scalar(sc[:, 2], sc[:, 2], 0.0, None, ALU.max).then_inc(s["gates_ready"], 1)
            dve.wait_ge(s["gate_act"], 3)
            nc.vector.tensor_scalar(sc[:, 4], sc[:, 4], 1.0, None, ALU.add).then_inc(s["gates_ready"], 1)
            dve.wait_ge(s["gate_act"], 4)
            chained(nc.vector.tensor_tensor(sc[:, 2], sc[:, 2], sc[:, 5], ALU.add))
            chained(nc.vector.tensor_tensor(sc[:, 2], sc[:, 2], sc[:, 6, 0, :].unsqueeze(1).to_broadcast([P, NT, H4]), ALU.mult))
            nc.vector.tensor_scalar(gg[:, :, :], sc[:, 2], -1.0, None, ALU.mult).then_inc(s["g_ready"], 1)
            dve.wait_ge(s["gc_ready"], 1)
            nc.vector.tensor_copy(gc[:, :, :], ps[:, 0, 0:NT * H4].rearrange("p (t h) -> p t h", h=H4)).then_inc(s["gc_copied"], 1)
            dve.wait_ge(s["gc_copied"], 1)
            dve.wait_ge(s["gate_act"], 5)
            nc.vector.tensor_tensor(be[:, :, :], beta[:, :, :], egc[:, :, :], ALU.mult).then_inc(s["be_ready"], 1)
            dve.wait_ge(s["be_ready"], 1)
            for i in range(N + 2):
                order(i, front, inv, rec)
            dve.wait_ge(s["osq_ready"], N)
            nc.vector.tensor_reduce(g.o_ss[:, N - 1, :], osq[:, :, :], AX.X, ALU.add).then_inc(s["o_summed"], 1)
            dve.wait_ge(s["o_summed"], N)

        @block.scalar
        def _(act):
            class front:
                @staticmethod
                def first(t):
                    act.wait_ge(s["diffs_done"], t + 1)
                    if t >= 1:
                        act.wait_ge(s["A_ready"], t)
                        act.wait_ge(s["attnT_ready"], t)
                        act.wait_ge(s["dec_masked"], t)
                        act.wait_ge(s["decT_masked"], t)
                    if t >= 3:
                        act.wait_ge(s["Sg_ready"], 2 * (t - 2))
                    nc.scalar.activation(dec[:, 0, :, :], dd[:, 0, :, :], ACT.Exp, scale=-1.0)
                    nc.scalar.activation(dec[:, 1, :, :], dd[:, 1, :, :], ACT.Exp)
                    nc.scalar.activation(etl[:, t % 3, :], tl[:, :], ACT.Exp).then_inc(s["decays_done"], 1)

                @staticmethod
                def khat_turn(t):
                    act.wait_ge(s["khatT_turned"], t + 1)
                    if t >= 1:
                        act.wait_ge(s["attn_ready"], t)
                    nc.scalar.copy(khatT[:, :, :], bank(1)).then_inc(s["khatT_ready"], 1)

                @staticmethod
                def gram(t):
                    pass

                @staticmethod
                def attn(t):
                    pass

                @staticmethod
                def x0(t):
                    act.wait_ge(s["X0_turned"], t + 1)
                    if t >= 2:
                        act.wait_ge(s["w_ready"], t - 1)
                    nc.scalar.copy(X[:, t % 2, :, :], bank(1)).then_inc(s["X0_ready"], 1)

            class inv:
                @staticmethod
                def z(t, l):
                    m = (LEVELS - 1) * t + l - 1
                    act.wait_ge(s["Z_ready"], m + 1)
                    if m >= 1:
                        act.wait_ge(s["dX_ready"], m)
                        act.wait_ge(s["dT_ready"], (LEVELS - 2) * t + l - 1)
                    nc.scalar.copy(Z[:, :, :], bank(3)).then_inc(s["Z_copied"], 1)

                @staticmethod
                def update(t, l):
                    pass

                @staticmethod
                def apply(t):
                    if t >= 2:
                        act.wait_ge(s["vnew_ready"], 2 * (t - 1))
                    act.wait_ge(s["u_ready"], t + 1)
                    nc.scalar.copy(u[:, t % 2, :, :], bank(3)).then_inc(s["u_copied"], 1)
                    if t >= 2:
                        act.wait_ge(s["wS_ready"], 2 * (t - 1))
                    act.wait_ge(s["w_ready"], t + 1)
                    nc.scalar.copy(wT[:, t % 2, :, :], bank(4)).then_inc(s["w_copied"], 1)

            class rec:
                @staticmethod
                def read(t, c):
                    pass

                @staticmethod
                def write(t, c):
                    pass

            act.wait_ge(s["consts"], 64)
            nc.scalar.activation(sc[:, 0], g.ba[:, :, 0:H4], ACT.Exp, scale=-1.0).then_inc(s["gate_act"], 1)
            nc.scalar.activation(sc[:, 6, 0, :], ab[:, 0, :], ACT.Exp).then_inc(s["gate_act"], 1)
            act.wait_ge(s["gates_ready"], 1)
            nc.scalar.activation(sc[:, 4], sc[:, 3], ACT.Exp).then_inc(s["gate_act"], 1)
            act.wait_ge(s["gates_ready"], 2)
            nc.scalar.activation(sc[:, 5], sc[:, 4], ACT.Ln).then_inc(s["gate_act"], 1)
            act.wait_ge(s["gc_copied"], 1)
            nc.scalar.activation(egc[:, :, :], gc[:, :, :], ACT.Exp).then_inc(s["gate_act"], 1)
            for i in range(N + 2):
                order(i, front, inv, rec)

        @block.gpsimd
        def _(pool):
            def over_heads(m):
                return m.unsqueeze(1).to_broadcast([P, H4, P])

            def per_row(col):
                return col.unsqueeze(2).to_broadcast([P, H4, P])

            class front:
                @staticmethod
                def first(t):
                    pool.wait_ge(s["decays_done"], t + 1)
                    nc.gpsimd.tensor_tensor(dec[:, 0, :, :], dec[:, 0, :, :], over_heads(strict[:, :]), ALU.mult).then_inc(s["strict_done"], 1)
                    pool.wait_ge(s["strict_done"], t + 1)
                    nc.gpsimd.tensor_tensor(dec[:, 0, :, :], dec[:, 0, :, :], per_row(beta[:, t, :]), ALU.mult).then_inc(s["dec_masked"], 1)
                    nc.gpsimd.tensor_tensor(dec[:, 1, :, :], dec[:, 1, :, :], over_heads(upper[:, :]), ALU.mult).then_inc(s["decT_masked"], 1)

                @staticmethod
                def khat_turn(t):
                    pool.wait_ge(s["khat_ready"], t + 1)
                    if t >= 2:
                        pool.wait_ge(s["w_ready"], t - 1)
                    nc.gpsimd.tensor_tensor(kbe[:, t % 2, :, :], khat[:, :, :], per_row(be[:, t, :]), ALU.mult).then_inc(s["kbe_ready"], 1)
                    if t >= 3:
                        pool.wait_ge(s["dS_ready"], 2 * (t - 2))
                    nc.gpsimd.tensor_tensor(ktail[:, t % 3, :, :], khat[:, :, :], per_row(etl[:, t % 3, 0:H4]), ALU.mult).then_inc(s["ktail_ready"], 1)

                @staticmethod
                def gram(t):
                    pool.wait_ge(s["A_ready"], t + 1)
                    for l in range(LEVELS):
                        if l == 0 and t >= 2:
                            pool.wait_ge(s["Z_ready"], (LEVELS - 1) * (t - 1))
                            pool.wait_ge(s["T0_ready"], t - 1)
                        nc.gpsimd.tensor_tensor(Al[:, t % 2, l, :, :], A[:, :, :], over_heads(levels[:, l, :]), ALU.mult).then_inc(s["level_masked"], 1)

                @staticmethod
                def attn(t):
                    pass

                @staticmethod
                def x0(t):
                    pass

            class inv:
                @staticmethod
                def z(t, l):
                    pass

                @staticmethod
                def update(t, l):
                    pass

                @staticmethod
                def apply(t):
                    pass

            class rec:
                @staticmethod
                def read(t, c):
                    n = 2 * t + c
                    if n >= 1:
                        pool.wait_ge(s["S_ready"], n)
                    decay = etl[:, t % 3, 4:12].rearrange("p (h c) -> p h c", c=2)[:, :, c]
                    nc.gpsimd.tensor_tensor(Sg[:, :, :], S[:, :, :], per_row(decay), ALU.mult).then_inc(s["Sg_ready"], 1)

                @staticmethod
                def write(t, c):
                    if c == 0 and t >= 1:
                        square(t - 1)

            def square(t):
                pool.wait_ge(s["o_ready"], t + 1)
                if t >= 1:
                    pool.wait_ge(s["o_summed"], t)
                o = g.vT[:, :, t * P:(t + 1) * P]
                nc.gpsimd.tensor_tensor(osq[:, :, :], o, o, ALU.mult).then_inc(s["osq_ready"], 1)

            pool.wait_ge(s["be_ready"], 1)
            pool.wait_ge(s["S_zeroed"], 1)
            for i in range(N + 2):
                order(i, front, inv, rec)
            square(N - 1)


def dilated_tile(p, i):
    if p == 0:
        return i * P, 1, i > 0
    if p == 1:
        return i // 2 + 4 * P * (i % 2), 4, i % 2 == 1
    return i, 8, False


def dilated_rows(ap, p):
    if p == 0:
        return ap.rearrange("(i j) c -> j i c", j=P)
    if p == 1:
        return ap.rearrange("(b j r) c -> j r b c", j=P, r=4)
    return ap.rearrange("(j i) c -> j i c", j=P)


def stage_dilated(nc, g, w_hi, w_lo):
    with ExitStack() as ctx:
        k = Kit(nc, ctx)
        ws = WeightSplit(nc, k, "c_w_", g.w_out2, w_hi, w_lo)
        ps = k.psum("c_ps")
        v = k.sb("c_v", [P, 2, NT, 512])
        table = k.sb("c_table", [P, 2, ATT_HEADS, 256])
        prob = k.sb("c_prob", [P, 3, 256])
        prob_t = k.sb("c_prob_t", [P, 3, 256])
        out = k.sb("c_out", [P, NT, 512])
        ml = k.sb("c_ml", [P, 3, NT, 2, ATT_HEADS])
        loaded = k.sems("c_loaded", 3)
        scores_ready = k.sem("c_scores_ready")
        max_ready = k.sem("c_max_ready")
        prob_ready = k.sem("c_prob_ready")
        turned = k.sem("c_turned")
        pt_by_dve = k.sem("c_pt_by_dve")
        pt_by_act = k.sem("c_pt_by_act")
        values_done = k.sem("c_values_done")
        group_emptied = k.sem("c_group_emptied")
        out_sent = k.sems("c_out_sent", 3)
        ml_sent = k.sem("c_ml_sent")
        units = [(p, h, i) for p in range(3) for h in range(ATT_HEADS) for i in range(NT)]
        n_units = len(units)
        PER_P = ATT_HEADS * NT

        def pt_ready(eng, n):
            if n > 0:
                eng.wait_ge(pt_by_dve, (n + 1) // 2)
            if n > 1:
                eng.wait_ge(pt_by_act, n // 2)

        block = ctx.enter_context(nc.Block())

        @block.sync
        def _(sp):
            def load(p):
                if p >= 2:
                    sp.wait_ge(values_done, PER_P * (p - 1))
                    sp.wait_ge(max_ready, PER_P * (p - 1))
                if p == 1:
                    src = dilated_rows(g.v_att, p)
                    for r in range(4):
                        sp.dma_start(v[:, p % 2, 2 * r:2 * r + 2, :], src[:, r, :, :]).then_inc(loaded[p], 16)
                else:
                    sp.dma_start(v[:, p % 2, :, :], dilated_rows(g.v_att, p)).then_inc(loaded[p], 16)
                W = DilatedTable.LINE * 3 * ATT_HEADS
                band = bass.AP(tensor=g.lines.tensor, offset=p * ATT_HEADS * DilatedTable.LINE + P - 1,
                               ap=[[W - 1, P], [DilatedTable.LINE, ATT_HEADS], [1, 256]])
                sp.dma_start(table[:, p % 2, :, :], band).then_inc(loaded[p], 16)

            def send(p):
                sp.wait_ge(group_emptied, ATT_HEADS * (p + 1))
                if p == 1:
                    dst = dilated_rows(g.o_att[p], p)
                    for r in range(4):
                        sp.dma_start(dst[:, r, :, :], out[:, 2 * r:2 * r + 2, :]).then_inc(out_sent[p], 16)
                else:
                    sp.dma_start(dilated_rows(g.o_att[p], p), out[:, :, :]).then_inc(out_sent[p], 16)
                sp.wait_ge(prob_ready, PER_P * (p + 1))
                dst = dilated_rows(g.ml[p], p)
                if p == 1:
                    for r in range(4):
                        sp.dma_start(dst[:, r, :, :], ml[:, p, 2 * r:2 * r + 2, :, :].rearrange("p i a h -> p i (a h)"))\
                            .then_inc(ml_sent, 16)
                else:
                    sp.dma_start(dst, ml[:, p, :, :, :].rearrange("p i a h -> p i (a h)")).then_inc(ml_sent, 16)

            load(0)
            load(1)
            for kt in range(KT):
                ws.load(sp, kt)
            send(0)
            load(2)
            send(1)
            send(2)
            for p, n in enumerate((1, 4, 1)):
                sp.wait_ge(out_sent[p], 16 * n)
            sp.wait_ge(ml_sent, 16 * 6)

        @block.gpsimd
        def _(pool):
            for kt in range(KT):
                ws.split(pool, kt)

        @block.tensor
        def _(pe):
            def scores(u):
                p, h, i = units[u]
                first, stride, before = dilated_tile(p, i)
                if u >= 3:
                    pe.wait_ge(max_ready, u - 2)
                r = slice(HD * (h % 2), HD * (h % 2) + HD)
                q = g.att_qT[r, h // 2, first:first + stride * (P - 1) + 1:stride]
                c0 = 0 if before else P
                k_first = first - stride * P if before else first
                n = 256 - c0
                keys = g.att_kT[r, h // 2, k_first:k_first + stride * (n - 1) + 1:stride]
                nc.tensor.matmul(ps[:, u % 3, c0:256], q, keys, start=True, stop=True).then_inc(scores_ready, 1)

            def turn_probs(u):
                p, h, i = units[u]
                before = dilated_tile(p, i)[2]
                pe.wait_ge(prob_ready, u + 1)
                pt_ready(pe, u - 2)
                for j in range(0 if before else 1, 2):
                    last = nc.tensor.transpose(ps[:, 3 + u % 3, j * P:(j + 1) * P],
                                               prob[:, u % 3, j * P:(j + 1) * P], g.ident[:, :])
                last.then_inc(turned, 1)

            def values(u):
                p, h, i = units[u]
                before = dilated_tile(p, i)[2]
                grp = u // NT
                pt_ready(pe, u + 1)
                if u % PER_P == 0:
                    pe.wait_ge(loaded[p], 80 if p == 1 else 32)
                if i == 0 and grp >= 2:
                    pe.wait_ge(group_emptied, grp - 1)
                for j in range(0 if before else 1, 2):
                    last = nc.tensor.matmul(ps[:, 6 + grp % 2, i * HD:(i + 1) * HD], prob_t[:, u % 3, j * P:(j + 1) * P],
                                            v[:, p % 2, i - 1 + j, h * HD:(h + 1) * HD],
                                            start=(j == (0 if before else 1)), stop=(j == 1))
                last.then_inc(values_done, 1)

            for u in range(n_units + 4):
                if u < n_units:
                    scores(u)
                if 2 <= u < n_units + 2:
                    turn_probs(u - 2)
                if u >= 4:
                    values(u - 4)

        @block.vector
        def _(dve):
            def bias_and_max(u):
                p, h, i = units[u]
                c0 = 0 if dilated_tile(p, i)[2] else P
                if u % PER_P == 0:
                    dve.wait_ge(loaded[p], 80 if p == 1 else 32)
                dve.wait_ge(scores_ready, u + 1)
                if u >= 3:
                    dve.wait_ge(turned, u - 2)
                nc.vector.tensor_tensor_reduce(prob[:, u % 3, c0:256], ps[:, u % 3, c0:256], table[:, p % 2, h, c0:256],
                                               -1.0, -NEG, ALU.add, ALU.min,
                                               ml[:, p, i, 0, h:h + 1]).then_inc(max_ready, 1)

            def empty(u):
                c0 = 0 if dilated_tile(units[u][0], units[u][2])[2] else P
                dve.wait_ge(turned, u + 1)
                if u >= 3:
                    dve.wait_ge(values_done, u - 2)
                nc.vector.tensor_copy(prob_t[:, u % 3, c0:256], ps[:, 3 + u % 3, c0:256]).then_inc(pt_by_dve, 1)

            def empty_group(grp):
                p, h, _ = units[grp * NT]
                dve.wait_ge(values_done, NT * (grp + 1))
                if p >= 1 and h == 0:
                    dve.wait_ge(out_sent[p - 1], (16, 64)[p - 1])
                nc.vector.tensor_copy(out[:, :, h * HD:(h + 1) * HD],
                                      ps[:, 6 + grp % 2, :].rearrange("p (i d) -> p i d", d=HD)).then_inc(group_emptied, 1)

            for u in range(n_units + 5):
                if u < n_units:
                    bias_and_max(u)
                if 2 <= u < n_units + 2 and u % 2 == 0:
                    empty(u - 2)
                if u >= 12 and (u - 12) % NT == 0:
                    empty_group((u - 12) // NT)

        @block.scalar
        def _(act):
            def exponentials(u):
                p, h, i = units[u]
                c0 = 0 if dilated_tile(p, i)[2] else P
                act.wait_ge(max_ready, u + 1)
                s = prob[:, u % 3, c0:256]
                nc.scalar.activation(s, s, ACT.Exp, bias=ml[:, p, i, 0, h:h + 1], scale=-1.0,
                                     accum_out=ml[:, p, i, 1, h:h + 1]).then_inc(prob_ready, 1)

            def empty(u):
                c0 = 0 if dilated_tile(units[u][0], units[u][2])[2] else P
                act.wait_ge(turned, u + 1)
                if u >= 3:
                    act.wait_ge(values_done, u - 2)
                nc.scalar.copy(prob_t[:, u % 3, c0:256], ps[:, 3 + u % 3, c0:256]).then_inc(pt_by_act, 1)

            for u in range(n_units + 2):
                if u < n_units:
                    exponentials(u)
                if 2 <= u and u % 2 == 1:
                    empty(u - 2)


def stage_out_2(nc, g, w_hi, w_lo):
    with ExitStack() as ctx:
        k = Kit(nc, ctx)
        ps = k.psum("o2_ps")
        gate = k.sb("o2_gate", [P, 2, 512])
        z = k.sb("o2_z", [P, 2, 512])
        o = k.sb("o2_o", [P, 2, 3, 512])
        x = k.sb("o2_x", [P, 2, D])
        y = k.sb("o2_y", [P, 2, D])
        mixed = k.sb("o2_mixed", [P, 2, D])
        norm_w = k.sb("o2_norm_w", [P, DK])
        ml = k.sb("o2_ml", [P, 3, NT, 2, ATT_HEADS])
        wt = k.sb("o2_wt", [P, 3, NT, ATT_HEADS])
        small = k.sb("o2_small", [P, 3, NT, ATT_HEADS])
        fac = k.sb("o2_fac", [P, 4, NT, DN_HEADS])
        ml_loaded = k.sem("o2_ml_loaded")
        norm_loaded = k.sem("o2_norm_loaded")
        o_loaded = k.sems("o2_o_loaded", 2)
        gate_loaded = k.sems("o2_gate_loaded", 2)
        z_loaded = k.sems("o2_z_loaded", 2)
        x_loaded = k.sems("o2_x_loaded", 2)
        step_done = k.sem("o2_step_done")
        exps_ready = k.sem("o2_exps_ready")
        diffs_ready = k.sem("o2_diffs_ready")
        var_ready = k.sem("o2_var_ready")
        std_ready = k.sem("o2_std_ready")
        fac_ready = k.sem("o2_fac_ready")
        dn_step = k.sem("o2_dn_step")
        dn_mixed = k.sem("o2_dn_mixed")
        att_mixed = k.sem("o2_mixed_ready")
        y_stored = g.out_stored
        op = OutProjection(nc, k, "o2_", g, ps, w_hi, w_lo, mixed, (dn_mixed, att_mixed))
        block = ctx.enter_context(nc.Block())

        @block.sync
        def _(sp):
            def load(t):
                if t >= 2:
                    sp.wait_ge(att_mixed, t - 1)
                for p in range(3):
                    sp.dma_start(o[:, t % 2, p, :], rows(g.o_att[p], t)).then_inc(o_loaded[t % 2], 16)
                sp.dma_start(gate[:, t % 2, :], rows(g.gate2, t)).then_inc(gate_loaded[t % 2], 16)
                if t >= 2:
                    sp.wait_ge(dn_mixed, t - 1)
                sp.dma_start(z[:, t % 2, :], rows(g.z, t)).then_inc(z_loaded[t % 2], 16)
                if t >= 2:
                    sp.wait_ge(op.job_emptied, 2 * (t - 1))
                sp.dma_start(x[:, t % 2, :], rows(g.x1, t)).then_inc(x_loaded[t % 2], 16)

            def store(t):
                sp.wait_ge(op.job_emptied, 2 * t + 2)
                sp.dma_start(rows(g.out, t), y[:, t % 2, :]).then_inc(y_stored[t % 2], 16)

            for p in range(3):
                sp.dma_start(ml[:, p, :, :, :].rearrange("p t a h -> p t (a h)"),
                             g.ml[p].rearrange("(t j) c -> j t c", j=P)).then_inc(ml_loaded, 16)
            sp.dma_start(norm_w[:, :], g.dn_norm).then_inc(norm_loaded, 16)
            load(0)
            load(1)
            for t in range(2, NT):
                load(t)
                store(t - 2)
            store(NT - 2)
            store(NT - 1)
            for i in range(2):
                sp.wait_ge(y_stored[i], 16 * (NT // 2))

        @block.gpsimd
        def _(pool):
            steps = 0

            def step(op_):
                nonlocal steps
                steps += 1
                op_.then_inc(dn_step, 1)
                pool.wait_ge(dn_step, steps)

            pool.wait_ge(fac_ready, 1)
            pool.wait_ge(norm_loaded, 16)
            for t in range(NT):
                m = mixed[:, t % 2, 0:512].rearrange("p (h c) -> p h c", h=DN_HEADS)
                src = g.vT[:, :, t * P:(t + 1) * P]
                if t >= 2:
                    pool.wait_ge(op.half_turned, 2 * (t - 1))
                step(nc.gpsimd.tensor_tensor(m, src, fac[:, 3, t, :].unsqueeze(2).to_broadcast([P, DN_HEADS, DK]), ALU.mult))
                step(nc.gpsimd.tensor_tensor(m, m, norm_w[:, :].unsqueeze(1).to_broadcast([P, DN_HEADS, DK]), ALU.mult))
                pool.wait_ge(z_loaded[t % 2], 16 * (t // 2 + 1))
                nc.gpsimd.tensor_tensor(mixed[:, t % 2, 0:512], mixed[:, t % 2, 0:512], z[:, t % 2, :],
                                        ALU.mult).then_inc(dn_mixed, 1)

        @block.tensor
        def _(pe):
            op.tensor(pe)

        @block.scalar
        def _(act):
            act.wait_ge(diffs_ready, 1)
            nc.scalar.activation(wt[:, :, :, :], wt[:, :, :, :], ACT.Exp).then_inc(exps_ready, 1)
            act.wait_ge(var_ready, 1)
            nc.scalar.activation(fac[:, 1], fac[:, 0], ACT.Sqrt).then_inc(std_ready, 1)
            for t in range(NT):
                op.split_hi(act, t)

        @block.vector
        def _(dve):
            steps = 0

            def step(op_):
                nonlocal steps
                steps += 1
                op_.then_inc(step_done, 1)
                dve.wait_ge(step_done, steps)

            dve.wait_ge(ml_loaded, 48)
            neg = [ml[:, p, :, 0, :] for p in range(3)]
            total = [ml[:, p, :, 1, :] for p in range(3)]
            step(nc.vector.tensor_tensor(small[:, 0], neg[0], neg[1], ALU.min))
            step(nc.vector.tensor_tensor(small[:, 0], small[:, 0], neg[2], ALU.min))
            for p in range(3):
                last = nc.vector.tensor_tensor(wt[:, p], small[:, 0], neg[p], ALU.subtract)
            last.then_inc(diffs_ready, 1)
            r = g.l2[:, 0:32].rearrange("p (h t) -> p t h", t=NT)
            step(nc.vector.tensor_tensor(fac[:, 2], r, r, ALU.mult))
            step(nc.vector.tensor_tensor(fac[:, 2], fac[:, 2], g.o_ss[:, :, :], ALU.mult))
            nc.vector.tensor_scalar(fac[:, 0], fac[:, 2], 1.0 / DK, EPS, ALU.mult, ALU.add).then_inc(var_ready, 1)
            dve.wait_ge(exps_ready, 1)
            step(nc.vector.tensor_tensor(small[:, 0], wt[:, 0], total[0], ALU.mult))
            for p in (1, 2):
                step(nc.vector.tensor_tensor(small[:, 1], wt[:, p], total[p], ALU.mult))
                step(nc.vector.tensor_tensor(small[:, 0], small[:, 0], small[:, 1], ALU.add))
            step(nc.vector.reciprocal(small[:, 2], small[:, 0]))
            for p in range(3):
                step(nc.vector.tensor_tensor(wt[:, p], wt[:, p], small[:, 2], ALU.mult))
            dve.wait_ge(std_ready, 1)
            step(nc.vector.reciprocal(fac[:, 2], fac[:, 1]))
            nc.vector.tensor_tensor(fac[:, 3], fac[:, 2], r, ALU.mult).then_inc(fac_ready, 1)

            def mix(t):
                dve.wait_ge(o_loaded[t % 2], 48 * (t // 2 + 1))
                parts = [o[:, t % 2, p, :].rearrange("p (h d) -> p h d", d=HD) for p in range(3)]
                for p in range(3):
                    last = nc.vector.tensor_tensor(parts[p], parts[p], wt[:, p, t, :].unsqueeze(2).to_broadcast([P, ATT_HEADS, HD]),
                                                   ALU.mult)
                step(last)
                step(nc.vector.tensor_tensor(parts[0], parts[0], parts[1], ALU.add))
                step(nc.vector.tensor_tensor(parts[0], parts[0], parts[2], ALU.add))
                if t >= 2:
                    dve.wait_ge(op.half_turned, 2 * (t - 1))
                dve.wait_ge(gate_loaded[t % 2], 16 * (t // 2 + 1))
                nc.vector.tensor_tensor(mixed[:, t % 2, 512:D], o[:, t % 2, 0, :], gate[:, t % 2, :],
                                        ALU.mult).then_inc(att_mixed, 1)

            mix(0)
            op.split_lo(dve, 0)
            for t in range(NT):
                if t + 1 < NT:
                    mix(t + 1)
                    op.split_lo(dve, t + 1)
                dve.wait_ge(x_loaded[t % 2], 16 * (t // 2 + 1))
                if t >= 2:
                    dve.wait_ge(y_stored[t % 2], 16 * (t // 2))
                op.add_residual(dve, t, y[:, t % 2, :], x[:, t % 2, :])


def t5_bucket(dist):
    max_exact = 16
    d = np.maximum(dist, 1).astype(np.float64)
    large = max_exact + (np.log(d / max_exact) / np.log(2048 / max_exact) * 16).astype(np.int32)
    return np.where(dist < max_exact, dist, np.minimum(large, 31)).astype(np.int32)


def second_constants():
    onehot = np.zeros((33, 3, DilatedTable.LINE), np.float32)
    for p, r in enumerate(DILATION):
        for u in range(DilatedTable.LINE):
            back = 255 - u
            if p == 2:
                ok, step = back >= 0 and back % 2 == 0, back // 2
            else:
                ok, step = 0 <= back <= P, back
            if ok:
                onehot[int(t5_bucket(np.array(step * r))), p, u] = 1.0
            else:
                onehot[32, p, u] = NEG
    i, j = np.arange(P)[:, None], np.arange(P)[None]
    same = i // CHUNK == j // CHUNK
    levels = np.stack([(i // (2 * s) == j // (2 * s)) & (i % (2 * s) >= s) & (j % (2 * s) < s)
                       for s in (1 << l for l in range(LEVELS))], 1)
    f = np.float32
    return {"c_di_onehot": onehot, "c_upper": (same & (i <= j)).astype(f), "c_strict": (same & (i > j)).astype(f),
            "c_levels": levels.astype(f), "c_ones": np.ones((P, 1), f)}


def second_inputs(f, everywhere):
    rel = np.ones((33, ATT_HEADS), np.float32)
    rel[:32] = f["rel_bias_2"].T
    return {"gain2": everywhere(f["norm_w_2"][0]), "w_in2": f["w_in_2"][0], "w_out2": f["w_out_2"][0],
            "conv_w": f["conv_w_2"][0].T.reshape(12, P, 4).transpose(1, 0, 2),
            "a_dt": everywhere(np.stack([f["a_log_2"][0], f["dt_bias_2"][0]])).reshape(P, 2, DN_HEADS),
            "dn_norm": everywhere(f["dn_norm_w_2"][0]),
            "att_gain": everywhere(np.stack([f["q_norm_w_2"][0], f["k_norm_w_2"][0]])).reshape(P, 2, HD),
            "rel": rel}


def second_block(nc, g, whole):
    d = g.second
    g.w_in2, g.w_out2, g.gain2, g.conv_w, g.a_dt = d["w_in2"], d["w_out2"], d["gain2"], d["conv_w"], d["a_dt"]
    g.dn_norm, g.att_gain, g.rel = d["dn_norm"], d["att_gain"], d["rel"]
    g.d_upper, g.d_strict, g.d_levels = d["c_upper"], d["c_strict"], d["c_levels"]

    def scratch(name, shape):
        return nc.dram_tensor(name, list(shape), F32, kind=g.scratch_kind).ap()

    g.v_att, g.gate2, g.z = (scratch("s_" + n, (SEQ, 512)) for n in ("v_att", "gate2", "z"))
    g.lines = scratch("s_lines", (P, 3 * ATT_HEADS, DilatedTable.LINE))
    g.o_att = [scratch(f"s_o_att{p}", (SEQ, 512)) for p in range(3)]
    g.ml = [scratch(f"s_ml{p}", (SEQ, 16)) for p in range(3)]
    g.l2 = whole.sb("l2", [P, 64])
    g.ba = whole.sb("ba", [P, NT, 8])
    g.o_ss = whole.sb("o_ss", [P, NT, DN_HEADS])
    with ExitStack() as ctx2:
        mid = Kit(nc, ctx2)
        g.att_qT = mid.sb("att_qT", [P, 4, SEQ])
        g.att_kT = mid.sb("att_kT", [P, 4, SEQ])
        g.vT = mid.sb("vT", [P, 4, SEQ])
        with ExitStack() as ctx3:
            early = Kit(nc, ctx3)
            g.qkT = early.sb("qkT", [P, 8, SEQ])
            with ExitStack() as ctx4:
                i = Kit(nc, ctx4)
                hT_hi = i.sb("h2T_hi", [P, KT, SEQ], F32R)
                hT_lo = i.sb("h2T_lo", [P, KT, SEQ], F32R)
                stage_norm(nc, "n2_", g.x1, g.gain2, g.ident, hT_hi, hT_lo,
                           lambda k: DilatedTable(k, nc, g.lines, d["c_di_onehot"], g.rel,
                                                  (g.vT, g.att_qT, g.att_kT)))
                stage_project_2(nc, g, hT_hi, hT_lo)
            stage_delta(nc, g)
        w_hi = mid.sb("w_out2_hi", [P, KT, D], F32R)
        w_lo = mid.sb("w_out2_lo", [P, KT, D], F32R)
        stage_dilated(nc, g, w_hi, w_lo)
        stage_out_2(nc, g, w_hi, w_lo)


class Arrays:
    pass


def build(nc, g):
    def scratch(name, shape):
        return nc.dram_tensor(name, list(shape), F32, kind=g.scratch_kind).ap()

    g.gate1 = scratch("s_gate1", (SEQ, D))
    g.vb = scratch("s_vb", (SEQ, 512))
    g.out_b = scratch("s_out_b", (SEQ, 512))
    g.x1 = scratch("s_x1", (SEQ, D))
    with ExitStack() as top:
        whole = Kit(nc, top, clears=False)
        g.ident = whole.sb("ident", [P, P])
        g.ones = whole.sb("ones", [P, 1])
        g.out_stored = whole.sems("out_stored", 2)
        load_constants(nc, whole, g)
        with ExitStack() as ctx:
            first = Kit(nc, ctx)
            g.na_table = first.sb("na_table", [P, 4 * RIDX, GRID_W])
            g.qkv_a = first.sb("qkv_a", [P, NT, 768])
            g.qbT = first.sb("qbT", [P, 4, SEQ])
            g.kbT = first.sb("kbT", [P, 4, SEQ])
            g.kk = first.sb("kk", [P, A_KV, SEQ], F32R)
            with ExitStack() as inner:
                i = Kit(nc, inner)
                hT_hi = i.sb("hT_hi", [P, KT, SEQ], F32R)
                hT_lo = i.sb("hT_lo", [P, KT, SEQ], F32R)
                stage_norm(nc, "n1_", g.x, g.gain1, g.ident, hT_hi, hT_lo,
                           lambda k: BiasTable(k, nc, g.na_table, g.rpb_t, g.na_onehot, g.na_mask))
                stage_project_1(nc, g, hT_hi, hT_lo)
            stage_attention_a(nc, g)
            w_hi = first.sb("w_out_hi", [P, KT, D], F32R)
            w_lo = first.sb("w_out_lo", [P, KT, D], F32R)
            stage_attention_b(nc, g, w_hi, w_lo)
            stage_out_1(nc, g, w_hi, w_lo)
        second_block(nc, g, whole)


def load_constants(nc, k, g):
    loaded = k.sem("ident_loaded")
    with nc.Block() as block:
        @block.sync
        def _(sp):
            sp.dma_start(g.ident[:, :], g.ident_d).then_inc(loaded, 16)
            sp.dma_start(g.ones[:, :], g.second["c_ones"]).then_inc(loaded, 16)
            sp.wait_ge(loaded, 32)


def shape_constants():
    t = np.arange(SEQ)
    inv = (np.float32(10000.0) ** (-np.arange(16, dtype=np.float32) * np.float32(2.0 / 32))).astype(np.float32)
    ang_r = (t // GRID_W).astype(np.float32)[:, None] * inv[None]
    ang_c = (t % GRID_W).astype(np.float32)[:, None] * inv[None]
    ang = np.concatenate([ang_r, ang_r, ang_c, ang_c], -1)
    sign = np.tile(np.repeat(np.array([-1.0, 1.0], np.float32), 16), 2)
    rope = np.stack([np.cos(ang), np.sin(ang) * sign]).astype(np.float32)
    rope = rope.reshape(2, NT, P, HD).transpose(2, 0, 1, 3)
    onehot = np.zeros((32, 127), np.float32)
    for c in range(CIDX):
        onehot[c, 78 - c] = 1.0
    q = np.arange(GRID_W)[:, None]
    kc = np.arange(GRID_W)[None]
    start = np.clip(q - NA_KW // 2, 0, GRID_W - NA_KW)
    mask = np.where((kc >= start) & (kc < start + NA_KW), 0.0, NEG).astype(np.float32)
    c = {"c_ident": np.eye(P, dtype=np.float32), "c_rope": np.ascontiguousarray(rope),
         "c_na_onehot": onehot, "c_na_mask": np.concatenate([mask, mask])}
    c.update(second_constants())
    return c


def lay_out(inputs):
    f = {n: np.asarray(a) for n, a in inputs.items()}

    def everywhere(a):
        return np.ascontiguousarray(np.broadcast_to(a.reshape(1, -1), (P, a.size)))

    gains = np.stack([f["q_norm_a"][0], f["k_norm_a"][0]])
    swapped = gains.reshape(2, 2, 2, 16)[:, :, ::-1].reshape(2, HD)
    rpb = np.zeros((32, 2, 4, RIDX), np.float32)
    rpb[:CIDX] = f["na_rpb"][0].reshape(4, 2, RIDX, CIDX).transpose(3, 1, 0, 2)
    a = {"x": f["x"][0], "w_in": f["w_in"][0], "w_out": f["w_out"][0], "gain1": everywhere(f["norm_gain"][0]),
         "final_gain": everywhere(f["final_norm_gain"]),
         "gain_a": everywhere(np.stack([gains, swapped])).reshape(P, 2, 2, HD),
         "rpb_t": rpb.reshape(32, 2, 4 * RIDX)}
    a.update(second_inputs(f, everywhere))
    return {n: np.ascontiguousarray(v) for n, v in a.items()}


def kernel(**inputs):
    import concourse.bacc as bacc
    from concourse.bass_utils import run_bass_kernel_spmd

    nc = bacc.Bacc("TRN2", target_bir_lowering=False, num_devices=1)
    g = Arrays()
    g.scratch_kind = "Internal"
    arrays = declare(nc, g, inputs)
    g.out = nc.dram_tensor("out", [SEQ, D], F32, kind="ExternalOutput").ap()
    build(nc, g)
    r = run_bass_kernel_spmd(nc, [arrays], core_ids=[0])
    return r.results[0]["out"].reshape(1, SEQ, D)


def declare(nc, g, inputs):
    arrays = {}
    laid, consts = lay_out(inputs), shape_constants()

    def declared(name, a):
        arrays[name] = a
        return nc.dram_tensor(name, list(a.shape), F32, kind="ExternalInput").ap()

    d = {n: declared(n, a) for n, a in {**laid, **consts}.items()}
    g.x, g.w_in, g.w_out, g.gain1, g.final_gain = d["x"], d["w_in"], d["w_out"], d["gain1"], d["final_gain"]
    g.gain_a, g.rpb_t = d["gain_a"], d["rpb_t"]
    g.ident_d, g.rope, g.na_onehot, g.na_mask = d["c_ident"], d["c_rope"], d["c_na_onehot"], d["c_na_mask"]
    g.second = d
    return arrays
```

```python
from contextlib import ExitStack

import numpy as np
import concourse.bass as bass
from concourse import mybir

F32 = mybir.dt.float32
F32R = mybir.dt.float32r
ACT = mybir.ActivationFunctionType
ALU = mybir.AluOpType
AX = mybir.AxisListType

P = 128
SEQ = 1024
NT = SEQ // P
D = 1024
KT = D // P
HD = 64
EPS = 1e-6
NEG = -1.0e30

A_HEADS, A_KV, B_HEADS = 8, 2, 8
GROUP = A_HEADS // A_KV
D_IN = 3328
QA0, KA0, VA0, GA0, QB0, KB0, VB0, GB0 = 0, 512, 640, 768, 1280, 1792, 2304, 2816
GRID_W, ROWS = 64, 16
NA_KH, NA_KW = 8, 16
RIDX = 2 * NA_KH - 1
CIDX = 2 * NA_KW - 1
NA_LINE = 2 * GRID_W

D_IN2 = 4104
DN_HEADS, DK = 4, 128
CHUNK = 64
Z2, BA2, AQ2, AK2, AV2, AG2 = 1536, 2048, 2056, 2568, 3080, 3592
ATT_HEADS = 8
DILATION = (1, 4, 16)
LEVELS = 6
CW = 256


class Kit:

    def __init__(self, nc, ctx, clears=True):
        self.nc, self.ctx, self.owned = nc, ctx, []
        if clears:
            ctx.callback(self.retire)

    def retire(self):
        if self.owned:
            self.nc.clear_and_free_semaphores(self.owned)
            self.nc.all_engine_barrier()

    def sb(self, name, shape, dt=F32):
        return self.ctx.enter_context(self.nc.sbuf_tensor(name, shape, dt))

    def psum(self, name, shape=(P, 8, 512)):
        return self.ctx.enter_context(self.nc.psum_tensor(name, list(shape), F32))

    def sem(self, name):
        self.owned.append(self.nc.alloc_semaphore(name))
        return self.owned[-1]

    def sems(self, name, n):
        return [self.sem(f"{name}{i}") for i in range(n)]


def keep_busy(nc, bank, ident, n):
    for _ in range(n):
        nc.tensor.matmul(bank.rearrange("p (a c) -> p a c", a=4), ident[:, :],
                         ident[:, :].unsqueeze(1).to_broadcast([P, 4, P]), start=True, stop=True)


def rows(ap, t, c0=0, c1=None):
    return ap[t * P:(t + 1) * P, c0:c1 if c1 is not None else ap.shape[1]]


class Norm:

    def __init__(self, nc, k, tag, x_dram, gain_dram, ident, hT_hi, hT_lo, ps, x_ring, h_ring, gain):
        self.nc, self.x_dram, self.gain_dram, self.ident, self.ps = nc, x_dram, gain_dram, ident, ps
        self.hT_hi, self.hT_lo, self.x, self.h, self.gain = hT_hi, hT_lo, x_ring, h_ring, gain
        self.stat = k.sb(tag + "stat", [P, 4, NT])
        self.x_loaded = k.sems(tag + "x_loaded", len(x_ring))
        self.gain_loaded = k.sem(tag + "gain_loaded")
        self.squares_summed = k.sem(tag + "squares_summed")
        self.var_ready = k.sem(tag + "var_ready")
        self.std_ready = k.sem(tag + "std_ready")
        self.rstd_ready = k.sem(tag + "rstd_ready")
        self.h_ready = k.sem(tag + "h_ready")
        self.half_transposed = k.sem(tag + "half_transposed")
        self.hi_ready = k.sem(tag + "hi_ready")
        self.lo_ready = k.sem(tag + "lo_ready")

    def load(self, sp, t):
        n = len(self.x)
        if t >= n:
            sp.wait_ge(self.h_ready, t - n + 1)
        sp.dma_start(self.x[t % n], rows(self.x_dram, t)).then_inc(self.x_loaded[t % n], 16)
        if t == 0:
            sp.dma_start(self.gain, self.gain_dram).then_inc(self.gain_loaded, 16)

    def std(self, act, t):
        act.wait_ge(self.x_loaded[t % len(self.x)], 16 * (t // len(self.x) + 1))
        if t >= 2:
            act.wait_ge(self.half_transposed, 2 * (t - 1))
        self.nc.scalar.activation(self.h[t % 2], self.x[t % len(self.x)], ACT.Square,
                                  accum_out=self.stat[:, 0, t:t + 1]).then_inc(self.squares_summed, 1)
        act.wait_ge(self.var_ready, t + 1)
        self.nc.scalar.activation(self.stat[:, 2, t:t + 1], self.stat[:, 1, t:t + 1], ACT.Sqrt).then_inc(self.std_ready, 1)

    def normalise(self, dve, t):
        stat = self.stat
        dve.wait_ge(self.squares_summed, t + 1)
        self.nc.vector.tensor_scalar(stat[:, 1, t:t + 1], stat[:, 0, t:t + 1], 1.0 / D, EPS,
                                     ALU.mult, ALU.add).then_inc(self.var_ready, 1)
        dve.wait_ge(self.std_ready, t + 1)
        self.nc.vector.reciprocal(stat[:, 3, t:t + 1], stat[:, 2, t:t + 1]).then_inc(self.rstd_ready, 1)
        dve.wait_ge(self.rstd_ready, t + 1)
        if t == 0:
            dve.wait_ge(self.gain_loaded, 16)
        self.nc.vector.scalar_tensor_tensor(self.h[t % 2], self.x[t % len(self.x)], stat[:, 3, t:t + 1], self.gain,
                                            ALU.mult, ALU.mult).then_inc(self.h_ready, 1)

    def turn(self, pe, t):
        pe.wait_ge(self.h_ready, t + 1)
        for half in range(2):
            if t >= 1:
                pe.wait_ge(self.lo_ready, 2 * t + half - 1)
            for j in range(4):
                c = 4 * half + j
                last = self.nc.tensor.transpose(self.ps[:, 6 + half, j * P:(j + 1) * P],
                                                self.h[t % 2][:, c * P:(c + 1) * P], self.ident[:, :])
            last.then_inc(self.half_transposed, 1)

    def part(self, t, half, out):
        return out[:, 4 * half:4 * half + 4, t * P:(t + 1) * P]

    def split_hi(self, act, t):
        for half in range(2):
            act.wait_ge(self.half_transposed, 2 * t + half + 1)
            self.nc.scalar.copy(self.part(t, half, self.hT_hi),
                                self.ps[:, 6 + half, :].rearrange("p (k c) -> p k c", k=4)).then_inc(self.hi_ready, 1)

    def split_lo(self, dve, t):
        for half in range(2):
            dve.wait_ge(self.hi_ready, 2 * t + half + 1)
            self.nc.vector.tensor_tensor(self.part(t, half, self.hT_lo),
                                         self.ps[:, 6 + half, :].rearrange("p (k c) -> p k c", k=4),
                                         self.part(t, half, self.hT_hi).bitcast(F32),
                                         ALU.subtract).then_inc(self.lo_ready, 1)


class Chunk:

    def __init__(self, col0, width, by, chan=False, dst=None, spill=None, at=0, silu=False, scale=None,
                 before=None, more=0, more_dst=None):
        self.col0, self.width, self.by, self.chan, self.dst = col0, width, by, chan, dst
        self.spill, self.at, self.silu, self.scale = spill, at, silu, scale
        self.before = before
        self.more, self.more_dst = more, more_dst
        self.total = width + more
        self.jobs = 2 * (width // P) if chan else NT


class Projection:
    BANKS = 6
    RING = 3
    LAG = 3

    def __init__(self, nc, k, tag, w_dram, chunks, hT_hi, hT_lo, ps, norm, more=0):
        self.norm = norm
        self.nc, self.w_dram, self.chunks, self.hi, self.lo, self.ps = nc, w_dram, chunks, hT_hi, hT_lo, ps
        self.raw = k.sb(tag + "w_raw", [P, KT, CW + more])
        self.w_hi = k.sb(tag + "w_hi", [P, 2, KT, CW + more], F32R)
        self.w_lo = k.sb(tag + "w_lo", [P, 2, KT, CW + more], F32R)
        self.stage = k.sb(tag + "spill", [P, self.RING, CW])
        self.w_loaded = k.sem(tag + "w_loaded")
        self.w_hi_ready = k.sem(tag + "w_hi_ready")
        self.w_lo_ready = k.sem(tag + "w_lo_ready")
        self.job_done = k.sem(tag + "job_done")
        self.emptied = {"act": k.sem(tag + "emptied_by_act"), "dve": k.sem(tag + "emptied_by_dve")}
        self.stored = k.sems(tag + "stored", self.RING)
        self.jobs = []
        for t in range(NT + self.LAG):
            self.jobs += [(c, j) for c, j in ((0, t), (1, t - self.LAG)) if 0 <= j < NT]
        self.jobs += [(c, j) for c, ch in enumerate(chunks) for j in range(ch.jobs) if c >= 2]
        self.number = {job: n for n, job in enumerate(self.jobs)}

    def emptied_before(self, n, by):
        return sum(self.chunks[c].by == by for c, _ in self.jobs[:n])

    def first_job(self, c):
        return self.number[c, 0]

    def chunk_end(self, c):
        return self.number[c, self.chunks[c].jobs - 1] + 1

    def spills(self):
        return [(c, j) for c, j in self.jobs if self.chunks[c].spill is not None]

    def load(self, sp, c):
        ch = self.chunks[c]
        if c >= 1:
            sp.wait_ge(self.w_lo_ready, c)
        src = self.w_dram[:, ch.col0:ch.col0 + ch.total].rearrange("(k p) n -> p k n", p=P)
        sp.dma_start(self.raw[:, :, 0:ch.total], src).then_inc(self.w_loaded, 16)

    def store(self, sp, n):
        c, j = self.spills()[n]
        ch = self.chunks[c]
        sp.wait_ge(self.emptied[ch.by], self.emptied_before(self.number[c, j] + 1, ch.by))
        sp.dma_start(rows(ch.spill, j, ch.at, ch.at + ch.width),
                     self.stage[:, n % self.RING, 0:ch.width]).then_inc(self.stored[n % self.RING], 16)

    def first_sync(self, sp):
        self.norm.load(sp, 0)
        self.load(sp, 0)
        for t in range(1, 4):
            self.norm.load(sp, t)
        self.load(sp, 1)
        for t in range(4, NT):
            self.norm.load(sp, t)
        self.load(sp, 2)

    def sync(self, sp, also=None):
        for c in range(1, len(self.chunks)):
            if 3 <= c + 1 < len(self.chunks):
                self.load(sp, c + 1)
            if also and c in also:
                also[c](sp)
            for n, (cc, _) in enumerate(self.spills()):
                if cc == c:
                    self.store(sp, n)
        for s in range(self.RING):
            sp.wait_ge(self.stored[s], 16 * len(range(s, len(self.spills()), self.RING)))

    def split_hi(self, act, c):
        if c >= len(self.chunks):
            return
        w = self.chunks[c].total
        act.wait_ge(self.w_loaded, 16 * (c + 1))
        if c >= 2:
            act.wait_ge(self.job_done, self.chunk_end(c - 2))
        self.nc.scalar.copy(self.w_hi[:, c % 2, :, 0:w], self.raw[:, :, 0:w]).then_inc(self.w_hi_ready, 1)

    def split_lo(self, eng, ops, c):
        w = self.chunks[c].total
        eng.wait_ge(self.w_hi_ready, c + 1)
        ops.tensor_tensor(self.w_lo[:, c % 2, :, 0:w], self.raw[:, :, 0:w],
                          self.w_hi[:, c % 2, :, 0:w].bitcast(F32), ALU.subtract).then_inc(self.w_lo_ready, 1)

    def gpsimd(self, pool):
        for c in range(2, len(self.chunks)):
            self.split_lo(pool, self.nc.gpsimd, c)

    def multiply(self, pe, c, j):
        ch, n = self.chunks[c], self.number[c, j]
        w_hi, w_lo = self.w_hi[:, c % 2], self.w_lo[:, c % 2]
        if j == 0:
            pe.wait_ge(self.w_lo_ready, c + 1)
        if n >= self.BANKS:
            by = self.chunks[self.jobs[n - self.BANKS][0]].by
            pe.wait_ge(self.emptied[by], self.emptied_before(n - self.BANKS + 1, by))
        for kt in range(KT):
            if ch.chan:
                tile, half = j // 2, j % 2
                cols, toks = slice(tile * P, (tile + 1) * P), slice(half * 512, half * 512 + 512)
                out = self.ps[:, n % self.BANKS, :]
                passes = [(w_hi[:, kt, cols], self.hi[:, kt, toks]), (w_hi[:, kt, cols], self.lo[:, kt, toks]),
                          (w_lo[:, kt, cols], self.hi[:, kt, toks])]
            else:
                toks = slice(j * P, (j + 1) * P)
                out = self.ps[:, n % self.BANKS, 0:ch.total]
                passes = [(self.hi[:, kt, toks], w_hi[:, kt, 0:ch.total]),
                          (self.hi[:, kt, toks], w_lo[:, kt, 0:ch.total]),
                          (self.lo[:, kt, toks], w_hi[:, kt, 0:ch.total])]
            for i, (lhs, rhs) in enumerate(passes):
                last = self.nc.tensor.matmul(out, lhs, rhs, start=(kt == 0 and i == 0),
                                             stop=(kt == KT - 1 and i == 2))
        last.then_inc(self.job_done, 1)

    def tensor_chunk(self, pe, c):
        for j in range(self.chunks[c].jobs):
            self.multiply(pe, c, j)

    def empty(self, eng, by, c, j):
        ch, n = self.chunks[c], self.number[c, j]
        eng.wait_ge(self.job_done, n + 1)
        src = self.ps[:, n % self.BANKS, 0:512 if ch.chan else ch.width]
        if ch.spill is not None:
            m = self.spills().index((c, j))
            if m >= self.RING:
                eng.wait_ge(self.stored[m % self.RING], 16 * (m // self.RING))
            dst = self.stage[:, m % self.RING, 0:ch.width]
        else:
            if ch.before is not None:
                ch.before(eng, j)
            dst = ch.dst(j)
        if ch.more:
            self.nc.scalar.copy(ch.more_dst(j), self.ps[:, n % self.BANKS, ch.width:ch.total])
        if by == "act":
            op = self.nc.scalar.activation(dst, src, ACT.Silu if ch.silu else ACT.Copy)
        elif ch.scale is not None:
            op = self.nc.vector.tensor_scalar(dst, src, ch.scale, None, ALU.mult)
        else:
            op = self.nc.vector.tensor_copy(dst, src)
        op.then_inc(self.emptied[by], 1)

    def empty_chunk(self, eng, by, c):
        if self.chunks[c].by == by:
            for j in range(self.chunks[c].jobs):
                self.empty(eng, by, c, j)

    def first_tensor(self, pe):
        for t in range(NT + self.LAG + 1):
            if t == 0:
                keep_busy(self.nc, self.ps[:, 0, :], self.norm.ident, 8)
            if t < NT:
                self.norm.turn(pe, t)
            if t == 0:
                keep_busy(self.nc, self.ps[:, 0, :], self.norm.ident, 3)
            if 1 <= t <= NT:
                pe.wait_ge(self.norm.lo_ready, 2 * t)
                self.multiply(pe, 0, t - 1)
            if t > self.LAG:
                self.multiply(pe, 1, t - 1 - self.LAG)

    def first_scalar(self, act):
        for t in range(NT + self.LAG + 2):
            if t < NT:
                self.norm.std(act, t)
            if t == 0:
                self.split_hi(act, 0)
            if 1 <= t <= NT:
                self.norm.split_hi(act, t - 1)
            if t == 2:
                self.split_hi(act, 1)
            if t == NT + 1:
                self.split_hi(act, 2)
            if 2 <= t < NT + 2:
                self.empty(act, "act", 0, t - 2)
            if t >= self.LAG + 2:
                self.empty(act, "act", 1, t - 2 - self.LAG)

    def first_vector(self, dve):
        for t in range(NT + 1):
            if t < NT:
                self.norm.normalise(dve, t)
            if t == 0:
                self.split_lo(dve, self.nc.vector, 0)
            if t >= 1:
                self.norm.split_lo(dve, t - 1)
            if t == 2:
                self.split_lo(dve, self.nc.vector, 1)


def stage_project_1(nc, g, hT_hi, hT_lo):
    with ExitStack() as ctx:
        k = Kit(nc, ctx)
        ps = k.psum("p1_ps")
        qkv = g.qkv_a

        def kb_dst(base):
            return lambda j: base[:, j // 2, (j % 2) * 512:(j % 2) * 512 + 512]

        chunks = [Chunk(QA0 + c * CW, CW, "act", dst=lambda t, c=c: qkv[:, t, c * CW:(c + 1) * CW]) for c in range(3)]
        chunks += [Chunk(GA0 + c * CW, CW, "act", spill=g.gate1, at=c * CW, silu=True) for c in range(2)]
        for c in range(2):
            chunks.append(Chunk(QB0 + c * CW, CW, "dve", chan=True, scale=HD ** -0.5, dst=kb_dst(g.qbT[:, 2 * c:2 * c + 2])))
        for c in range(2):
            chunks.append(Chunk(KB0 + c * CW, CW, "dve", chan=True, dst=kb_dst(g.kbT[:, 2 * c:2 * c + 2])))
        chunks += [Chunk(VB0 + c * CW, CW, "act", spill=g.vb, at=c * CW) for c in range(2)]
        chunks += [Chunk(GB0 + c * CW, CW, "act", spill=g.gate1, at=512 + c * CW, silu=True) for c in range(2)]
        ring_x = [g.kbT[:, i, :] for i in range(4)]
        norm = Norm(nc, k, "n1_", g.x, g.gain1, g.ident, hT_hi, hT_lo, ps, ring_x, [g.qbT[:, i, :] for i in range(2)],
                    g.qbT[:, 2, :])
        pr = Projection(nc, k, "p1_", g.w_in, chunks, hT_hi, hT_lo, ps, norm)
        na_mask = k.sb("na_mask", [P, GRID_W])
        na_loaded = k.sem("na_loaded")
        NH = A_HEADS + A_KV
        tab = k.sb("rope_tab", [P, 2, NT, HD])
        gains = k.sb("rope_gain", [P, 2, 2, HD])
        rot = k.sb("rope_rot", [P, 2, 2, HD])
        tmp = k.sb("rope_tmp", [P, NH * HD])
        tmp2 = k.sb("rope_tmp2", [P, NH * HD])
        stat = k.sb("rope_stat", [P, 3, NT * NH])
        k_twice = k.sb("k_twice", [P, 2, 4, 2, HD])
        k_doubled = k.sem("k_doubled")
        tab_loaded = k.sem("tab_loaded")
        var_ready = k.sem("rope_var_ready")
        std_ready = k.sem("rope_std_ready")
        roped = k.sem("roped")
        dve_step = k.sem("rope_step")
        k_transposed = k.sem("k_transposed")
        kk_ready = k.sem("kk_ready")
        n_a = 3 * NT
        block = ctx.enter_context(nc.Block())

        @block.sync
        def _(sp):
            pr.first_sync(sp)
            sp.dma_start(tab[:, :, :, :], g.rope).then_inc(tab_loaded, 16)
            sp.dma_start(gains[:, :, :, :], g.gain_a).then_inc(tab_loaded, 16)
            sp.dma_start(na_mask[:, :], g.na_mask).then_inc(na_loaded, 16)
            W = 4 * RIDX * NA_LINE
            for i in range(2):
                band = bass.AP(tensor=g.na_lines.tensor, offset=i * GRID_W * W + GRID_W - 1,
                               ap=[[W - 1, GRID_W], [NA_LINE, 4 * RIDX], [1, GRID_W]])
                sp.dma_start(g.na_table[i * GRID_W:(i + 1) * GRID_W, :, :], band).then_inc(na_loaded, 16)
            pr.sync(sp)

        @block.gpsimd
        def _(pool):
            pr.gpsimd(pool)
            pool.wait_ge(roped, NT)
            for n in range(2 * A_KV):
                kv, half = n // 2, n % 2
                if n >= 2:
                    pool.wait_ge(k_transposed, n - 1)
                src = qkv[:, 4 * half:4 * half + 4, 512 + kv * HD:512 + (kv + 1) * HD]
                nc.gpsimd.tensor_copy(k_twice[:, n % 2, :, :, :],
                                      src.unsqueeze(2).to_broadcast([P, 4, 2, HD])).then_inc(k_doubled, 1)

        @block.tensor
        def _(pe):
            pr.first_tensor(pe)
            for c in range(2, len(chunks)):
                pr.tensor_chunk(pe, c)
            for n in range(2 * A_KV):
                pe.wait_ge(k_doubled, n + 1)
                if n >= 2:
                    pe.wait_ge(kk_ready, n - 1)
                for j in range(4):
                    last = nc.tensor.transpose(ps[:, 6 + n % 2, j * P:(j + 1) * P],
                                               k_twice[:, n % 2, j, :, :].rearrange("p a d -> p (a d)"), g.ident[:, :])
                last.then_inc(k_transposed, 1)

        @block.scalar
        def _(act):
            pr.first_scalar(act)
            for c in range(2, len(chunks)):
                pr.split_hi(act, c + 1)
                pr.empty_chunk(act, "act", c)
                if c == 3:
                    act.wait_ge(var_ready, 1)
                    nc.scalar.activation(stat[:, 1, :], stat[:, 0, :], ACT.Sqrt).then_inc(std_ready, 1)

        @block.vector
        def _(dve):
            steps = 0

            def step(op):
                nonlocal steps
                steps += 1
                op.then_inc(dve_step, 1)
                dve.wait_ge(dve_step, steps)

            pr.first_vector(dve)
            for t in range(NT):
                dve.wait_ge(pr.emptied["act"], 2 * NT + t + 1)
                x = qkv[:, t, 0:NH * HD]
                step(nc.vector.tensor_tensor(tmp[:, :], x, x, ALU.mult))
                step(nc.vector.tensor_reduce(stat[:, 0, t * NH:(t + 1) * NH],
                                             tmp[:, :].rearrange("p (h d) -> p h d", d=HD), AX.X, ALU.add))
            nc.vector.tensor_scalar(stat[:, 0, :], stat[:, 0, :], 1.0 / HD, EPS, ALU.mult, ALU.add).then_inc(var_ready, 1)
            dve.wait_ge(std_ready, 1)
            step(nc.vector.reciprocal(stat[:, 2, :], stat[:, 1, :]))
            q_rstd = stat[:, 2, :].rearrange("p (t h) -> p t h", h=NH)[:, :, 0:A_HEADS]
            step(nc.vector.tensor_scalar(q_rstd, q_rstd, HD ** -0.5, None, ALU.mult))
            dve.wait_ge(tab_loaded, 32)
            for t in range(NT):
                x = qkv[:, t, 0:NH * HD].rearrange("p (h d) -> p h d", d=HD)
                r = stat[:, 2, t * NH:(t + 1) * NH].unsqueeze(2).to_broadcast([P, NH, HD])
                step(nc.vector.tensor_tensor(x, x, r, ALU.mult))
                for i in range(2):
                    c = tab[:, i, t, :].unsqueeze(1).to_broadcast([P, 2, HD])
                    step(nc.vector.tensor_tensor(rot[:, i, :, :], c, gains[:, i, :, :], ALU.mult))
                for i, (h0, h1) in enumerate(((0, A_HEADS), (A_HEADS, NH))):
                    n = h1 - h0
                    xs = x[:, h0:h1, :]
                    c = rot[:, 0, i, :].unsqueeze(1).to_broadcast([P, n, HD])
                    a = tmp[:, h0 * HD:h1 * HD].rearrange("p (h d) -> p h d", d=HD)
                    b = tmp2[:, h0 * HD:h1 * HD].rearrange("p (h x s e) -> p h x s e", x=2, s=2, e=16)
                    x5 = qkv[:, t, h0 * HD:h1 * HD].rearrange("p (h x s e) -> p h x s e", x=2, s=2, e=16)
                    s5 = rot[:, 1, i, :].rearrange("p (x s e) -> p x s e", x=2, s=2)
                    nc.vector.tensor_tensor(a, xs, c, ALU.mult)
                    for half in range(2):
                        s = s5[:, :, half, :].unsqueeze(1).to_broadcast([P, n, 2, 16])
                        op = nc.vector.tensor_tensor(b[:, :, :, half, :], x5[:, :, :, 1 - half, :], s, ALU.mult)
                    step(op)
                    op = nc.vector.tensor_tensor(xs, a, tmp2[:, h0 * HD:h1 * HD].rearrange("p (h d) -> p h d", d=HD), ALU.add)
                    if i == 0:
                        step(op)
                    else:
                        op.then_inc(roped, 1)
            dve.wait_ge(na_loaded, 48)
            nc.vector.tensor_tensor(g.na_table[:, :, :], g.na_table[:, :, :],
                                    na_mask[:, :].unsqueeze(1).to_broadcast([P, 4 * RIDX, GRID_W]), ALU.add)
            for c in range(len(chunks)):
                pr.empty_chunk(dve, "dve", c)
            for n in range(2 * A_KV):
                kv, half = n // 2, n % 2
                dve.wait_ge(k_transposed, n + 1)
                both = g.kk[:, kv, half * 512:half * 512 + 512]
                step(nc.vector.tensor_copy(both, ps[:, 6 + n % 2, :]))
                lo = g.kk[HD:P, kv, half * 512:half * 512 + 512]
                nc.vector.tensor_tensor(lo, ps[HD:P, 6 + n % 2, :], lo.bitcast(F32), ALU.subtract).then_inc(kk_ready, 1)



def stage_attention_a(nc, g):
    with ExitStack() as ctx:
        k = Kit(nc, ctx)
        ps = k.psum("a_ps")
        units = [(t, h) for t in range(NT) for h in range(A_HEADS)]
        n_units = len(units)
        n_groups = n_units // 4
        q_hi = k.sb("a_q_hi", [P, 2, 4 * P], F32R)
        q_lo = k.sb("a_q_lo", [P, 2, 4 * P], F32R)
        q_twice = k.sb("a_q_twice", [P, 2, 4, 2, HD])
        v = k.sb("a_v", [P, A_KV, NT, 2, HD], F32R)
        prob = k.sb("a_prob", [P, 2, SEQ])
        pt_hi = k.sb("a_pt_hi", [P, 3, NT, 4 * P], F32R)
        pt_lo = k.sb("a_pt_lo", [P, 3, NT, 4 * P], F32R)
        out_t = k.sb("a_out_t", [P, 4 * P])
        fold = k.sb("a_fold", [P, HD])
        stat = k.sb("a_stat", [P, 3, n_units])
        fold_loaded = k.sem("a_fold_loaded")
        q_doubled = k.sem("a_q_doubled")
        q_transposed = k.sem("a_q_transposed")
        q_hi_ready = k.sem("a_q_hi_ready")
        q_lo_ready = k.sem("a_q_lo_ready")
        v_hi_ready = k.sem("a_v_hi_ready")
        v_lo_ready = k.sem("a_v_lo_ready")
        scores_ready = k.sem("a_scores_ready")
        max_ready = k.sem("a_max_ready")
        prob_ready = k.sem("a_prob_ready")
        half_transposed = k.sem("a_half_transposed")
        pt_hi_ready = k.sem("a_pt_hi_ready")
        pt_lo_ready = k.sem("a_pt_lo_ready")
        values_done = k.sem("a_values_done")
        out_t_ready = k.sem("a_out_t_ready")
        folded = k.sem("a_folded")
        recip_ready = k.sem("a_recip_ready")
        out_stored = k.sem("a_out_stored")
        block = ctx.enter_context(nc.Block())

        @block.sync
        def _(sp):
            sp.dma_start(fold[:, :], g.fold_d).then_inc(fold_loaded, 16)

        @block.gpsimd
        def _(pool):
            for grp in range(n_groups):
                t, h = units[4 * grp]
                if grp >= 2:
                    pool.wait_ge(q_transposed, grp - 1)
                src = g.qkv_a[:, t, h * HD:(h + 4) * HD].rearrange("p (h d) -> p h d", d=HD)
                nc.gpsimd.tensor_copy(q_twice[:, grp % 2, :, :, :],
                                      src.unsqueeze(2).to_broadcast([P, 4, 2, HD])).then_inc(q_doubled, 1)

        def part(t, grp, half, i):
            return t[:, grp % 3, 4 * half:4 * half + 4, i * P:(i + 1) * P]

        @block.tensor
        def _(pe):
            def turn_q(grp):
                pe.wait_ge(q_doubled, grp + 1)
                if grp >= 1:
                    pe.wait_ge(q_lo_ready, grp)
                for i in range(4):
                    last = nc.tensor.transpose(ps[:, 6, i * P:(i + 1) * P],
                                               q_twice[:, grp % 2, i, :, :].rearrange("p a d -> p (a d)"), g.ident[:, :])
                last.then_inc(q_transposed, 1)

            def scores(u):
                t, h = units[u]
                grp, i = u // 4, u % 4
                pe.wait_ge(q_lo_ready, grp + 1)
                if u >= 2:
                    pe.wait_ge(prob_ready, u - 1)
                for half in range(2):
                    keys = g.kk[:, h // GROUP, half * 512:half * 512 + 512]
                    bank = ps[:, 2 * (u % 2) + half, :]
                    nc.tensor.matmul(bank, q_hi[:, grp % 2, i * P:(i + 1) * P], keys, start=True, stop=False)
                    last = nc.tensor.matmul(bank, q_lo[:, grp % 2, i * P:(i + 1) * P], keys, start=False, stop=True)
                last.then_inc(scores_ready, 1)

            def turn_probs(u):
                pe.wait_ge(prob_ready, u + 1)
                for half in range(2):
                    if u >= 1:
                        pe.wait_ge(pt_lo_ready, 2 * u + half - 1)
                    for j in range(4):
                        c = 4 * half + j
                        last = nc.tensor.transpose(ps[:, 4 + half, j * P:(j + 1) * P],
                                                   prob[:, u % 2, c * P:(c + 1) * P], g.ident[:, :])
                    last.then_inc(half_transposed, 1)

            def values(grp, tiles):
                kv = units[4 * grp][1] // GROUP
                if tiles[0] == 0:
                    pe.wait_ge(pt_lo_ready, 8 * (grp + 1))
                    pe.wait_ge(v_lo_ready, kv + 1)
                    if grp >= 1:
                        pe.wait_ge(out_stored, grp)
                for c in tiles:
                    if c >= 1:
                        nc.tensor.matmul(ps[0:HD, 7, :], v[:, kv, c, 0, :], pt_lo[:, grp % 3, c, :], start=False, stop=False)
                    last = nc.tensor.matmul(ps[:, 7, :], v[:, kv, c, :, :].rearrange("p a d -> p (a d)"),
                                            pt_hi[:, grp % 3, c, :], start=(c == 0), stop=(c == NT - 1))
                    if c == 0:
                        nc.tensor.matmul(ps[0:HD, 7, :], v[:, kv, c, 0, :], pt_lo[:, grp % 3, c, :], start=False, stop=False)
                if tiles[-1] == NT - 1:
                    last.then_inc(values_done, 1)

            def turn_back(grp):
                pe.wait_ge(out_t_ready, grp + 1)
                if grp == 0:
                    pe.wait_ge(fold_loaded, 16)
                for i in range(4):
                    last = nc.tensor.matmul(ps[:, 7, i * HD:(i + 1) * HD], out_t[:, i * P:(i + 1) * P], fold[:, :],
                                            start=True, stop=True)
                last.then_inc(folded, 1)

            turn_q(0)
            scores(0)
            scores(1)
            turn_q(1)
            for u in range(n_units + 6):
                grp = u // 4
                if u < n_units:
                    turn_probs(u)
                if u + 2 < n_units:
                    scores(u + 2)
                if u % 4 == 0 and grp >= 2:
                    values(grp - 2, (6, 7))
                if u % 4 == 1 and grp >= 2:
                    turn_back(grp - 2)
                if u % 4 == 2 and 1 <= grp <= n_groups:
                    values(grp - 1, (0, 1, 2))
                if u % 4 == 3:
                    if grp + 2 < n_groups:
                        turn_q(grp + 2)
                    if 1 <= grp <= n_groups:
                        values(grp - 1, (3, 4, 5))

        @block.vector
        def _(dve):
            def split_v(kv):
                v0 = 640 + kv * HD
                src = g.qkv_a[:, :, v0:v0 + HD]
                nc.vector.tensor_copy(v[:, kv, :, 0, :], src).then_inc(v_hi_ready, 1)
                dve.wait_ge(v_hi_ready, kv + 1)
                nc.vector.tensor_tensor(v[:, kv, :, 1, :], src, v[:, kv, :, 0, :].bitcast(F32),
                                        ALU.subtract).then_inc(v_lo_ready, 1)

            def q_low(grp):
                dve.wait_ge(q_hi_ready, grp + 1)
                nc.vector.tensor_tensor(q_lo[:, grp % 2, :], ps[:, 6, :], q_hi[:, grp % 2, :].bitcast(F32),
                                        ALU.subtract).then_inc(q_lo_ready, 1)

            def row_max(u):
                dve.wait_ge(scores_ready, u + 1)
                s = ps[:, 2 * (u % 2):2 * (u % 2) + 2, :].rearrange("p b n -> p (b n)")
                nc.vector.tensor_reduce(stat[:, 0, u:u + 1], s, AX.X, ALU.max, negate=True).then_inc(max_ready, 1)

            def probs_low(u, half):
                grp, i = u // 4, u % 4
                dve.wait_ge(pt_hi_ready, 2 * u + half + 1)
                nc.vector.tensor_tensor(part(pt_lo, grp, half, i), ps[:, 4 + half, :].rearrange("p (c q) -> p c q", c=4),
                                        part(pt_hi, grp, half, i).bitcast(F32), ALU.subtract).then_inc(pt_lo_ready, 1)

            def copy_out(grp):
                dve.wait_ge(values_done, grp + 1)
                if grp >= 1:
                    dve.wait_ge(folded, grp)
                nc.vector.tensor_copy(out_t[:, :], ps[:, 7, :]).then_inc(out_t_ready, 1)

            def store(grp):
                t, h = units[4 * grp]
                dve.wait_ge(prob_ready, 4 * grp + 4)
                nc.vector.reciprocal(stat[:, 2, 4 * grp:4 * grp + 4], stat[:, 1, 4 * grp:4 * grp + 4]).then_inc(recip_ready, 1)
                dve.wait_ge(recip_ready, grp + 1)
                dve.wait_ge(folded, grp + 1)
                out = g.qkv_a[:, t, h * HD:(h + 4) * HD].rearrange("p (h d) -> p h d", d=HD)
                nc.vector.tensor_tensor(out, ps[:, 7, 0:4 * HD].rearrange("p (h d) -> p h d", d=HD),
                                        stat[:, 2, 4 * grp:4 * grp + 4].unsqueeze(2).to_broadcast([P, 4, HD]),
                                        ALU.mult).then_inc(out_stored, 1)

            q_low(0)
            row_max(0)
            split_v(0)
            split_v(1)
            for u in range(n_units + 7):
                grp = u // 4
                if u + 1 < n_units:
                    row_max(u + 1)
                if u % 4 == 0 and grp + 1 < n_groups:
                    q_low(grp + 1)
                if u % 4 == 1 and grp >= 2:
                    copy_out(grp - 2)
                if u % 4 == 2 and grp >= 2:
                    store(grp - 2)
                if u < n_units:
                    probs_low(u, 0)
                    probs_low(u, 1)

        @block.scalar
        def _(act):
            def q_high(grp):
                act.wait_ge(q_transposed, grp + 1)
                if grp >= 2:
                    act.wait_ge(scores_ready, 4 * (grp - 1))
                nc.scalar.copy(q_hi[:, grp % 2, :], ps[:, 6, :]).then_inc(q_hi_ready, 1)

            def exponentials(u):
                act.wait_ge(max_ready, u + 1)
                if u >= 2:
                    act.wait_ge(half_transposed, 2 * (u - 1))
                s = ps[:, 2 * (u % 2):2 * (u % 2) + 2, :].rearrange("p b n -> p (b n)")
                nc.scalar.activation(prob[:, u % 2, :], s, ACT.Exp, bias=stat[:, 0, u:u + 1],
                                     accum_out=stat[:, 1, u:u + 1]).then_inc(prob_ready, 1)

            def probs_high(u, half):
                grp, i = u // 4, u % 4
                if i == 0 and half == 0 and grp >= 3:
                    act.wait_ge(values_done, grp - 2)
                act.wait_ge(half_transposed, 2 * u + half + 1)
                nc.scalar.copy(part(pt_hi, grp, half, i),
                               ps[:, 4 + half, :].rearrange("p (c q) -> p c q", c=4)).then_inc(pt_hi_ready, 1)

            q_high(0)
            exponentials(0)
            q_high(1)
            for u in range(n_units):
                probs_high(u, 0)
                probs_high(u, 1)
                if u + 1 < n_units:
                    exponentials(u + 1)
                if u % 4 == 3 and u // 4 + 2 < n_groups:
                    q_high(u // 4 + 2)


def stage_attention_b(nc, g, w_hi, w_lo):
    with ExitStack() as ctx:
        k = Kit(nc, ctx)
        ws = WeightSplit(nc, k, "b_w_", g.w_out, w_hi, w_lo)
        ps = k.psum("b_ps")
        PAIRS = B_HEADS // 2
        units = [(p, r) for p in range(PAIRS) for r in range(ROWS)]
        n_units = len(units)
        W = NA_KH * GRID_W
        v = k.sb("b_v", [P, NT, 512])
        q_diag = k.sb("b_q_diag", [P, 4, 2, P], F32R)
        zeros = k.sb("b_zeros", [P, P])
        k_hi = k.sb("b_k_hi", [P, 2, SEQ], F32R)
        k_lo = k.sb("b_k_lo", [P, 2, SEQ], F32R)
        zeros_ready = k.sem("b_zeros_ready")
        k_hi_ready = k.sem("b_k_hi_ready")
        k_lo_ready = k.sem("b_k_lo_ready")
        prob = k.sb("b_prob", [P, 2, W + 2 * GRID_W])
        prob_t = k.sb("b_prob_t", [P, 2, 5 * P])
        out = k.sb("b_out", [P, 2, ROWS, HD])
        stat = k.sb("b_stat", [P, 3, n_units])
        v_loaded = k.sem("b_v_loaded")
        q_zeroed = k.sem("b_q_zeroed")
        margins_zeroed = k.sem("b_margins_zeroed")
        q_placed = k.sem("b_q_placed")
        scores_ready = k.sem("b_scores_ready")
        max_ready = k.sem("b_max_ready")
        prob_ready = k.sem("b_prob_ready")
        turned_first = k.sem("b_turned_first")
        turned_second = k.sem("b_turned_second")
        pt_first_ready = k.sem("b_pt_first_ready")
        pt_second_ready = k.sem("b_pt_second_ready")
        out_ready = k.sem("b_out_ready")
        recip_ready = k.sem("b_recip_ready")
        out_stored = k.sem("b_out_stored")
        pair_sent = k.sems("b_pair_sent", 2)

        def window(r):
            r0 = min(max(r - NA_KH // 2, 0), ROWS - NA_KH)
            return r0, r0 // 2, 4 + r0 % 2, GRID_W * (1 - r0 % 2)

        block = ctx.enter_context(nc.Block())

        @block.sync
        def _(sp):
            sp.dma_start(v[:, :, :], g.vb.rearrange("(t p) c -> p t c", p=P)).then_inc(v_loaded, 16)
            for kt in range(4):
                ws.load(sp, kt)
            for p in range(PAIRS):
                if 0 < p < 3:
                    ws.load(sp, 2 * p + 2)
                    ws.load(sp, 2 * p + 3)
                sp.wait_ge(out_stored, 2 * ROWS * (p + 1))
                for i in range(2):
                    h = 2 * p + i
                    dst = g.out_b[:, h * HD:(h + 1) * HD].rearrange("(r c) d -> c r d", c=GRID_W)
                    sp.dma_start(dst, out[i * HD:(i + 1) * HD, p % 2, :, :]).then_inc(pair_sent[p % 2], 16)
            for i in range(2):
                sp.wait_ge(pair_sent[i], 32 * (PAIRS // 2))

        @block.gpsimd
        def _(pool):
            pool.wait_ge(q_zeroed, 1)
            for u, (p, r) in enumerate(units):
                if u >= 4:
                    pool.wait_ge(scores_ready, u - 3)
                for i in range(2):
                    half = slice(i * HD, (i + 1) * HD)
                    q = g.qbT[half, p, r * GRID_W:(r + 1) * GRID_W]
                    hi = q_diag[half, u % 4, 0, half]
                    nc.gpsimd.tensor_copy(hi, q).then_inc(q_placed, 1)
                    pool.wait_ge(q_placed, 4 * u + 2 * i + 1)
                    nc.gpsimd.tensor_tensor(q_diag[half, u % 4, 1, half], q, hi.bitcast(F32), ALU.subtract).then_inc(q_placed, 1)
                    pool.wait_ge(q_placed, 4 * u + 2 * i + 2)

        @block.tensor
        def _(pe):
            def scores(u):
                p, r = units[u]
                r0 = window(r)[0]
                pe.wait_ge(q_placed, 4 * u + 4)
                pe.wait_ge(k_lo_ready, p + 1)
                if u >= 2:
                    pe.wait_ge(max_ready, u - 1)
                hi, lo = (t[:, p % 2, r0 * GRID_W:r0 * GRID_W + W] for t in (k_hi, k_lo))
                nc.tensor.matmul(ps[:, u % 2, :], q_diag[:, u % 4, 0, :], hi, start=True, stop=False)
                nc.tensor.matmul(ps[:, u % 2, :], q_diag[:, u % 4, 0, :], lo, start=False, stop=False)
                nc.tensor.matmul(ps[:, u % 2, :], q_diag[:, u % 4, 1, :], hi, start=False, stop=True).then_inc(scores_ready, 1)

            def turn_probs(u):
                _, _, tiles, c0 = window(units[u][1])
                pe.wait_ge(prob_ready, u + 1)
                if u >= 2:
                    pe.wait_ge(pt_first_ready, u - 1)
                    pe.wait_ge(pt_second_ready, u - 1)
                for j in range(tiles):
                    bank, at = (2 * (u % 2) + 2, j) if j < 2 else (2 * (u % 2) + 3, j - 2)
                    op = nc.tensor.transpose(ps[:, bank, at * P:(at + 1) * P],
                                             prob[:, u % 2, c0 + j * P:c0 + (j + 1) * P], g.ident[:, :])
                    if j == 1:
                        op.then_inc(turned_first, 1)
                    if j == tiles - 1:
                        op.then_inc(turned_second, 1)

            def values(u):
                p, r = units[u]
                _, t0, tiles, _ = window(r)
                pe.wait_ge(pt_first_ready, u + 1)
                pe.wait_ge(pt_second_ready, u + 1)
                if u == 0:
                    pe.wait_ge(v_loaded, 16)
                if u >= 2:
                    pe.wait_ge(out_stored, 2 * (u - 1))
                for j in range(tiles):
                    last = nc.tensor.matmul(ps[:, 6 + u % 2, 0:P], prob_t[:, u % 2, j * P:(j + 1) * P],
                                            v[:, t0 + j, p * P:(p + 1) * P], start=(j == 0), stop=(j == tiles - 1))
                last.then_inc(out_ready, 1)

            scores(0)
            scores(1)
            for u in range(n_units):
                turn_probs(u)
                if u + 2 < n_units:
                    scores(u + 2)
                if u >= 1:
                    values(u - 1)
            values(n_units - 1)

        @block.vector
        def _(dve):
            def bias_and_max(u):
                p, r = units[u]
                first = window(r)[0] - r + NA_KH - 1
                dve.wait_ge(scores_ready, u + 1)
                if u >= 2:
                    dve.wait_ge(turned_second, u - 1)
                bias = g.na_table[:, p * RIDX + first:p * RIDX + first + NA_KH, :].rearrange("p r c -> p (r c)")
                nc.vector.tensor_tensor_reduce(prob[:, u % 2, GRID_W:GRID_W + W], ps[:, u % 2, :], bias, -1.0, -NEG,
                                               ALU.add, ALU.min, stat[:, 0, u:u + 1]).then_inc(max_ready, 1)

            def empty_second(u):
                n = window(units[u][1])[2] - 2
                dve.wait_ge(turned_second, u + 1)
                if u >= 2:
                    dve.wait_ge(out_ready, u - 1)
                nc.vector.tensor_copy(prob_t[:, u % 2, 2 * P:(2 + n) * P],
                                      ps[:, 2 * (u % 2) + 3, 0:n * P]).then_inc(pt_second_ready, 1)

            def store(u):
                p, r = units[u]
                dve.wait_ge(prob_ready, u + 1)
                nc.vector.reciprocal(stat[:, 2, u:u + 1], stat[:, 1, u:u + 1]).then_inc(recip_ready, 1)
                dve.wait_ge(recip_ready, u + 1)
                dve.wait_ge(out_ready, u + 1)
                if r == 0 and p >= 2:
                    dve.wait_ge(pair_sent[p % 2], 32)
                for i in range(2):
                    half = slice(i * HD, (i + 1) * HD)
                    nc.vector.tensor_scalar(out[half, p % 2, r, :], ps[half, 6 + u % 2, half],
                                            stat[half, 2, u:u + 1], None, ALU.mult).then_inc(out_stored, 1)

            def keys_low(p):
                dve.wait_ge(k_hi_ready, p + 1)
                nc.vector.tensor_tensor(k_lo[:, p % 2, :], g.kbT[:, p, :], k_hi[:, p % 2, :].bitcast(F32),
                                        ALU.subtract).then_inc(k_lo_ready, 1)

            nc.vector.memset(zeros[:, :], 0.0).then_inc(zeros_ready, 1)
            dve.wait_ge(zeros_ready, 1)
            nc.vector.tensor_copy(q_diag[:, :, :, :].rearrange("p n a c -> p (n a) c"),
                                  zeros[:, :].unsqueeze(1).to_broadcast([P, 8, P])).then_inc(q_zeroed, 1)
            nc.vector.memset(prob[:, :, :], 0.0).then_inc(margins_zeroed, 1)
            keys_low(0)
            dve.wait_ge(margins_zeroed, 1)
            bias_and_max(0)
            bias_and_max(1)
            for u in range(n_units):
                if u % ROWS == 4 and u // ROWS + 1 < PAIRS:
                    keys_low(u // ROWS + 1)
                if u % 6 == 5 and u // 6 < KT:
                    ws.split_lo(dve, nc.vector, u // 6)
                empty_second(u)
                if u >= 2:
                    store(u - 2)
                if u + 2 < n_units:
                    bias_and_max(u + 2)
            store(n_units - 2)
            store(n_units - 1)

        @block.scalar
        def _(act):
            def exponentials(u):
                act.wait_ge(max_ready, u + 1)
                s = prob[:, u % 2, GRID_W:GRID_W + W]
                nc.scalar.activation(s, s, ACT.Exp, bias=stat[:, 0, u:u + 1], scale=-1.0,
                                     accum_out=stat[:, 1, u:u + 1]).then_inc(prob_ready, 1)

            def empty_first(u):
                act.wait_ge(turned_first, u + 1)
                if u >= 2:
                    act.wait_ge(out_ready, u - 1)
                nc.scalar.copy(prob_t[:, u % 2, 0:2 * P], ps[:, 2 * (u % 2) + 2, 0:2 * P]).then_inc(pt_first_ready, 1)

            def keys_high(p):
                if p >= 2:
                    act.wait_ge(scores_ready, ROWS * (p - 1))
                nc.scalar.copy(k_hi[:, p % 2, :], g.kbT[:, p, :]).then_inc(k_hi_ready, 1)

            keys_high(0)
            exponentials(0)
            exponentials(1)
            for u in range(n_units):
                if u % ROWS == 2 and u // ROWS + 1 < PAIRS:
                    keys_high(u // ROWS + 1)
                if u % 6 == 3 and u // 6 < KT:
                    ws.split_hi(act, nc.scalar.copy, u // 6)
                empty_first(u)
                if u + 2 < n_units:
                    exponentials(u + 2)


class WeightSplit:

    def __init__(self, nc, k, tag, w_dram, w_hi, w_lo):
        self.nc, self.w_dram, self.hi, self.lo = nc, w_dram, w_hi, w_lo
        self.raw = k.sb(tag + "raw", [P, 2, D])
        self.loaded = k.sems(tag + "loaded", 2)
        self.hi_ready = k.sem(tag + "hi_ready")
        self.lo_ready = k.sem(tag + "lo_ready")

    def load(self, sp, kt):
        if kt >= 2:
            sp.wait_ge(self.lo_ready, kt - 1)
        sp.dma_start(self.raw[:, kt % 2, :], rows(self.w_dram, kt)).then_inc(self.loaded[kt % 2], 16)

    def split_hi(self, eng, copy, kt):
        eng.wait_ge(self.loaded[kt % 2], 16 * (kt // 2 + 1))
        copy(self.hi[:, kt, :], self.raw[:, kt % 2, :]).then_inc(self.hi_ready, 1)

    def split_lo(self, eng, ops, kt):
        eng.wait_ge(self.hi_ready, kt + 1)
        ops.tensor_tensor(self.lo[:, kt, :], self.raw[:, kt % 2, :], self.hi[:, kt, :].bitcast(F32),
                                     ALU.subtract).then_inc(self.lo_ready, 1)


class OutProjection:

    def __init__(self, nc, k, tag, g, ps, w_hi, w_lo, mixed, mixed_ready):
        self.nc, self.g, self.ps, self.w_hi, self.w_lo = nc, g, ps, w_hi, w_lo
        self.mixed, self.mixed_ready = mixed, mixed_ready
        self.hi = k.sb(tag + "mT_hi", [P, 2, KT, P], F32R)
        self.lo = k.sb(tag + "mT_lo", [P, 2, KT, P], F32R)
        self.half_turned = k.sem(tag + "half_turned")
        self.hi_ready = k.sem(tag + "mT_hi_ready")
        self.lo_ready = k.sem(tag + "mT_lo_ready")
        self.job_done = k.sem(tag + "job_done")
        self.job_emptied = k.sem(tag + "job_emptied")

    def turn(self, pe, t):
        for half in range(2):
            n = 2 * t + half
            pe.wait_ge(self.mixed_ready[half], t + 1)
            if n >= 4:
                pe.wait_ge(self.lo_ready, n - 3)
            for j in range(4):
                c = 4 * half + j
                last = self.nc.tensor.transpose(self.ps[:, n % 4, j * P:(j + 1) * P],
                                                self.mixed[:, t % 2, c * P:(c + 1) * P], self.g.ident[:, :])
            last.then_inc(self.half_turned, 1)

    def multiply(self, pe, t):
        pe.wait_ge(self.lo_ready, 2 * t + 2)
        for half in range(2):
            n = 2 * t + half
            if n >= 4:
                pe.wait_ge(self.job_emptied, n - 3)
            cols = slice(half * 512, half * 512 + 512)
            for kt in range(KT):
                hi, lo = self.hi[:, t % 2, kt, :], self.lo[:, t % 2, kt, :]
                for i, (a, b) in enumerate(((hi, self.w_hi), (hi, self.w_lo), (lo, self.w_hi))):
                    last = self.nc.tensor.matmul(self.ps[:, 4 + n % 4, :], a, b[:, kt, cols],
                                                 start=(kt == 0 and i == 0), stop=(kt == KT - 1 and i == 2))
            last.then_inc(self.job_done, 1)

    def tensor(self, pe, waiting):
        keep_busy(self.nc, self.ps[:, 4, :], self.g.ident, waiting)
        self.turn(pe, 0)
        for t in range(NT):
            if t + 1 < NT:
                self.turn(pe, t + 1)
            self.multiply(pe, t)

    def split_hi(self, act, t):
        for half in range(2):
            n = 2 * t + half
            act.wait_ge(self.half_turned, n + 1)
            if n >= 4:
                act.wait_ge(self.job_done, 2 * (t - 1))
            self.nc.scalar.copy(self.hi[:, t % 2, 4 * half:4 * half + 4, :],
                                self.ps[:, n % 4, :].rearrange("p (k c) -> p k c", k=4)).then_inc(self.hi_ready, 1)

    def split_lo(self, dve, t):
        for half in range(2):
            n = 2 * t + half
            dve.wait_ge(self.hi_ready, n + 1)
            hi = self.hi[:, t % 2, 4 * half:4 * half + 4, :]
            self.nc.vector.tensor_tensor(self.lo[:, t % 2, 4 * half:4 * half + 4, :],
                                         self.ps[:, n % 4, :].rearrange("p (k c) -> p k c", k=4),
                                         hi.bitcast(F32), ALU.subtract).then_inc(self.lo_ready, 1)

    def add_residual(self, dve, t, y, x):
        for half in range(2):
            n = 2 * t + half
            cols = slice(half * 512, half * 512 + 512)
            dve.wait_ge(self.job_done, n + 1)
            self.nc.vector.tensor_tensor(y[:, cols], self.ps[:, 4 + n % 4, :], x[:, cols],
                                         ALU.add).then_inc(self.job_emptied, 1)


def stage_out_1(nc, g, w_hi, w_lo):
    with ExitStack() as ctx:
        k = Kit(nc, ctx)
        ps = k.psum("o1_ps")
        gate = k.sb("o1_gate", [P, 2, D])
        out_b = k.sb("o1_out_b", [P, 2, 512])
        x = k.sb("o1_x", [P, 2, D])
        mixed = k.sb("o1_mixed", [P, 2, D])
        y = k.sb("o1_y", [P, 2, D])
        junk = k.sb("o1_junk", [P, D])
        gain = k.sb("o1_gain", [P, D])
        stat = k.sb("o1_stat", [P, 4, NT])
        gate_loaded = k.sems("o1_gate_loaded", 2)
        b_loaded = k.sems("o1_b_loaded", 2)
        x_loaded = k.sems("o1_x_loaded", 2)
        gain_loaded = k.sem("o1_gain_loaded")
        mixed_a_ready = k.sem("o1_mixed_a_ready")
        mixed_b_ready = k.sem("o1_mixed_b_ready")
        squares_summed = k.sem("o1_squares_summed")
        var_ready = k.sem("o1_var_ready")
        std_ready = k.sem("o1_std_ready")
        rstd_ready = k.sem("o1_rstd_ready")
        y_ready = k.sem("o1_y_ready")
        y_stored = k.sems("o1_y_stored", 2)
        op = OutProjection(nc, k, "o1_", g, ps, w_hi, w_lo, mixed, (mixed_a_ready, mixed_b_ready))
        block = ctx.enter_context(nc.Block())

        @block.sync
        def _(sp):
            def load(t):
                if t >= 2:
                    sp.wait_ge(mixed_a_ready, t - 1)
                    sp.wait_ge(mixed_b_ready, t - 1)
                sp.dma_start(gate[:, t % 2, :], rows(g.gate1, t)).then_inc(gate_loaded[t % 2], 16)
                sp.dma_start(out_b[:, t % 2, :], rows(g.out_b, t)).then_inc(b_loaded[t % 2], 16)
                if t >= 2:
                    sp.wait_ge(op.job_emptied, 2 * (t - 1))
                sp.dma_start(x[:, t % 2, :], rows(g.x, t)).then_inc(x_loaded[t % 2], 16)

            def store(t):
                sp.wait_ge(y_ready, t + 1)
                sp.dma_start(rows(g.x1, t), y[:, t % 2, :]).then_inc(y_stored[t % 2], 16)

            load(0)
            load(1)
            sp.dma_start(gain[:, :], g.final_gain).then_inc(gain_loaded, 16)
            for t in range(2, NT):
                load(t)
                store(t - 2)
            store(NT - 2)
            store(NT - 1)
            for i in range(2):
                sp.wait_ge(y_stored[i], 16 * (NT // 2))

        @block.gpsimd
        def _(pool):
            for t in range(NT):
                if t >= 2:
                    pool.wait_ge(op.half_turned, 2 * (t - 1))
                pool.wait_ge(gate_loaded[t % 2], 16 * (t // 2 + 1))
                nc.gpsimd.tensor_tensor(mixed[:, t % 2, 0:512], g.qkv_a[:, t, 0:512], gate[:, t % 2, 0:512],
                                        ALU.mult).then_inc(mixed_a_ready, 1)
                pool.wait_ge(b_loaded[t % 2], 16 * (t // 2 + 1))
                nc.gpsimd.tensor_tensor(mixed[:, t % 2, 512:D], out_b[:, t % 2, :], gate[:, t % 2, 512:D],
                                        ALU.mult).then_inc(mixed_b_ready, 1)

        @block.tensor
        def _(pe):
            op.tensor(pe, 5)

        @block.scalar
        def _(act):
            def norm(t):
                act.wait_ge(op.job_emptied, 2 * t + 2)
                nc.scalar.activation(junk[:, :], y[:, t % 2, :], ACT.Square,
                                     accum_out=stat[:, 0, t:t + 1]).then_inc(squares_summed, 1)
                act.wait_ge(var_ready, t + 1)
                nc.scalar.activation(stat[:, 2, t:t + 1], stat[:, 1, t:t + 1], ACT.Sqrt).then_inc(std_ready, 1)

            op.split_hi(act, 0)
            for t in range(NT):
                if t + 1 < NT:
                    op.split_hi(act, t + 1)
                norm(t)

        @block.vector
        def _(dve):
            def norm(t):
                dve.wait_ge(squares_summed, t + 1)
                nc.vector.tensor_scalar(stat[:, 1, t:t + 1], stat[:, 0, t:t + 1], 1.0 / D, EPS,
                                        ALU.mult, ALU.add).then_inc(var_ready, 1)
                dve.wait_ge(std_ready, t + 1)
                nc.vector.reciprocal(stat[:, 3, t:t + 1], stat[:, 2, t:t + 1]).then_inc(rstd_ready, 1)
                dve.wait_ge(rstd_ready, t + 1)
                if t == 0:
                    dve.wait_ge(gain_loaded, 16)
                yt = y[:, t % 2, :]
                nc.vector.scalar_tensor_tensor(yt, yt, stat[:, 3, t:t + 1], gain[:, :],
                                               ALU.mult, ALU.mult).then_inc(y_ready, 1)

            op.split_lo(dve, 0)
            for t in range(NT):
                if t + 1 < NT:
                    op.split_lo(dve, t + 1)
                dve.wait_ge(x_loaded[t % 2], 16 * (t // 2 + 1))
                if t >= 2:
                    dve.wait_ge(y_stored[t % 2], 16 * (t // 2))
                op.add_residual(dve, t, y[:, t % 2, :], x[:, t % 2, :])
                norm(t)


class DilatedTable:

    LINE = 384

    def __init__(self, k, nc, lines_dram, onehot_d, rel_d, ps, onehot_at, lines_at):
        self.nc, self.lines_dram, self.onehot_d, self.rel_d, self.ps = nc, lines_dram, onehot_d, rel_d, ps
        self.onehot = self.piece(onehot_at, 33)
        self.lines = self.piece(lines_at, ATT_HEADS)
        self.rel = k.sb("di_rel", [33, ATT_HEADS])
        self.loaded = k.sem("di_loaded")
        self.line_ready = k.sem("di_line_ready")
        self.line_copied = k.sem("di_line_copied")
        self.stored = k.sem("di_stored")

    def piece(self, t, partitions):
        return t[0:partitions, :, :].rearrange("p a b -> p (a b)")[:, 0:3 * self.LINE].rearrange("p (n u) -> p n u", n=3)

    def load(self, sp):
        sp.dma_start(self.onehot[:, :, :], self.onehot_d).then_inc(self.loaded, 16)
        sp.dma_start(self.rel[:, :], self.rel_d).then_inc(self.loaded, 16)

    def store(self, sp):
        sp.wait_ge(self.line_copied, 3)
        for p in range(3):
            dst = self.lines_dram[:, p * ATT_HEADS:(p + 1) * ATT_HEADS, :].rearrange("q h u -> h q u")
            sp.dma_start(dst, self.lines[:, p, :].unsqueeze(1).to_broadcast([ATT_HEADS, P, self.LINE])).then_inc(self.stored, 16)

    def tensor(self, pe):
        pe.wait_ge(self.loaded, 32)
        for p in range(3):
            if p >= 2:
                pe.wait_ge(self.line_copied, p - 1)
            self.nc.tensor.matmul(self.ps[0:ATT_HEADS, 6 + p % 2, 0:self.LINE], self.rel[:, :],
                                  self.onehot[:, p, :], start=True, stop=True).then_inc(self.line_ready, 1)

    def vector(self, dve):
        for p in range(3):
            dve.wait_ge(self.line_ready, p + 1)
            self.nc.vector.tensor_copy(self.lines[:, p, :],
                                       self.ps[0:ATT_HEADS, 6 + p % 2, 0:self.LINE]).then_inc(self.line_copied, 1)


def stage_project_2(nc, g, hT_hi, hT_lo):
    with ExitStack() as ctx:
        k = Kit(nc, ctx)
        ps = k.psum("p2_ps")
        att_tok = g.qkT[:, :, :]
        conv_in = k.sb("conv_in", [P, 2, SEQ + 3])
        conv_y = k.sb("conv_y", [P, 2, SEQ])
        conv_w = k.sb("p2_conv_w", [P, 12, 4])
        gain = k.sb("p2_att_gain", [P, 2, HD])
        stat = k.sb("att_stat", [P, 2, NT * 16])
        nstat = k.sb("l2_stat", [P, 2, 64])
        consts_loaded = k.sem("p2_consts_loaded")
        var_ready = k.sem("att_var_ready")
        std_ready = k.sem("att_std_ready")
        att_normed = k.sem("att_normed")
        att_turned = k.sem("att_turned")
        att_placed = k.sem("att_placed")
        dve_step = k.sem("p2_dve_step")
        pads_zeroed = k.sem("pads_zeroed")
        conv_done = k.sem("conv_done")
        silu_done = k.sem("silu_done")
        squared = k.sem("l2_squared")
        l2_summed = k.sem("l2_summed")
        l2_var_ready = k.sem("l2_var_ready")
        l2_std_ready = k.sem("l2_std_ready")

        slots = [8, 9, 10, 11, 0, 1, 2, 3, 4, 5, 6, 7]
        att = [Chunk(AQ2 + c * CW, CW, "act", dst=lambda t, c=c: att_tok[:, t, c * CW:(c + 1) * CW]) for c in range(4)]
        spills = [Chunk(AV2 + c * CW, CW, "act", spill=g.v_att, at=c * CW) for c in range(2)]
        spills += [Chunk(AG2 + c * CW, CW, "act", spill=g.gate2, at=c * CW, silu=True) for c in range(2)]
        zs = [Chunk(Z2, CW, "act", spill=g.z, silu=True),
              Chunk(Z2 + CW, CW, "act", spill=g.z, at=CW, silu=True, more=8, more_dst=lambda t: g.ba[:, t, :])]

        def conv_chunk(i):
            def before(act, j):
                n = 2 * i + j // 2
                if j % 2 == 0 and n >= 2:
                    act.wait_ge(conv_done, n - 1)
                if n < 2 and j == 0:
                    act.wait_ge(pads_zeroed, 1)

            def dst(j):
                n, half = 2 * i + j // 2, j % 2
                return conv_in[:, n % 2, 3 + half * 512:3 + half * 512 + 512]

            col = slots[2 * i] * P
            return Chunk(col, CW, "act", chan=True, dst=dst, before=before)

        conv = [conv_chunk(i) for i in range(6)]
        chunks = att + spills + conv + zs
        first_conv = len(att + spills)
        TURN_AT = 7
        norm = Norm(nc, k, "n2_", g.x1, g.gain2, g.ident, hT_hi, hT_lo, ps, [g.vT[:, i, :] for i in range(4)],
                    [conv_y[:, i, :] for i in range(2)], conv_in[:, 0, 3:3 + SEQ])
        pr = Projection(nc, k, "p2_", g.w_in2, chunks, hT_hi, hT_lo, ps, norm, more=8)
        lines = DilatedTable(k, nc, g.lines, g.di_onehot, g.rel, ps, g.att_qT, g.att_kT)
        block = ctx.enter_context(nc.Block())

        @block.sync
        def _(sp):
            pr.first_sync(sp)
            lines.load(sp)
            sp.dma_start(conv_w[:, :, :], g.conv_w).then_inc(consts_loaded, 16)
            sp.dma_start(gain[:, :, :], g.att_gain).then_inc(consts_loaded, 16)
            pr.sync(sp, {3: lines.store})
            sp.wait_ge(lines.stored, 48)

        @block.gpsimd
        def _(pool):
            nc.gpsimd.memset(conv_in[:, :, 0:3], 0.0).then_inc(pads_zeroed, 1)
            pr.gpsimd(pool)

        @block.tensor
        def _(pe):
            def l2_sums(s, tiles):
                pe.wait_ge(squared, s + 1)
                if s == 0:
                    pe.wait_ge(att_placed, 2 * NT)
                for t in tiles:
                    last = nc.tensor.matmul(ps[:, 7, s * NT + t:s * NT + t + 1], conv_y[:, s % 2, t * P:(t + 1) * P],
                                            g.ones[:, 0:1], start=True, stop=True)
                if tiles[-1] == NT - 1:
                    last.then_inc(l2_summed, 1)

            pr.first_tensor(pe)
            for c in range(2, len(chunks)):
                for j in range(chunks[c].jobs):
                    pr.multiply(pe, c, j)
                    s = 2 * (c - first_conv - 4)
                    if 0 <= s < 8 and j < 3:
                        l2_sums(s + (j + 1) // 2, (range(4, NT), range(0, 4))[j % 2])
                if c == 2:
                    lines.tensor(pe)
                if c == TURN_AT:
                    for n in range(2 * NT):
                        t, which = n // 2, n % 2
                        pe.wait_ge(att_normed, t + 1)
                        if n >= 2:
                            pe.wait_ge(att_placed, n - 1)
                        for j in range(4):
                            c0 = which * 512 + j * P
                            last = nc.tensor.transpose(ps[:, 6 + n % 2, j * P:(j + 1) * P],
                                                       att_tok[:, t, c0:c0 + P], g.ident[:, :])
                        last.then_inc(att_turned, 1)
                if 3 <= c - first_conv <= 6:
                    l2_sums(2 * (c - first_conv - 3), range(0, 4))

        @block.scalar
        def _(act):
            def silu(n):
                act.wait_ge(conv_done, n + 1)
                if n == 4:
                    act.wait_ge(att_turned, 2 * NT)
                dst = g.qkT[:, slots[n], :] if n >= 4 else g.vT[:, n, :]
                nc.scalar.activation(dst, conv_y[:, n % 2, :], ACT.Silu).then_inc(silu_done, 1)
                if n >= 4:
                    act.wait_ge(silu_done, n + 1)
                    nc.scalar.activation(conv_y[:, n % 2, :], dst, ACT.Square).then_inc(squared, 1)

            pr.first_scalar(act)
            for c in range(2, len(chunks)):
                pr.split_hi(act, c + 1)
                if 1 <= c - first_conv <= 6:
                    silu(2 * (c - first_conv) - 2)
                    silu(2 * (c - first_conv) - 1)
                pr.empty_chunk(act, "act", c)
                if c == 5:
                    act.wait_ge(var_ready, 1)
                    nc.scalar.activation(stat[:, 1, :], stat[:, 0, :], ACT.Sqrt).then_inc(std_ready, 1)
            act.wait_ge(l2_var_ready, 1)
            nc.scalar.activation(nstat[:, 1, :], nstat[:, 0, :], ACT.Sqrt).then_inc(l2_std_ready, 1)

        @block.vector
        def _(dve):
            steps = 0

            def step(op):
                nonlocal steps
                steps += 1
                op.then_inc(dve_step, 1)
                dve.wait_ge(dve_step, steps)

            pr.first_vector(dve)
            lines.vector(dve)
            for t in range(NT):
                dve.wait_ge(pr.emptied["act"], 3 * NT + t + 1)
                x = att_tok[:, t, :]
                step(nc.vector.tensor_tensor(conv_y[:, 0, :], x, x, ALU.mult))
                step(nc.vector.tensor_reduce(stat[:, 0, t * 16:(t + 1) * 16],
                                             conv_y[:, 0, :].rearrange("p (h d) -> p h d", d=HD), AX.X, ALU.add))
            nc.vector.tensor_scalar(stat[:, 0, :], stat[:, 0, :], 1.0 / HD, EPS, ALU.mult, ALU.add).then_inc(var_ready, 1)
            dve.wait_ge(std_ready, 1)
            step(nc.vector.reciprocal(stat[:, 1, :], stat[:, 1, :]))
            q_rstd = stat[:, 1, :].rearrange("p (t h) -> p t h", h=16)[:, :, 0:ATT_HEADS]
            step(nc.vector.tensor_scalar(q_rstd, q_rstd, HD ** -0.5, None, ALU.mult))
            dve.wait_ge(consts_loaded, 32)
            for t in range(NT):
                x = att_tok[:, t, :].rearrange("p (h d) -> p h d", d=HD)
                step(nc.vector.tensor_tensor(x, x, stat[:, 1, t * 16:(t + 1) * 16].unsqueeze(2).to_broadcast([P, 16, HD]),
                                             ALU.mult))
                x4 = att_tok[:, t, :].rearrange("p (w h d) -> p w h d", w=2, d=HD)
                nc.vector.tensor_tensor(x4, x4, gain[:, :, :].unsqueeze(2).to_broadcast([P, 2, 8, HD]),
                                        ALU.mult).then_inc(att_normed, 1)
            dve.wait_ge(lines.stored, 48)
            for n in range(2 * NT):
                t, which = n // 2, n % 2
                dve.wait_ge(att_turned, n + 1)
                dst = (g.att_qT, g.att_kT)[which]
                nc.vector.tensor_copy(dst[:, :, t * P:(t + 1) * P],
                                      ps[:, 6 + n % 2, :].rearrange("p (k c) -> p k c", k=4)).then_inc(att_placed, 1)
            for n in range(12):
                s = slots[n]
                dve.wait_ge(pr.emptied["act"], pr.emptied_before(pr.first_job(first_conv) + 2 * n + 2, "act"))
                if 2 <= n < 6:
                    dve.wait_ge(silu_done, n - 1)
                elif n >= 6:
                    dve.wait_ge(l2_summed, n - 5)
                y = conv_y[:, n % 2, :]
                step(nc.vector.tensor_scalar(y, conv_in[:, n % 2, 3:3 + SEQ], conv_w[:, s, 3:4], None, ALU.mult))
                for i in (2, 1, 0):
                    op = nc.vector.scalar_tensor_tensor(y, conv_in[:, n % 2, i:i + SEQ], conv_w[:, s, i:i + 1], y,
                                                        ALU.mult, ALU.add)
                    if i:
                        step(op)
                    else:
                        op.then_inc(conv_done, 1)
            dve.wait_ge(l2_summed, 8)
            nc.vector.tensor_scalar(nstat[:, 0, :], ps[:, 7, 0:64], EPS, None, ALU.add).then_inc(l2_var_ready, 1)
            dve.wait_ge(l2_std_ready, 1)
            step(nc.vector.reciprocal(g.l2[:, :], nstat[:, 1, :]))
            step(nc.vector.tensor_scalar(g.l2[:, 0:32], g.l2[:, 0:32], DK ** -0.5, None, ALU.mult))


def stage_delta(nc, g):
    H4 = DN_HEADS
    with ExitStack() as ctx:
        k = Kit(nc, ctx)
        ps = k.psum("d_ps")
        upper = k.sb("d_upper", [P, P])
        strict = k.sb("d_strict", [P, P])
        levels = k.sb("d_levels", [P, LEVELS, P])
        ab = k.sb("d_ab", [P, 2, H4])
        sc = k.sb("d_sc", [P, 8, NT, H4])
        beta, gg, gc, egc, be = (k.sb(n, [P, NT, H4]) for n in ("d_beta", "d_g", "d_gc", "d_egc", "d_be"))
        dd = k.sb("d_dd", [P, 2, H4, P])
        dec = k.sb("d_dec", [P, 2, H4, P])
        tl = k.sb("d_tl", [P, 12])
        etl = k.sb("d_etl", [P, 3, 12])
        khat = k.sb("d_khat", [P, H4, P])
        khatT = k.sb("d_khatT", [P, H4, P])
        kbe = k.sb("d_kbe", [P, 2, H4, P])
        vb = k.sb("d_vb", [P, 2, H4, P])
        ktail = k.sb("d_ktail", [P, 3, H4, P])
        attnT = k.sb("d_attnT", [P, 3, H4, P])
        A = k.sb("d_A", [P, H4, P])
        Al = k.sb("d_Al", [P, 2, LEVELS, H4, P])
        T = k.sb("d_T", [P, 2, H4, P])
        X = k.sb("d_X", [P, 2, H4, P])
        Z = k.sb("d_Z", [P, H4, P])
        u = k.sb("d_u", [P, 2, H4, P])
        wT = k.sb("d_wT", [P, 2, H4, P])
        S = k.sb("d_S", [P, H4, P])
        Sg = k.sb("d_Sg", [P, H4, P])
        vnew = k.sb("d_vnew", [P, H4, P])
        oq = k.sb("d_oq", [P, H4, P])
        osq = k.sb("d_osq", [P, H4, P])

        def bank(b):
            return ps[:, b, :].rearrange("p (h c) -> p h c", h=H4)

        names = ("consts ab_loaded gate_dve gate_act g_ready gc_ready gates_ready gc_copied "
                 "gcb_ready kt_ready vt_ready diffs_done decays_done dec_masked decT_masked khat_ready khatT_turned "
                 "khatT_ready kbe_ready ktail_ready vb_ready G_ready A_ready attn_ready attnT_ready level_masked "
                 "T0_ready X0_turned X0_ready Z_ready Z_copied dX_ready dT_ready X_ready T_ready u_ready w_ready "
                 "u_copied w_copied wS_ready vnew_ready av_ready dS_ready S_ready Sg_ready oq_ready o_ready osq_ready "
                 "S_zeroed o_summed strict_done be_ready").split()
        s = {n: k.sem("d_" + n) for n in names}
        block = ctx.enter_context(nc.Block())
        N = NT

        def order(i, front, inv, rec):
            f, v, r = i < N, 0 <= i - 1 < N, 0 <= i - 2 < N
            if v:
                inv.z(i - 1, 1)
            if f:
                front.first(i)
            for l in range(1, LEVELS):
                if v and l >= 2:
                    inv.z(i - 1, l)
                if f and l >= 2:
                    (front.khat_turn, front.gram, front.attn, front.x0)[l - 2](i)
                if v:
                    inv.update(i - 1, l)
                if f and l == 1:
                    front.khat(i)
                if r and l <= 4:
                    (rec.read, rec.write)[(l - 1) % 2](i - 2, (l - 1) // 2)
            if v:
                inv.apply(i - 1)
            if r:
                rec.finish(i - 2)

        @block.sync
        def _(sp):
            sp.dma_start(ab[:, :, :], g.a_dt).then_inc(s["ab_loaded"], 16)
            sp.dma_start(upper[:, :], g.d_upper).then_inc(s["consts"], 16)
            sp.dma_start(strict[:, :], g.d_strict).then_inc(s["consts"], 16)
            sp.dma_start(levels[:, :, :], g.d_levels).then_inc(s["consts"], 16)

        @block.tensor
        def _(pe):
            class front:
                @staticmethod
                def first(t):
                    if t >= 1:
                        pe.wait_ge(s["attnT_ready"], t)
                        pe.wait_ge(s["X0_ready"], t)
                        pe.wait_ge(s["A_ready"], t)
                    for h in range(H4):
                        last = nc.tensor.matmul(bank(0)[:, h, :], gg[:, t, h:h + 1].to_broadcast([P, P]), upper[:, :],
                                                start=True, stop=True)
                    last.then_inc(s["gcb_ready"], 1)
                    for h in range(H4):
                        last = nc.tensor.transpose(bank(1)[:, h, :], g.qkT[:, 4 + h, t * P:(t + 1) * P], g.ident[:, :])
                    last.then_inc(s["kt_ready"], 1)
                    for h in range(H4):
                        last = nc.tensor.transpose(bank(2)[:, h, :], g.vT[:, h, t * P:(t + 1) * P], g.ident[:, :])
                    last.then_inc(s["vt_ready"], 1)

                @staticmethod
                def khat(t):
                    pass

                @staticmethod
                def khat_turn(t):
                    pe.wait_ge(s["khat_ready"], t + 1)
                    for h in range(H4):
                        last = nc.tensor.transpose(bank(1)[:, h, :], khat[:, h, :], g.ident[:, :])
                    last.then_inc(s["khatT_turned"], 1)

                @staticmethod
                def gram(t):
                    pe.wait_ge(s["khatT_ready"], t + 1)
                    pe.wait_ge(s["vb_ready"], t + 1)
                    for h in range(H4):
                        last = nc.tensor.matmul(bank(2)[:, h, :], khatT[:, h, :], khatT[:, h, :], start=True, stop=True)
                    last.then_inc(s["G_ready"], 1)

                @staticmethod
                def attn(t):
                    pe.wait_ge(s["diffs_done"], t + 1)
                    for h in range(H4):
                        last = nc.tensor.matmul(bank(0)[:, h, :], khatT[:, h, :], g.qkT[:, h, t * P:(t + 1) * P],
                                                start=True, stop=True)
                    last.then_inc(s["attn_ready"], 1)

                @staticmethod
                def x0(t):
                    pe.wait_ge(s["T0_ready"], t + 1)
                    for h in range(H4):
                        last = nc.tensor.transpose(bank(1)[:, h, :], T[:, t % 2, h, :], g.ident[:, :])
                    last.then_inc(s["X0_turned"], 1)

            class inv:
                @staticmethod
                def z(t, l):
                    m = (LEVELS - 1) * t + l - 1
                    pe.wait_ge(s["X0_ready"], t + 1)
                    if m >= 1:
                        pe.wait_ge(s["X_ready"], m)
                        pe.wait_ge(s["T_ready"], (LEVELS - 2) * t + l - 1)
                    if l == 1 and t >= 1:
                        pe.wait_ge(s["u_copied"], t)
                    pe.wait_ge(s["level_masked"], LEVELS * t + l + 1)
                    for h in range(H4):
                        last = nc.tensor.matmul(bank(3)[:, h, :], Al[:, t % 2, l, h, :], X[:, t % 2, h, :],
                                                start=True, stop=True)
                    last.then_inc(s["Z_ready"], 1)

                @staticmethod
                def update(t, l):
                    m = (LEVELS - 1) * t + l - 1
                    pe.wait_ge(s["Z_copied"], m + 1)
                    if l == 1 and t >= 1:
                        pe.wait_ge(s["w_copied"], t)
                    for h in range(H4):
                        last = nc.tensor.matmul(bank(4)[:, h, :], T[:, t % 2, h, :], Z[:, h, :], start=True, stop=True)
                    last.then_inc(s["dX_ready"], 1)
                    if l < LEVELS - 1:
                        for h in range(H4):
                            last = nc.tensor.matmul(bank(3)[:, h, :], Z[:, h, :], T[:, t % 2, h, :], start=True, stop=True)
                        last.then_inc(s["dT_ready"], 1)

                @staticmethod
                def apply(t):
                    pe.wait_ge(s["X_ready"], (LEVELS - 1) * (t + 1))
                    pe.wait_ge(s["vb_ready"], t + 1)
                    pe.wait_ge(s["kbe_ready"], t + 1)
                    for h in range(H4):
                        last = nc.tensor.matmul(bank(3)[:, h, :], X[:, t % 2, h, :], vb[:, t % 2, h, :], start=True, stop=True)
                    last.then_inc(s["u_ready"], 1)
                    for h in range(H4):
                        last = nc.tensor.matmul(bank(4)[:, h, :], kbe[:, t % 2, h, :], X[:, t % 2, h, :], start=True, stop=True)
                    last.then_inc(s["w_ready"], 1)

            class rec:
                @staticmethod
                def read(t, c):
                    n = 2 * t + c
                    r = slice(c * CHUNK, (c + 1) * CHUNK)
                    pe.wait_ge(s["w_copied"], t + 1)
                    if n >= 1:
                        pe.wait_ge(s["S_ready"], n)
                    if c == 0 and t >= 1:
                        pe.wait_ge(s["oq_ready"], t)
                    for h in range(H4):
                        last = nc.tensor.matmul(bank(6)[r, h, :], wT[:, t % 2, h, r], S[:, h, :], start=True, stop=True)
                    last.then_inc(s["wS_ready"], 1)
                    for h in range(H4):
                        last = nc.tensor.matmul(bank(7)[r, h, :], g.qkT[:, h, t * P + c * CHUNK:t * P + (c + 1) * CHUNK],
                                                S[:, h, :], start=True, stop=True)

                @staticmethod
                def write(t, c):
                    n = 2 * t + c
                    r = slice(c * CHUNK, (c + 1) * CHUNK)
                    pe.wait_ge(s["vnew_ready"], n + 1)
                    if c == 0 and t >= 1:
                        pe.wait_ge(s["o_ready"], t)
                    for h in range(H4):
                        last = nc.tensor.matmul(bank(6)[:, h, :], ktail[r, t % 3, h, :], vnew[r, h, :], start=True, stop=True)
                    last.then_inc(s["dS_ready"], 1)
                    for h in range(H4):
                        last = nc.tensor.matmul(bank(5)[r, h, :], attnT[r, t % 3, h, r], vnew[r, h, :], start=True, stop=True)
                    last.then_inc(s["av_ready"], 1)

                @staticmethod
                def finish(t):
                    pass

            pe.wait_ge(s["consts"], 48)
            pe.wait_ge(s["g_ready"], 1)
            nc.tensor.matmul(ps[:, 0, 0:NT * H4], upper[:, :], gg[:, :, :].rearrange("p t h -> p (t h)"),
                             start=True, stop=True).then_inc(s["gc_ready"], 1)
            pe.wait_ge(s["gc_copied"], 1)
            pe.wait_ge(s["S_zeroed"], 1)
            for i in range(N + 2):
                order(i, front, inv, rec)

        @block.vector
        def _(dve):
            def chained(op, n=[0]):
                n[0] += 1
                op.then_inc(s["gate_dve"], 1)
                dve.wait_ge(s["gate_dve"], n[0])

            class front:
                @staticmethod
                def first(t):
                    dve.wait_ge(s["gcb_ready"], t + 1)
                    if t >= 1:
                        dve.wait_ge(s["decays_done"], t)
                    for h in range(H4):
                        nc.vector.tensor_scalar(dd[:, 0, h, :], bank(0)[:, h, :], gc[:, t, h:h + 1], 0.0,
                                                ALU.subtract, ALU.max)
                        nc.vector.tensor_scalar(dd[:, 1, h, :], bank(0)[:, h, :], gc[:, t, h:h + 1], 0.0,
                                                ALU.subtract, ALU.min)
                    for c in range(2):
                        r = slice(c * CHUNK, (c + 1) * CHUNK)
                        nc.vector.tensor_tensor(tl[r, 0:H4], bank(0)[r, :, (c + 1) * CHUNK - 1], gc[r, t, :], ALU.subtract)
                    ends = bank(0).rearrange("p h (c j) -> p h c j", c=2)[:, :, :, CHUNK - 1]
                    nc.vector.tensor_copy(tl[:, 4:12].rearrange("p (h c) -> p h c", c=2), ends).then_inc(s["diffs_done"], 1)

                @staticmethod
                def khat(t):
                    dve.wait_ge(s["kt_ready"], t + 1)
                    if t >= 1:
                        dve.wait_ge(s["khatT_turned"], t)
                        dve.wait_ge(s["kbe_ready"], t)
                        dve.wait_ge(s["ktail_ready"], t)
                    rk = g.l2[:, 32:64].rearrange("p (h t) -> p t h", t=NT)[:, t, :]
                    nc.vector.tensor_tensor(khat[:, :, :], bank(1), rk.unsqueeze(2).to_broadcast([P, H4, P]),
                                            ALU.mult).then_inc(s["khat_ready"], 1)

                @staticmethod
                def khat_turn(t):
                    dve.wait_ge(s["vt_ready"], t + 1)
                    if t >= 2:
                        dve.wait_ge(s["u_ready"], t - 1)
                    nc.vector.tensor_tensor(vb[:, t % 2, :, :], bank(2), beta[:, t, :].unsqueeze(2).to_broadcast([P, H4, P]),
                                            ALU.mult).then_inc(s["vb_ready"], 1)

                @staticmethod
                def gram(t):
                    dve.wait_ge(s["G_ready"], t + 1)
                    dve.wait_ge(s["dec_masked"], t + 1)
                    if t >= 1:
                        dve.wait_ge(s["level_masked"], LEVELS * t)
                    nc.vector.tensor_tensor(A[:, :, :], bank(2), dec[:, 0, :, :], ALU.mult).then_inc(s["A_ready"], 1)

                @staticmethod
                def attn(t):
                    dve.wait_ge(s["attn_ready"], t + 1)
                    dve.wait_ge(s["decT_masked"], t + 1)
                    if t >= 3:
                        dve.wait_ge(s["av_ready"], 2 * (t - 2))
                    nc.vector.tensor_tensor(attnT[:, t % 3, :, :], bank(0), dec[:, 1, :, :], ALU.mult).then_inc(s["attnT_ready"], 1)
                    dve.wait_ge(s["level_masked"], LEVELS * t + 1)
                    nc.vector.tensor_tensor(T[:, t % 2, :, :], g.ident[:, :].unsqueeze(1).to_broadcast([P, H4, P]),
                                            Al[:, t % 2, 0, :, :], ALU.subtract).then_inc(s["T0_ready"], 1)

                @staticmethod
                def x0(t):
                    pass

            class inv:
                @staticmethod
                def z(t, l):
                    pass

                @staticmethod
                def update(t, l):
                    m = (LEVELS - 1) * t + l - 1
                    dve.wait_ge(s["dX_ready"], m + 1)
                    nc.vector.tensor_tensor(X[:, t % 2, :, :], X[:, t % 2, :, :], bank(4), ALU.subtract).then_inc(s["X_ready"], 1)
                    if l < LEVELS - 1:
                        dve.wait_ge(s["dT_ready"], (LEVELS - 2) * t + l)
                        nc.vector.tensor_tensor(T[:, t % 2, :, :], T[:, t % 2, :, :], bank(3), ALU.subtract).then_inc(s["T_ready"], 1)

                @staticmethod
                def apply(t):
                    pass

            class rec:
                @staticmethod
                def read(t, c):
                    n = 2 * t + c
                    r = slice(c * CHUNK, (c + 1) * CHUNK)
                    dve.wait_ge(s["wS_ready"], n + 1)
                    dve.wait_ge(s["u_copied"], t + 1)
                    if n >= 2:
                        dve.wait_ge(s["av_ready"], n - 1)
                    nc.vector.tensor_tensor(vnew[r, :, :], u[r, t % 2, :, :], bank(6)[r, :, :], ALU.subtract).then_inc(s["vnew_ready"], 1)

                @staticmethod
                def write(t, c):
                    n = 2 * t + c
                    dve.wait_ge(s["dS_ready"], n + 1)
                    dve.wait_ge(s["Sg_ready"], n + 1)
                    nc.vector.tensor_tensor(S[:, :, :], Sg[:, :, :], bank(6), ALU.add).then_inc(s["S_ready"], 1)

                @staticmethod
                def finish(t):
                    dve.wait_ge(s["av_ready"], 2 * t + 2)
                    if t >= 1:
                        dve.wait_ge(s["o_ready"], t)
                    nc.vector.tensor_tensor(oq[:, :, :], bank(7), egc[:, t, :].unsqueeze(2).to_broadcast([P, H4, P]),
                                            ALU.mult).then_inc(s["oq_ready"], 1)
                    dve.wait_ge(s["oq_ready"], t + 1)
                    o = g.vT[:, :, t * P:(t + 1) * P]
                    nc.vector.tensor_tensor(o, oq[:, :, :], bank(5), ALU.add).then_inc(s["o_ready"], 1)
                    if t >= 1:
                        dve.wait_ge(s["osq_ready"], t)
                        nc.vector.tensor_reduce(g.o_ss[:, t - 1, :], osq[:, :, :], AX.X, ALU.add).then_inc(s["o_summed"], 1)

            nc.vector.memset(S[:, :, :], 0.0).then_inc(s["S_zeroed"], 1)
            a_in = g.ba[:, :, H4:2 * H4]
            dve.wait_ge(s["gate_act"], 2)
            chained(nc.vector.tensor_scalar(sc[:, 1], sc[:, 0], 1.0, None, ALU.add))
            chained(nc.vector.reciprocal(beta[:, :, :], sc[:, 1]))
            dve.wait_ge(s["ab_loaded"], 16)
            chained(nc.vector.tensor_tensor(sc[:, 2], a_in, ab[:, 1, :].unsqueeze(1).to_broadcast([P, NT, H4]), ALU.add))
            chained(nc.vector.tensor_scalar(sc[:, 3], sc[:, 2], -1.0, None, ALU.mult))
            chained(nc.vector.tensor_tensor(sc[:, 3], sc[:, 2], sc[:, 3], ALU.min))
            nc.vector.tensor_scalar(sc[:, 2], sc[:, 2], 0.0, None, ALU.max).then_inc(s["gates_ready"], 1)
            dve.wait_ge(s["gate_act"], 3)
            nc.vector.tensor_scalar(sc[:, 4], sc[:, 4], 1.0, None, ALU.add).then_inc(s["gates_ready"], 1)
            dve.wait_ge(s["gate_act"], 4)
            chained(nc.vector.tensor_tensor(sc[:, 2], sc[:, 2], sc[:, 5], ALU.add))
            chained(nc.vector.tensor_tensor(sc[:, 2], sc[:, 2], sc[:, 6, 0, :].unsqueeze(1).to_broadcast([P, NT, H4]), ALU.mult))
            nc.vector.tensor_scalar(gg[:, :, :], sc[:, 2], -1.0, None, ALU.mult).then_inc(s["g_ready"], 1)
            dve.wait_ge(s["gc_ready"], 1)
            nc.vector.tensor_copy(gc[:, :, :], ps[:, 0, 0:NT * H4].rearrange("p (t h) -> p t h", h=H4)).then_inc(s["gc_copied"], 1)
            dve.wait_ge(s["gc_copied"], 1)
            dve.wait_ge(s["gate_act"], 5)
            nc.vector.tensor_tensor(be[:, :, :], beta[:, :, :], egc[:, :, :], ALU.mult).then_inc(s["be_ready"], 1)
            dve.wait_ge(s["be_ready"], 1)
            for i in range(N + 2):
                order(i, front, inv, rec)
            dve.wait_ge(s["osq_ready"], N)
            nc.vector.tensor_reduce(g.o_ss[:, N - 1, :], osq[:, :, :], AX.X, ALU.add).then_inc(s["o_summed"], 1)
            dve.wait_ge(s["o_summed"], N)

        @block.scalar
        def _(act):
            class front:
                @staticmethod
                def first(t):
                    act.wait_ge(s["diffs_done"], t + 1)
                    if t >= 1:
                        act.wait_ge(s["A_ready"], t)
                        act.wait_ge(s["attnT_ready"], t)
                        act.wait_ge(s["dec_masked"], t)
                        act.wait_ge(s["decT_masked"], t)
                    if t >= 3:
                        act.wait_ge(s["Sg_ready"], 2 * (t - 2))
                    nc.scalar.activation(dec[:, 0, :, :], dd[:, 0, :, :], ACT.Exp, scale=-1.0)
                    nc.scalar.activation(dec[:, 1, :, :], dd[:, 1, :, :], ACT.Exp)
                    nc.scalar.activation(etl[:, t % 3, :], tl[:, :], ACT.Exp).then_inc(s["decays_done"], 1)

                @staticmethod
                def khat(t):
                    pass

                @staticmethod
                def khat_turn(t):
                    act.wait_ge(s["khatT_turned"], t + 1)
                    if t >= 1:
                        act.wait_ge(s["attn_ready"], t)
                    nc.scalar.copy(khatT[:, :, :], bank(1)).then_inc(s["khatT_ready"], 1)

                @staticmethod
                def gram(t):
                    pass

                @staticmethod
                def attn(t):
                    pass

                @staticmethod
                def x0(t):
                    act.wait_ge(s["X0_turned"], t + 1)
                    if t >= 2:
                        act.wait_ge(s["w_ready"], t - 1)
                    nc.scalar.copy(X[:, t % 2, :, :], bank(1)).then_inc(s["X0_ready"], 1)

            class inv:
                @staticmethod
                def z(t, l):
                    m = (LEVELS - 1) * t + l - 1
                    act.wait_ge(s["Z_ready"], m + 1)
                    if m >= 1:
                        act.wait_ge(s["dX_ready"], m)
                        act.wait_ge(s["dT_ready"], (LEVELS - 2) * t + l - 1)
                    nc.scalar.copy(Z[:, :, :], bank(3)).then_inc(s["Z_copied"], 1)

                @staticmethod
                def update(t, l):
                    pass

                @staticmethod
                def apply(t):
                    if t >= 2:
                        act.wait_ge(s["vnew_ready"], 2 * (t - 1))
                    act.wait_ge(s["u_ready"], t + 1)
                    nc.scalar.copy(u[:, t % 2, :, :], bank(3)).then_inc(s["u_copied"], 1)
                    if t >= 2:
                        act.wait_ge(s["wS_ready"], 2 * (t - 1))
                    act.wait_ge(s["w_ready"], t + 1)
                    nc.scalar.copy(wT[:, t % 2, :, :], bank(4)).then_inc(s["w_copied"], 1)

            class rec:
                @staticmethod
                def read(t, c):
                    pass

                @staticmethod
                def finish(t):
                    pass

                @staticmethod
                def write(t, c):
                    pass

            nc.scalar.activation(sc[:, 0], g.ba[:, :, 0:H4], ACT.Exp, scale=-1.0).then_inc(s["gate_act"], 1)
            act.wait_ge(s["ab_loaded"], 16)
            nc.scalar.activation(sc[:, 6, 0, :], ab[:, 0, :], ACT.Exp).then_inc(s["gate_act"], 1)
            act.wait_ge(s["gates_ready"], 1)
            nc.scalar.activation(sc[:, 4], sc[:, 3], ACT.Exp).then_inc(s["gate_act"], 1)
            act.wait_ge(s["gates_ready"], 2)
            nc.scalar.activation(sc[:, 5], sc[:, 4], ACT.Ln).then_inc(s["gate_act"], 1)
            act.wait_ge(s["gc_copied"], 1)
            nc.scalar.activation(egc[:, :, :], gc[:, :, :], ACT.Exp).then_inc(s["gate_act"], 1)
            for i in range(N + 2):
                order(i, front, inv, rec)

        @block.gpsimd
        def _(pool):
            def over_heads(m):
                return m.unsqueeze(1).to_broadcast([P, H4, P])

            def per_row(col):
                return col.unsqueeze(2).to_broadcast([P, H4, P])

            class front:
                @staticmethod
                def first(t):
                    pool.wait_ge(s["decays_done"], t + 1)
                    nc.gpsimd.tensor_tensor(dec[:, 0, :, :], dec[:, 0, :, :], over_heads(strict[:, :]), ALU.mult).then_inc(s["strict_done"], 1)
                    pool.wait_ge(s["strict_done"], t + 1)
                    nc.gpsimd.tensor_tensor(dec[:, 0, :, :], dec[:, 0, :, :], per_row(beta[:, t, :]), ALU.mult).then_inc(s["dec_masked"], 1)
                    nc.gpsimd.tensor_tensor(dec[:, 1, :, :], dec[:, 1, :, :], over_heads(upper[:, :]), ALU.mult).then_inc(s["decT_masked"], 1)

                @staticmethod
                def khat(t):
                    pass

                @staticmethod
                def khat_turn(t):
                    pool.wait_ge(s["khat_ready"], t + 1)
                    if t >= 2:
                        pool.wait_ge(s["w_ready"], t - 1)
                    nc.gpsimd.tensor_tensor(kbe[:, t % 2, :, :], khat[:, :, :], per_row(be[:, t, :]), ALU.mult).then_inc(s["kbe_ready"], 1)
                    if t >= 3:
                        pool.wait_ge(s["dS_ready"], 2 * (t - 2))
                    nc.gpsimd.tensor_tensor(ktail[:, t % 3, :, :], khat[:, :, :], per_row(etl[:, t % 3, 0:H4]), ALU.mult).then_inc(s["ktail_ready"], 1)

                @staticmethod
                def gram(t):
                    pool.wait_ge(s["A_ready"], t + 1)
                    if t >= 2:
                        pool.wait_ge(s["Z_ready"], (LEVELS - 1) * (t - 1))
                        pool.wait_ge(s["T0_ready"], t - 1)
                    mask_levels(t, 0, 1)

                @staticmethod
                def attn(t):
                    mask_levels(t, 1, LEVELS)

                @staticmethod
                def x0(t):
                    pass

            def mask_levels(t, first, end):
                for l in range(first, end):
                    nc.gpsimd.tensor_tensor(Al[:, t % 2, l, :, :], A[:, :, :], over_heads(levels[:, l, :]), ALU.mult).then_inc(s["level_masked"], 1)

            class inv:
                @staticmethod
                def z(t, l):
                    pass

                @staticmethod
                def update(t, l):
                    pass

                @staticmethod
                def apply(t):
                    pass

            class rec:
                @staticmethod
                def read(t, c):
                    n = 2 * t + c
                    if n >= 1:
                        pool.wait_ge(s["S_ready"], n)
                    decay = etl[:, t % 3, 4:12].rearrange("p (h c) -> p h c", c=2)[:, :, c]
                    nc.gpsimd.tensor_tensor(Sg[:, :, :], S[:, :, :], per_row(decay), ALU.mult).then_inc(s["Sg_ready"], 1)

                @staticmethod
                def write(t, c):
                    if c == 0 and t >= 1:
                        square(t - 1)

                @staticmethod
                def finish(t):
                    pass

            def square(t):
                pool.wait_ge(s["o_ready"], t + 1)
                if t >= 1:
                    pool.wait_ge(s["o_summed"], t)
                o = g.vT[:, :, t * P:(t + 1) * P]
                nc.gpsimd.tensor_tensor(osq[:, :, :], o, o, ALU.mult).then_inc(s["osq_ready"], 1)

            pool.wait_ge(s["consts"], 48)
            pool.wait_ge(s["be_ready"], 1)
            pool.wait_ge(s["S_zeroed"], 1)
            for i in range(N + 2):
                order(i, front, inv, rec)
            square(N - 1)


def dilated_tile(p, i):
    if p == 0:
        return i * P, 1, i > 0
    if p == 1:
        return i // 2 + 4 * P * (i % 2), 4, i % 2 == 1
    return i, 8, False


def dilated_rows(ap, p):
    if p == 0:
        return ap.rearrange("(i j) c -> j i c", j=P)
    if p == 1:
        return ap.rearrange("(b j r) c -> j r b c", j=P, r=4)
    return ap.rearrange("(j i) c -> j i c", j=P)


def stage_dilated(nc, g, w_hi, w_lo):
    with ExitStack() as ctx:
        k = Kit(nc, ctx)
        ws = WeightSplit(nc, k, "c_w_", g.w_out2, w_hi, w_lo)
        ps = k.psum("c_ps")
        v = k.sb("c_v", [P, 2, NT, 512])
        table = k.sb("c_table", [P, 2, ATT_HEADS, 256])
        prob = k.sb("c_prob", [P, 3, 256])
        prob_t = k.sb("c_prob_t", [P, 3, 256])
        out = k.sb("c_out", [P, NT, 512])
        ml = k.sb("c_ml", [P, 3, NT, 2, ATT_HEADS])
        table_loaded = k.sems("c_table_loaded", 3)
        v_loaded = k.sems("c_v_loaded", 3)
        scores_ready = k.sem("c_scores_ready")
        max_ready = k.sem("c_max_ready")
        prob_ready = k.sem("c_prob_ready")
        turned = k.sem("c_turned")
        pt_by_dve = k.sem("c_pt_by_dve")
        pt_by_act = k.sem("c_pt_by_act")
        values_done = k.sem("c_values_done")
        group_emptied = k.sem("c_group_emptied")
        out_sent = k.sems("c_out_sent", 6)
        ml_sent = k.sem("c_ml_sent")
        units = [(p, h, i) for p in range(3) for h in range(ATT_HEADS) for i in range(NT)]
        n_units = len(units)
        PER_P = ATT_HEADS * NT

        def pt_ready(eng, n):
            if n > 0:
                eng.wait_ge(pt_by_dve, (n + 1) // 2)
            if n > 1:
                eng.wait_ge(pt_by_act, n // 2)

        block = ctx.enter_context(nc.Block())

        @block.sync
        def _(sp):
            def load(p):
                if p >= 2:
                    sp.wait_ge(values_done, PER_P * (p - 1))
                    sp.wait_ge(max_ready, PER_P * (p - 1))
                W = DilatedTable.LINE * 3 * ATT_HEADS
                band = bass.AP(tensor=g.lines.tensor, offset=p * ATT_HEADS * DilatedTable.LINE + P - 1,
                               ap=[[W - 1, P], [DilatedTable.LINE, ATT_HEADS], [1, 256]])
                sp.dma_start(table[:, p % 2, :, :], band).then_inc(table_loaded[p], 16)
                if p == 1:
                    src = dilated_rows(g.v_att, p)
                    for r in range(4):
                        sp.dma_start(v[:, p % 2, 2 * r:2 * r + 2, :], src[:, r, :, :]).then_inc(v_loaded[p], 16)
                else:
                    sp.dma_start(v[:, p % 2, :, :], dilated_rows(g.v_att, p)).then_inc(v_loaded[p], 16)

            def send(p, half):
                sp.wait_ge(group_emptied, ATT_HEADS * p + 4 * (half + 1))
                cols = slice(half * 4 * HD, (half + 1) * 4 * HD)
                dst = dilated_rows(g.o_att[p][:, cols], p)
                if p == 1:
                    for r in range(4):
                        sp.dma_start(dst[:, r, :, :], out[:, 2 * r:2 * r + 2, cols]).then_inc(out_sent[2 * p + half], 16)
                else:
                    sp.dma_start(dst, out[:, :, cols]).then_inc(out_sent[2 * p + half], 16)

            def send_ml(p):
                sp.wait_ge(prob_ready, PER_P * (p + 1))
                dst = dilated_rows(g.ml[p], p)
                if p == 1:
                    for r in range(4):
                        sp.dma_start(dst[:, r, :, :], ml[:, p, 2 * r:2 * r + 2, :, :].rearrange("p i a h -> p i (a h)"))\
                            .then_inc(ml_sent, 16)
                else:
                    sp.dma_start(dst, ml[:, p, :, :, :].rearrange("p i a h -> p i (a h)")).then_inc(ml_sent, 16)

            load(0)
            load(1)
            for kt in range(KT):
                ws.load(sp, kt)
            for p in range(3):
                send(p, 0)
                send(p, 1)
                send_ml(p)
                if p == 0:
                    load(2)
            for p, n in enumerate((1, 4, 1)):
                for half in range(2):
                    sp.wait_ge(out_sent[2 * p + half], 16 * n)
            sp.wait_ge(ml_sent, 16 * 6)

        @block.gpsimd
        def _(pool):
            for kt in range(KT):
                ws.split_hi(pool, nc.gpsimd.tensor_copy, kt)
                ws.split_lo(pool, nc.gpsimd, kt)

        @block.tensor
        def _(pe):
            def scores(u):
                p, h, i = units[u]
                first, stride, before = dilated_tile(p, i)
                if u >= 3:
                    pe.wait_ge(max_ready, u - 2)
                r = slice(HD * (h % 2), HD * (h % 2) + HD)
                q = g.att_qT[r, h // 2, first:first + stride * (P - 1) + 1:stride]
                c0 = 0 if before else P
                k_first = first - stride * P if before else first
                n = 256 - c0
                keys = g.att_kT[r, h // 2, k_first:k_first + stride * (n - 1) + 1:stride]
                nc.tensor.matmul(ps[:, u % 3, c0:256], q, keys, start=True, stop=True).then_inc(scores_ready, 1)

            def turn_probs(u):
                p, h, i = units[u]
                before = dilated_tile(p, i)[2]
                pe.wait_ge(prob_ready, u + 1)
                pt_ready(pe, u - 2)
                for j in range(0 if before else 1, 2):
                    last = nc.tensor.transpose(ps[:, 3 + u % 3, j * P:(j + 1) * P],
                                               prob[:, u % 3, j * P:(j + 1) * P], g.ident[:, :])
                last.then_inc(turned, 1)

            def values(u):
                p, h, i = units[u]
                before = dilated_tile(p, i)[2]
                grp = u // NT
                pt_ready(pe, u + 1)
                if u % PER_P == 0:
                    pe.wait_ge(v_loaded[p], 64 if p == 1 else 16)
                if i == 0 and grp >= 2:
                    pe.wait_ge(group_emptied, grp - 1)
                for j in range(0 if before else 1, 2):
                    last = nc.tensor.matmul(ps[:, 6 + grp % 2, i * HD:(i + 1) * HD], prob_t[:, u % 3, j * P:(j + 1) * P],
                                            v[:, p % 2, i - 1 + j, h * HD:(h + 1) * HD],
                                            start=(j == (0 if before else 1)), stop=(j == 1))
                last.then_inc(values_done, 1)

            for u in range(n_units + 4):
                if u == 2:
                    keep_busy(nc, ps[:, 5, :], g.ident, 6)
                if u < n_units:
                    scores(u)
                if 2 <= u < n_units + 2:
                    turn_probs(u - 2)
                if u >= 4:
                    values(u - 4)

        @block.vector
        def _(dve):
            def bias_and_max(u):
                p, h, i = units[u]
                c0 = 0 if dilated_tile(p, i)[2] else P
                if u % PER_P == 0:
                    dve.wait_ge(table_loaded[p], 16)
                dve.wait_ge(scores_ready, u + 1)
                if u >= 3:
                    dve.wait_ge(turned, u - 2)
                nc.vector.tensor_tensor_reduce(prob[:, u % 3, c0:256], ps[:, u % 3, c0:256], table[:, p % 2, h, c0:256],
                                               -1.0, -NEG, ALU.add, ALU.min,
                                               ml[:, p, i, 0, h:h + 1]).then_inc(max_ready, 1)

            def empty(u):
                c0 = 0 if dilated_tile(units[u][0], units[u][2])[2] else P
                dve.wait_ge(turned, u + 1)
                if u >= 3:
                    dve.wait_ge(values_done, u - 2)
                nc.vector.tensor_copy(prob_t[:, u % 3, c0:256], ps[:, 3 + u % 3, c0:256]).then_inc(pt_by_dve, 1)

            def empty_group(grp):
                p, h, _ = units[grp * NT]
                dve.wait_ge(values_done, NT * (grp + 1))
                if p >= 1 and h % 4 == 0:
                    dve.wait_ge(out_sent[2 * (p - 1) + h // 4], (16, 64)[p - 1])
                nc.vector.tensor_copy(out[:, :, h * HD:(h + 1) * HD],
                                      ps[:, 6 + grp % 2, :].rearrange("p (i d) -> p i d", d=HD)).then_inc(group_emptied, 1)

            for u in range(n_units + 5):
                if u < n_units:
                    bias_and_max(u)
                if 2 <= u < n_units + 2 and u % 2 == 0:
                    empty(u - 2)
                if u >= 12 and (u - 12) % NT == 0:
                    empty_group((u - 12) // NT)

        @block.scalar
        def _(act):
            def exponentials(u):
                p, h, i = units[u]
                c0 = 0 if dilated_tile(p, i)[2] else P
                act.wait_ge(max_ready, u + 1)
                s = prob[:, u % 3, c0:256]
                nc.scalar.activation(s, s, ACT.Exp, bias=ml[:, p, i, 0, h:h + 1], scale=-1.0,
                                     accum_out=ml[:, p, i, 1, h:h + 1]).then_inc(prob_ready, 1)

            def empty(u):
                c0 = 0 if dilated_tile(units[u][0], units[u][2])[2] else P
                act.wait_ge(turned, u + 1)
                if u >= 3:
                    act.wait_ge(values_done, u - 2)
                nc.scalar.copy(prob_t[:, u % 3, c0:256], ps[:, 3 + u % 3, c0:256]).then_inc(pt_by_act, 1)

            for u in range(n_units + 2):
                if u < n_units:
                    exponentials(u)
                if 2 <= u and u % 2 == 1:
                    empty(u - 2)


def stage_out_2(nc, g, w_hi, w_lo):
    with ExitStack() as ctx:
        k = Kit(nc, ctx)
        ps = k.psum("o2_ps")
        gate = k.sb("o2_gate", [P, 2, 512])
        z = k.sb("o2_z", [P, 2, 512])
        o = k.sb("o2_o", [P, 2, 3, 512])
        x = k.sb("o2_x", [P, 2, D])
        y = k.sb("o2_y", [P, 2, D])
        mixed = k.sb("o2_mixed", [P, 2, D])
        norm_w = k.sb("o2_norm_w", [P, DK])
        ml = k.sb("o2_ml", [P, 3, NT, 2, ATT_HEADS])
        wt = k.sb("o2_wt", [P, 3, NT, ATT_HEADS])
        small = k.sb("o2_small", [P, 3, NT, ATT_HEADS])
        fac = k.sb("o2_fac", [P, 4, NT, DN_HEADS])
        ml_loaded = k.sem("o2_ml_loaded")
        norm_loaded = k.sem("o2_norm_loaded")
        o_loaded = k.sems("o2_o_loaded", 2)
        gate_loaded = k.sems("o2_gate_loaded", 2)
        z_loaded = k.sems("o2_z_loaded", 2)
        x_loaded = k.sems("o2_x_loaded", 2)
        step_done = k.sem("o2_step_done")
        exps_ready = k.sem("o2_exps_ready")
        diffs_ready = k.sem("o2_diffs_ready")
        var_ready = k.sem("o2_var_ready")
        std_ready = k.sem("o2_std_ready")
        fac_ready = k.sem("o2_fac_ready")
        dn_step = k.sem("o2_dn_step")
        dn_mixed = k.sem("o2_dn_mixed")
        att_mixed = k.sem("o2_mixed_ready")
        y_stored = g.out_stored
        op = OutProjection(nc, k, "o2_", g, ps, w_hi, w_lo, mixed, (dn_mixed, att_mixed))
        block = ctx.enter_context(nc.Block())

        @block.sync
        def _(sp):
            def load_parts(t):
                if t >= 2:
                    sp.wait_ge(att_mixed, t - 1)
                for p in range(3):
                    sp.dma_start(o[:, t % 2, p, :], rows(g.o_att[p], t)).then_inc(o_loaded[t % 2], 16)
                sp.dma_start(gate[:, t % 2, :], rows(g.gate2, t)).then_inc(gate_loaded[t % 2], 16)
                if t >= 2:
                    sp.wait_ge(dn_mixed, t - 1)
                sp.dma_start(z[:, t % 2, :], rows(g.z, t)).then_inc(z_loaded[t % 2], 16)

            def load_x(t):
                if t >= 2:
                    sp.wait_ge(op.job_emptied, 2 * (t - 1))
                sp.dma_start(x[:, t % 2, :], rows(g.x1, t)).then_inc(x_loaded[t % 2], 16)

            def store(t):
                sp.wait_ge(op.job_emptied, 2 * t + 2)
                sp.dma_start(rows(g.out, t), y[:, t % 2, :]).then_inc(y_stored[t % 2], 16)

            for p in range(3):
                sp.dma_start(ml[:, p, :, :, :].rearrange("p t a h -> p t (a h)"),
                             g.ml[p].rearrange("(t j) c -> j t c", j=P)).then_inc(ml_loaded, 16)
            sp.dma_start(norm_w[:, :], g.dn_norm).then_inc(norm_loaded, 16)
            load_parts(0)
            load_parts(1)
            load_x(0)
            load_x(1)
            load_parts(2)
            for t in range(2, NT):
                if t + 1 < NT:
                    load_parts(t + 1)
                load_x(t)
                store(t - 2)
            store(NT - 2)
            store(NT - 1)
            for i in range(2):
                sp.wait_ge(y_stored[i], 16 * (NT // 2))

        @block.gpsimd
        def _(pool):
            steps = 0

            def step(op_):
                nonlocal steps
                steps += 1
                op_.then_inc(dn_step, 1)
                pool.wait_ge(dn_step, steps)

            pool.wait_ge(fac_ready, 1)
            pool.wait_ge(norm_loaded, 16)
            for t in range(NT):
                m = mixed[:, t % 2, 0:512].rearrange("p (h c) -> p h c", h=DN_HEADS)
                src = g.vT[:, :, t * P:(t + 1) * P]
                if t >= 2:
                    pool.wait_ge(op.half_turned, 2 * (t - 1))
                step(nc.gpsimd.tensor_tensor(m, src, fac[:, 3, t, :].unsqueeze(2).to_broadcast([P, DN_HEADS, DK]), ALU.mult))
                step(nc.gpsimd.tensor_tensor(m, m, norm_w[:, :].unsqueeze(1).to_broadcast([P, DN_HEADS, DK]), ALU.mult))
                pool.wait_ge(z_loaded[t % 2], 16 * (t // 2 + 1))
                nc.gpsimd.tensor_tensor(mixed[:, t % 2, 0:512], mixed[:, t % 2, 0:512], z[:, t % 2, :],
                                        ALU.mult).then_inc(dn_mixed, 1)

        @block.tensor
        def _(pe):
            op.tensor(pe, 10)

        @block.scalar
        def _(act):
            act.wait_ge(var_ready, 1)
            nc.scalar.activation(fac[:, 1], fac[:, 0], ACT.Sqrt).then_inc(std_ready, 1)
            act.wait_ge(diffs_ready, 1)
            nc.scalar.activation(wt[:, :, :, :], wt[:, :, :, :], ACT.Exp).then_inc(exps_ready, 1)
            for t in range(NT):
                op.split_hi(act, t)

        @block.vector
        def _(dve):
            steps = 0

            def step(op_):
                nonlocal steps
                steps += 1
                op_.then_inc(step_done, 1)
                dve.wait_ge(step_done, steps)

            r = g.l2[:, 0:32].rearrange("p (h t) -> p t h", t=NT)
            step(nc.vector.tensor_tensor(fac[:, 2], r, r, ALU.mult))
            step(nc.vector.tensor_tensor(fac[:, 2], fac[:, 2], g.o_ss[:, :, :], ALU.mult))
            nc.vector.tensor_scalar(fac[:, 0], fac[:, 2], 1.0 / DK, EPS, ALU.mult, ALU.add).then_inc(var_ready, 1)
            dve.wait_ge(std_ready, 1)
            step(nc.vector.reciprocal(fac[:, 2], fac[:, 1]))
            nc.vector.tensor_tensor(fac[:, 3], fac[:, 2], r, ALU.mult).then_inc(fac_ready, 1)
            dve.wait_ge(ml_loaded, 48)
            neg = [ml[:, p, :, 0, :] for p in range(3)]
            total = [ml[:, p, :, 1, :] for p in range(3)]
            step(nc.vector.tensor_tensor(small[:, 0], neg[0], neg[1], ALU.min))
            step(nc.vector.tensor_tensor(small[:, 0], small[:, 0], neg[2], ALU.min))
            for p in range(3):
                last = nc.vector.tensor_tensor(wt[:, p], small[:, 0], neg[p], ALU.subtract)
            last.then_inc(diffs_ready, 1)
            dve.wait_ge(exps_ready, 1)
            step(nc.vector.tensor_tensor(small[:, 0], wt[:, 0], total[0], ALU.mult))
            for p in (1, 2):
                step(nc.vector.tensor_tensor(small[:, 1], wt[:, p], total[p], ALU.mult))
                step(nc.vector.tensor_tensor(small[:, 0], small[:, 0], small[:, 1], ALU.add))
            step(nc.vector.reciprocal(small[:, 2], small[:, 0]))
            for p in range(3):
                step(nc.vector.tensor_tensor(wt[:, p], wt[:, p], small[:, 2], ALU.mult))

            def mix(t):
                dve.wait_ge(o_loaded[t % 2], 48 * (t // 2 + 1))
                parts = [o[:, t % 2, p, :].rearrange("p (h d) -> p h d", d=HD) for p in range(3)]
                for p in range(3):
                    last = nc.vector.tensor_tensor(parts[p], parts[p], wt[:, p, t, :].unsqueeze(2).to_broadcast([P, ATT_HEADS, HD]),
                                                   ALU.mult)
                step(last)
                step(nc.vector.tensor_tensor(parts[0], parts[0], parts[1], ALU.add))
                step(nc.vector.tensor_tensor(parts[0], parts[0], parts[2], ALU.add))
                if t >= 2:
                    dve.wait_ge(op.half_turned, 2 * (t - 1))
                dve.wait_ge(gate_loaded[t % 2], 16 * (t // 2 + 1))
                nc.vector.tensor_tensor(mixed[:, t % 2, 512:D], o[:, t % 2, 0, :], gate[:, t % 2, :],
                                        ALU.mult).then_inc(att_mixed, 1)

            mix(0)
            op.split_lo(dve, 0)
            mix(1)
            for t in range(NT):
                if t + 1 < NT:
                    op.split_lo(dve, t + 1)
                if t + 2 < NT:
                    mix(t + 2)
                dve.wait_ge(x_loaded[t % 2], 16 * (t // 2 + 1))
                if t >= 2:
                    dve.wait_ge(y_stored[t % 2], 16 * (t // 2))
                op.add_residual(dve, t, y[:, t % 2, :], x[:, t % 2, :])


def t5_bucket(dist):
    max_exact = 16
    d = np.maximum(dist, 1).astype(np.float64)
    large = max_exact + (np.log(d / max_exact) / np.log(2048 / max_exact) * 16).astype(np.int32)
    return np.where(dist < max_exact, dist, np.minimum(large, 31)).astype(np.int32)


def second_constants():
    onehot = np.zeros((33, 3, DilatedTable.LINE), np.float32)
    for p, r in enumerate(DILATION):
        for u in range(DilatedTable.LINE):
            back = 255 - u
            if p == 2:
                ok, step = back >= 0 and back % 2 == 0, back // 2
            else:
                ok, step = 0 <= back <= P, back
            if ok:
                onehot[int(t5_bucket(np.array(step * r))), p, u] = 1.0
            else:
                onehot[32, p, u] = NEG
    i, j = np.arange(P)[:, None], np.arange(P)[None]
    same = i // CHUNK == j // CHUNK
    levels = np.stack([(i // (2 * s) == j // (2 * s)) & (i % (2 * s) >= s) & (j % (2 * s) < s)
                       for s in (1 << l for l in range(LEVELS))], 1)
    f = np.float32
    return {"c_di_onehot": onehot, "c_upper": (same & (i <= j)).astype(f), "c_strict": (same & (i > j)).astype(f),
            "c_levels": levels.astype(f), "c_ones": np.ones((P, 1), f)}


def second_inputs(f, everywhere):
    rel = np.ones((33, ATT_HEADS), np.float32)
    rel[:32] = f["rel_bias_2"].T
    return {"gain2": everywhere(f["norm_w_2"][0]), "w_in2": f["w_in_2"][0], "w_out2": f["w_out_2"][0],
            "conv_w": f["conv_w_2"][0].T.reshape(12, P, 4).transpose(1, 0, 2),
            "a_dt": everywhere(np.stack([f["a_log_2"][0], f["dt_bias_2"][0]])).reshape(P, 2, DN_HEADS),
            "dn_norm": everywhere(f["dn_norm_w_2"][0]),
            "att_gain": everywhere(np.stack([f["q_norm_w_2"][0], f["k_norm_w_2"][0]])).reshape(P, 2, HD),
            "rel": rel}


def second_block(nc, g, whole):
    d = g.second
    g.w_in2, g.w_out2, g.gain2, g.conv_w, g.a_dt = d["w_in2"], d["w_out2"], d["gain2"], d["conv_w"], d["a_dt"]
    g.di_onehot = d["c_di_onehot"]
    g.dn_norm, g.att_gain, g.rel = d["dn_norm"], d["att_gain"], d["rel"]
    g.d_upper, g.d_strict, g.d_levels = d["c_upper"], d["c_strict"], d["c_levels"]

    def scratch(name, shape):
        return nc.dram_tensor(name, list(shape), F32, kind=g.scratch_kind).ap()

    g.v_att, g.gate2, g.z = (scratch("s_" + n, (SEQ, 512)) for n in ("v_att", "gate2", "z"))
    g.lines = scratch("s_lines", (P, 3 * ATT_HEADS, DilatedTable.LINE))
    g.o_att = [scratch(f"s_o_att{p}", (SEQ, 512)) for p in range(3)]
    g.ml = [scratch(f"s_ml{p}", (SEQ, 16)) for p in range(3)]
    g.l2 = whole.sb("l2", [P, 64])
    g.ba = whole.sb("ba", [P, NT, 8])
    g.o_ss = whole.sb("o_ss", [P, NT, DN_HEADS])
    with ExitStack() as ctx2:
        mid = Kit(nc, ctx2)
        g.att_qT = mid.sb("att_qT", [P, 4, SEQ])
        g.att_kT = mid.sb("att_kT", [P, 4, SEQ])
        g.vT = mid.sb("vT", [P, 4, SEQ])
        with ExitStack() as ctx3:
            early = Kit(nc, ctx3)
            g.qkT = early.sb("qkT", [P, 8, SEQ])
            with ExitStack() as ctx4:
                i = Kit(nc, ctx4)
                hT_hi = i.sb("h2T_hi", [P, KT, SEQ], F32R)
                hT_lo = i.sb("h2T_lo", [P, KT, SEQ], F32R)
                stage_project_2(nc, g, hT_hi, hT_lo)
            stage_delta(nc, g)
        w_hi = mid.sb("w_out2_hi", [P, KT, D], F32R)
        w_lo = mid.sb("w_out2_lo", [P, KT, D], F32R)
        stage_dilated(nc, g, w_hi, w_lo)
        stage_out_2(nc, g, w_hi, w_lo)


class Arrays:
    pass


def build(nc, g):
    def scratch(name, shape):
        return nc.dram_tensor(name, list(shape), F32, kind=g.scratch_kind).ap()

    g.gate1 = scratch("s_gate1", (SEQ, D))
    g.vb = scratch("s_vb", (SEQ, 512))
    g.out_b = scratch("s_out_b", (SEQ, 512))
    g.x1 = scratch("s_x1", (SEQ, D))
    with ExitStack() as top:
        whole = Kit(nc, top, clears=False)
        g.ident = whole.sb("ident", [P, P])
        g.ones = whole.sb("ones", [P, 1])
        g.out_stored = whole.sems("out_stored", 2)
        load_constants(nc, whole, g)
        with ExitStack() as ctx:
            first = Kit(nc, ctx)
            g.na_table = first.sb("na_table", [P, 4 * RIDX, GRID_W])
            g.qkv_a = first.sb("qkv_a", [P, NT, 768])
            g.qbT = first.sb("qbT", [P, 4, SEQ])
            g.kbT = first.sb("kbT", [P, 4, SEQ])
            g.kk = first.sb("kk", [P, A_KV, SEQ], F32R)
            with ExitStack() as inner:
                i = Kit(nc, inner)
                hT_hi = i.sb("hT_hi", [P, KT, SEQ], F32R)
                hT_lo = i.sb("hT_lo", [P, KT, SEQ], F32R)
                stage_project_1(nc, g, hT_hi, hT_lo)
            stage_attention_a(nc, g)
            w_hi = first.sb("w_out_hi", [P, KT, D], F32R)
            w_lo = first.sb("w_out_lo", [P, KT, D], F32R)
            stage_attention_b(nc, g, w_hi, w_lo)
            stage_out_1(nc, g, w_hi, w_lo)
        second_block(nc, g, whole)


def load_constants(nc, k, g):
    loaded = k.sem("ident_loaded")
    with nc.Block() as block:
        @block.sync
        def _(sp):
            sp.dma_start(g.ident[:, :], g.ident_d).then_inc(loaded, 16)
            sp.dma_start(g.ones[:, :], g.second["c_ones"]).then_inc(loaded, 16)
            sp.wait_ge(loaded, 32)


def shape_constants():
    t = np.arange(SEQ)
    inv = (np.float32(10000.0) ** (-np.arange(16, dtype=np.float32) * np.float32(2.0 / 32))).astype(np.float32)
    ang_r = (t // GRID_W).astype(np.float32)[:, None] * inv[None]
    ang_c = (t % GRID_W).astype(np.float32)[:, None] * inv[None]
    ang = np.concatenate([ang_r, ang_r, ang_c, ang_c], -1)
    sign = np.tile(np.repeat(np.array([-1.0, 1.0], np.float32), 16), 2)
    rope = np.stack([np.cos(ang), np.sin(ang) * sign]).astype(np.float32)
    rope = rope.reshape(2, NT, P, HD).transpose(2, 0, 1, 3)
    q = np.arange(GRID_W)[:, None]
    kc = np.arange(GRID_W)[None]
    start = np.clip(q - NA_KW // 2, 0, GRID_W - NA_KW)
    mask = np.where((kc >= start) & (kc < start + NA_KW), 0.0, NEG).astype(np.float32)
    c = {"c_ident": np.eye(P, dtype=np.float32), "c_fold": np.tile(np.eye(HD, dtype=np.float32), (2, 1)), "c_rope": np.ascontiguousarray(rope),
         "c_na_mask": np.concatenate([mask, mask])}
    c.update(second_constants())
    return c


def lay_out(inputs):
    f = {n: np.asarray(a) for n, a in inputs.items()}

    def everywhere(a):
        return np.ascontiguousarray(np.broadcast_to(a.reshape(1, -1), (P, a.size)))

    gains = np.stack([f["q_norm_a"][0], f["k_norm_a"][0]])
    swapped = gains.reshape(2, 2, 2, 16)[:, :, ::-1].reshape(2, HD)
    lines = np.zeros((2, GRID_W, 4, RIDX, NA_LINE), np.float32)
    at = GRID_W - NA_KW
    lines[..., at:at + CIDX] = f["na_rpb"][0].reshape(4, 2, RIDX, CIDX).transpose(1, 0, 2, 3)[:, None]
    a = {"x": f["x"][0], "w_in": f["w_in"][0], "w_out": f["w_out"][0], "gain1": everywhere(f["norm_gain"][0]),
         "final_gain": everywhere(f["final_norm_gain"]),
         "gain_a": everywhere(np.stack([gains, swapped])).reshape(P, 2, 2, HD),
         "na_lines": lines.reshape(P, 4 * RIDX, NA_LINE)}
    a.update(second_inputs(f, everywhere))
    return {n: np.ascontiguousarray(v) for n, v in a.items()}


def kernel(**inputs):
    import concourse.bacc as bacc
    from concourse.bass_utils import run_bass_kernel_spmd

    nc = bacc.Bacc("TRN2", target_bir_lowering=False, num_devices=1)
    g = Arrays()
    g.scratch_kind = "Internal"
    arrays = declare(nc, g, inputs)
    g.out = nc.dram_tensor("out", [SEQ, D], F32, kind="ExternalOutput").ap()
    build(nc, g)
    r = run_bass_kernel_spmd(nc, [arrays], core_ids=[0])
    return r.results[0]["out"].reshape(1, SEQ, D)


def declare(nc, g, inputs):
    arrays = {}
    laid, consts = lay_out(inputs), shape_constants()

    def declared(name, a):
        arrays[name] = a
        return nc.dram_tensor(name, list(a.shape), F32, kind="ExternalInput").ap()

    d = {n: declared(n, a) for n, a in {**laid, **consts}.items()}
    g.x, g.w_in, g.w_out, g.gain1, g.final_gain = d["x"], d["w_in"], d["w_out"], d["gain1"], d["final_gain"]
    g.gain_a, g.na_lines = d["gain_a"], d["na_lines"]
    g.fold_d = d["c_fold"]
    g.ident_d, g.rope, g.na_mask = d["c_ident"], d["c_rope"], d["c_na_mask"]
    g.second = d
    return arrays
```
